# Optimizing a Trainium2 kernel written in Bass

```python
import jax, jax.numpy as jnp
from jax import lax
import numpy as np

D_MODEL = 1024
BATCH = 1
SEQ = 1024
DEPTH = 1
DEC_BATCH = 1
DEC_SEQ = 32
PAST_LEN = 512

CHUNK = 64
N_META = 16
D_RG = 1024
N_RG_HEADS = 16
RG_HEAD_DIM = D_RG // N_RG_HEADS
RG_CONV = 4
RG_C = 8.0
D_CV = 1024
CV_CONV = 31
D_MIX = D_RG + D_CV
D_IN = 2 * D_RG + 3 * D_CV
EPS = 1e-6

kernel_name = 'hymba_rglru_conformer_stream_step'

def rms_norm(x, g):
    xf = x.astype(jnp.float32)
    y = xf * lax.rsqrt(jnp.mean(xf * xf, axis=-1, keepdims=True) + EPS)
    return (y * g.astype(jnp.float32)).astype(x.dtype)

def layer_norm(x, g, b):
    xf = x.astype(jnp.float32)
    mu = jnp.mean(xf, axis=-1, keepdims=True)
    xc = xf - mu
    var = jnp.mean(xc * xc, axis=-1, keepdims=True)
    y = xc * lax.rsqrt(var + EPS) * g.astype(jnp.float32) + b.astype(jnp.float32)
    return y.astype(x.dtype)

def causal_dwconv(x, buf, w, b):
    width = w.shape[0]
    xp = jnp.concatenate([buf.astype(x.dtype), x], axis=1)
    y = lax.conv_general_dilated(
        xp, w[:, None, :].astype(x.dtype), window_strides=(1,), padding='VALID',
        dimension_numbers=('NWC', 'WIO', 'NWC'), feature_group_count=x.shape[-1])
    return y + b.astype(x.dtype), xp[:, xp.shape[1] - (width - 1):]

def rg_lru(x, h0, w_a, b_a, w_x, b_x, lam):
    bsz, t_len, _ = x.shape
    xf = x.astype(jnp.float32)
    xh = xf.reshape(bsz, t_len, N_RG_HEADS, RG_HEAD_DIM)
    r = jax.nn.sigmoid(jnp.einsum('bthi,hij->bthj', xh, w_a.astype(jnp.float32)).reshape(bsz, t_len, D_RG)
                       + b_a.astype(jnp.float32))
    i = jax.nn.sigmoid(jnp.einsum('bthi,hij->bthj', xh, w_x.astype(jnp.float32)).reshape(bsz, t_len, D_RG)
                       + b_x.astype(jnp.float32))
    log_a = -RG_C * r * jax.nn.softplus(-lam.astype(jnp.float32))
    a = jnp.exp(log_a)
    bx = jnp.sqrt(-jnp.expm1(2.0 * log_a)) * (i * xf)

    def step(h, ab):
        a_t, b_t = ab
        h = a_t * h + b_t
        return h, h

    h_last, hs = lax.scan(step, h0.astype(jnp.float32), (a.swapaxes(0, 1), bx.swapaxes(0, 1)))
    return hs.swapaxes(0, 1).astype(x.dtype), h_last.astype(h0.dtype)

def hybrid_layer(x, rg_buf, rg_h, cv_buf, pre_g, w_in, rg_cw, rg_cb, rg_wa, rg_ba, rg_wx, rg_bx, rg_lam,
                 cv_cw, cv_cb, cv_lg, cv_lb, cv_w2, cv_b2, w_out, post_g):
    xn = rms_norm(x, pre_g)
    u = jnp.einsum('btd,de->bte', xn, w_in.astype(x.dtype))
    xr, gr, cv_v, cv_g, gc = jnp.split(u, [D_RG, 2 * D_RG, 2 * D_RG + D_CV, 2 * D_RG + 2 * D_CV], axis=-1)
    xr, rg_buf_new = causal_dwconv(xr, rg_buf, rg_cw, rg_cb)
    hr, rg_h_new = rg_lru(xr, rg_h, rg_wa, rg_ba, rg_wx, rg_bx, rg_lam)
    y_r = hr * jax.nn.silu(gr)
    v = cv_v * jax.nn.sigmoid(cv_g)
    v, cv_buf_new = causal_dwconv(v, cv_buf, cv_cw, cv_cb)
    v = jax.nn.silu(layer_norm(v, cv_lg, cv_lb))
    y_c = (jnp.einsum('btc,ce->bte', v, cv_w2.astype(x.dtype)) + cv_b2.astype(x.dtype)) * jax.nn.silu(gc)
    y = jnp.einsum('btm,md->btd', jnp.concatenate([y_r, y_c], axis=-1), w_out.astype(x.dtype))
    return x + rms_norm(y, post_g), rg_buf_new, rg_h_new, cv_buf_new

def setup_inputs(seed: int = 0) -> dict:
    key = jax.random.key(seed)
    ks = jax.random.split(key, 24)
    f32 = jnp.float32
    nrm = lambda k, s, sc: jax.random.normal(k, s, f32) * sc
    u = jax.random.uniform(ks[12], (DEPTH, D_RG), f32, 0.9, 0.999)
    a0 = u ** (1.0 / RG_C)
    lam = jnp.log(a0) - jnp.log1p(-a0)
    return {
        'x_prompt': nrm(ks[0], (BATCH, SEQ, D_MODEL), 1.0),
        'x_sample': nrm(ks[1], (DEC_BATCH, DEC_SEQ, D_MODEL), 1.0),
        'state_rg_h': nrm(ks[2], (DEPTH, DEC_BATCH, D_RG), 0.5),
        'state_rg_conv': nrm(ks[3], (DEPTH, DEC_BATCH, RG_CONV - 1, D_RG), 1.0),
        'state_cv_conv': nrm(ks[4], (DEPTH, DEC_BATCH, CV_CONV - 1, D_CV), 0.5),
        'meta_tokens': nrm(ks[5], (N_META, D_MODEL), 1.0),
        'pre_norm_g': 1.0 + nrm(ks[6], (DEPTH, D_MODEL), 0.02),
        'w_in': nrm(ks[7], (DEPTH, D_MODEL, D_IN), D_MODEL ** -0.5),
        'rg_conv_w': nrm(ks[8], (DEPTH, RG_CONV, D_RG), RG_CONV ** -0.5),
        'rg_conv_b': nrm(ks[9], (DEPTH, D_RG), 0.02),
        'rg_wa': nrm(ks[10], (DEPTH, N_RG_HEADS, RG_HEAD_DIM, RG_HEAD_DIM), RG_HEAD_DIM ** -0.5),
        'rg_ba': nrm(ks[11], (DEPTH, D_RG), 0.02),
        'rg_wx': nrm(ks[13], (DEPTH, N_RG_HEADS, RG_HEAD_DIM, RG_HEAD_DIM), RG_HEAD_DIM ** -0.5),
        'rg_bx': nrm(ks[14], (DEPTH, D_RG), 0.02),
        'rg_lambda': lam,
        'cv_conv_w': nrm(ks[15], (DEPTH, CV_CONV, D_CV), CV_CONV ** -0.5),
        'cv_conv_b': nrm(ks[16], (DEPTH, D_CV), 0.02),
        'cv_ln_g': 1.0 + nrm(ks[17], (DEPTH, D_CV), 0.02),
        'cv_ln_b': nrm(ks[18], (DEPTH, D_CV), 0.02),
        'cv_w_pw2': nrm(ks[19], (DEPTH, D_CV, D_CV), D_CV ** -0.5),
        'cv_b_pw2': nrm(ks[20], (DEPTH, D_CV), 0.02),
        'w_out': nrm(ks[21], (DEPTH, D_MIX, D_MODEL), D_MIX ** -0.5),
        'post_norm_g': 1.0 + nrm(ks[22], (DEPTH, D_MODEL), 0.02),
    }

def reference(x_prompt, x_sample, state_rg_h, state_rg_conv, state_cv_conv, meta_tokens, pre_norm_g, w_in,
              rg_conv_w, rg_conv_b, rg_wa, rg_ba, rg_wx, rg_bx, rg_lambda, cv_conv_w, cv_conv_b, cv_ln_g,
              cv_ln_b, cv_w_pw2, cv_b_pw2, w_out, post_norm_g):
    bsz = x_prompt.shape[0]
    dt = x_prompt.dtype
    hp = jnp.concatenate([jnp.broadcast_to(meta_tokens.astype(dt)[None], (bsz, N_META, D_MODEL)), x_prompt], axis=1)
    hs = x_sample
    p_rgh, p_rgc, p_cvc, s_rgh, s_rgc, s_cvc = [], [], [], [], [], []
    for l in range(DEPTH):
        w = (pre_norm_g[l], w_in[l], rg_conv_w[l], rg_conv_b[l], rg_wa[l], rg_ba[l], rg_wx[l], rg_bx[l],
             rg_lambda[l], cv_conv_w[l], cv_conv_b[l], cv_ln_g[l], cv_ln_b[l], cv_w_pw2[l], cv_b_pw2[l],
             w_out[l], post_norm_g[l])
        hp, rgc, rgh, cvc = hybrid_layer(
            hp, jnp.zeros((bsz, RG_CONV - 1, D_RG), dt), jnp.zeros((bsz, D_RG), dt),
            jnp.zeros((bsz, CV_CONV - 1, D_CV), dt), *w)
        p_rgh.append(rgh); p_rgc.append(rgc); p_cvc.append(cvc)
        hs, rgc, rgh, cvc = hybrid_layer(hs, state_rg_conv[l], state_rg_h[l], state_cv_conv[l], *w)
        s_rgh.append(rgh); s_rgc.append(rgc); s_cvc.append(cvc)
    y_prompt = hp[:, N_META:]
    y_sample = hs
    return (y_prompt, y_sample, jnp.stack(p_rgh), jnp.stack(p_rgc), jnp.stack(p_cvc),
            jnp.stack(s_rgh), jnp.stack(s_rgc), jnp.stack(s_cvc))


_drawn_inputs = setup_inputs


def setup_inputs(seed=0):
    import zlib

    import numpy as np

    out = dict(_drawn_inputs(seed))
    spreads = {}
    factors = {'rg_ba': 8.0,
     'rg_bx': 8.0,
     'cv_conv_b': 2.737,
     'cv_ln_g': 4.788,
     'cv_ln_b': 5.623,
     'cv_b_pw2': 3.459,
     'post_norm_g': 3.99}
    for name, (base, spread) in spreads.items():
        noise = np.random.default_rng([zlib.crc32(name.encode()), seed]).standard_normal(out[name].shape)
        drawn = base * np.exp(spread * noise) if base else spread * noise
        out[name] = __import__('jax').numpy.asarray(drawn.astype(out[name].dtype))
    for name, factor in factors.items():
        out[name] = (out[name] * factor).astype(out[name].dtype)
    return out
```

```python
from contextlib import ExitStack

import numpy as np

import concourse.bass as bass
from concourse import mybir
from concourse.alu_op_type import AluOpType as ALU

F32 = mybir.dt.float32
F32R = mybir.dt.float32r
ACT = mybir.ActivationFunctionType

P = 128
D = 1024
KT = D // P
META, SEQ, DEC = 16, 1024, 32
T = META + SEQ + DEC
TO = SEQ + DEC
EPS = 1e-6

XCH = [(0, 358), (358, 358), (716, 356)]
OCH = 352
assert sum(n for _, n in XCH) == T and 3 * OCH == TO

RW = 4
RPAD = RW - 1
R_SAMPLE_IN = RPAD + META + SEQ + RPAD
R_LEN = 1080
R_CH = R_LEN // 3
R_SAMPLE = R_SAMPLE_IN - RPAD
R_IN = R_LEN + RPAD
assert R_SAMPLE + DEC <= R_LEN

CW = 31
CPAD = CW - 1
V_SAMPLE_IN = CPAD + META + SEQ + CPAD
V_IN = V_SAMPLE_IN + DEC
C_LEN = SEQ + CPAD + DEC
C_SAMPLE = SEQ + CPAD
C_CH = C_LEN // 3
assert 3 * C_CH == C_LEN and META + C_LEN + CPAD == V_IN

P_CW, P_RW, P_RB, P_BA, P_BX, P_LAM, P_CB, P_LG, P_LB, P_B2, P_PG, P_H0, P_RS, P_CS = (
    0, 31, 35, 36, 37, 38, 39, 40, 41, 42, 43, 44, 45, 48)
PAR = P_CS + CPAD
Q_CW, Q_BA, Q_BX, Q_SP, Q_NSP = PAR, PAR + CW, PAR + CW + 1, PAR + CW + 2, PAR + CW + 3
PARQ = Q_NSP + 1

O_HP, O_HS, O_RP, O_RS, O_CP, O_CS = 0, 1, 2, 5, 8, 38
NOUT = O_CS + CPAD

SECTIONS = ["g", "v", "x", "gc", "gr"]
COLUMN = {"x": 0, "gr": 1, "v": 2, "g": 3, "gc": 4}
NS = len(SECTIONS)
ORDER = {s: i for i, s in enumerate(SECTIONS)}
WSLOT = {"g": 0, "v": 1, "x": 2, "gc": 0, "gr": 1}
BANK = {"g": 4, "v": 0, "x": 6, "gc": 4, "gr": 1}
GATE_R_BANK, GATE_I_BANK = 7, 0

N_IN = NS * KT
N_PW = N_IN
N_OUT = N_IN + KT
DER_STEPS = 22
YCH = [(0, 384), (384, 384), (768, 288)]


def build(nc, x_prompt, x_sample, state_rg_h, state_rg_conv, state_cv_conv, meta_tokens, pre_norm_g,
          w_in, rg_conv_w, rg_conv_b, rg_wa, rg_ba, rg_wx, rg_bx, rg_lambda, cv_conv_w, cv_conv_b,
          cv_ln_g, cv_ln_b, cv_w_pw2, cv_b_pw2, w_out, post_norm_g,
          y_prompt, y_sample, rg_h_p, rg_c_p, cv_c_p, rg_h_s, rg_c_s, cv_c_s):
    top = [(nc.sbuf_base + 31) // 32 * 32]

    def take(nbytes):
        at = top[0]
        top[0] = at + (nbytes + 31) // 32 * 32
        assert top[0] <= nc.sbuf_usable_end, (top[0], nc.sbuf_usable_end)
        return at

    def at(name, shape, dt, offset):
        return nc.alloc_sbuf_tensor_at(name, [P] + shape, dt, offset=offset)

    def new(name, shape, dt=F32):
        return at(name, shape, dt, take(4 * int(np.prod(shape))))

    act_hi = new("act_hi", [KT, T], F32R)
    act_lo = new("act_lo", [KT, T], F32R)
    conv_at = take(4 * KT * C_LEN)
    conv_out = at("conv_out", [KT, C_LEN], F32, conv_at)
    yc_lo = at("yc_lo", [KT, C_LEN], F32R, conv_at)
    wstage_at = take(2 * 4 * D)
    wstage = at("wstage", [2, KT, P], F32, wstage_at)
    w_hi = new("w_hi", [2, KT, P], F32R)
    w_lo = new("w_lo", [2, KT, P], F32R)
    w2_at = take(2 * 4 * D)
    w2_hi = at("w2_hi", [KT, P], F32R, w2_at)
    w2_lo = at("w2_lo", [KT, P], F32R, w2_at + 4 * D)
    par = new("par", [KT, PARQ])
    ident = new("ident", [P])
    mean_w = new("mean_w", [P])
    eps_col = new("eps_col", [1])
    WHI = [w_hi[:, 0], w_hi[:, 1], w2_hi[:, :, :]]
    WLO = [w_lo[:, 0], w_lo[:, 1], w2_lo[:, :, :]]
    arena = top[0]

    def phase(start):
        spot = [start]

        def put(name, shape, dt=F32):
            o = spot[0]
            spot[0] = (o + 4 * int(np.prod(shape)) + 31) // 32 * 32
            assert spot[0] <= nc.sbuf_usable_end, (name, spot[0], nc.sbuf_usable_end)
            return at(name, shape, dt, o)
        return put, spot

    put, spot = phase(conv_at)
    x_in = put("x_in", [4, D])
    x_norm = put("x_norm", [2, D])
    g_bcast = put("g_bcast", [D])
    sq_junk = put("sq_junk", [D])
    assert spot[0] <= conv_at + 4 * KT * C_LEN

    put, spot = phase(arena)
    ra = put("ra", [R_LEN])
    rb = put("rb", [R_LEN])
    rc = put("rc", [R_LEN])
    rd = put("rd", [R_LEN])
    rg_in = put("rg_in", [R_IN + 1])
    rg_x = put("rg_x", [R_LEN])
    rg_xh = put("rg_xh", [R_LEN], F32R)
    rg_xl = put("rg_xl", [R_LEN], F32R)
    silu_gr = put("silu_gr", [TO])
    silu_gc = put("silu_gc", [TO])
    tanh_g = put("tanh_g", [T])
    cv_in = put("cv_in", [V_IN])
    acc = put("acc", [C_LEN])
    y_rg = put("y_rg", [TO])
    gate_w = put("gate_w", [2, KT, 64])
    gate_h = put("gate_h", [2, P], F32R)
    gate_l = put("gate_l", [2, P], F32R)
    states = put("states", [KT, NOUT])
    par_a = put("par_a", [PARQ])
    par_v = put("par_v", [PARQ])
    prm = put("prm", [2, KT])
    small = put("small", [4, KT])
    sums = put("sums", [16])
    par_rows = at("par_rows", [D], F32, arena)

    put, _ = phase(arena)
    yr = put("yr", [KT, TO])
    put2, _ = phase(arena + 4 * KT * TO)
    sqs = put2("sqs", [2, C_LEN])
    rstd_b = put2("rstd_b", [C_LEN])
    silu_v = put2("silu_v", [2, C_LEN])
    silu_l = put2("silu_l", [2, TO])
    yr_lo = at("yr_lo", [KT, TO], F32R, arena)
    state_rows = at("state_rows", [D], F32, arena)

    put3, _ = phase(arena + 4 * KT * TO)
    o_t = put3("o_t", [KT, TO])
    ssq = put3("ssq", [TO])
    rs_o = put3("rs_o", [3, 9])
    x_res = at("x_res", [2, D], F32, wstage_at)
    y_out = at("y_out", [2, D], F32, w2_at)

    ps = nc.alloc_psum_tensor("ps", [P, 8, 512], F32)
    silu_spill = nc.dram_tensor("silu_spill", [KT, P, TO], F32, kind="Internal").ap()
    yr_spill = nc.dram_tensor("yr_spill", [KT, P, TO], F32, kind="Internal").ap()

    ctx = ExitStack()
    with ctx:
        def sem(name):
            return ctx.enter_context(nc.semaphore(name))

        x_loaded = [sem(f"x_loaded{i}") for i in range(4)]
        g_loaded = sem("g_loaded")
        par_loaded = sem("par_loaded")
        gatew_loaded = sem("gatew_loaded")
        consts = sem("consts")
        x_ss = sem("x_ss")
        x_rt = sem("x_rt")
        x_rs = sem("x_rs")
        x_normed = sem("x_normed")
        x_turned = sem("x_turned")
        x_hi = sem("x_hi")
        x_lo = sem("x_lo")
        par_turned = sem("par_turned")
        par_ready = sem("par_ready")
        der = sem("der")
        der_exp = sem("der_exp")
        pads = sem("pads")
        w_loaded = [sem("w_loaded0"), sem("w_loaded1")]
        sp_steps = sem("sp_steps")
        w_his = sem("w_his")
        w_los = sem("w_los")
        proj = sem("proj")
        g_read = sem("g_read")
        v_read = sem("v_read")
        x_read = sem("x_read")
        gc_read = sem("gc_read")
        gr_read = sem("gr_read")
        gates = sem("gates")
        gates_read = sem("gates_read")
        para = sem("para")
        parv = sem("parv")
        parv2 = sem("parv2")
        tap0 = sem("tap0")
        taps = sem("taps")
        conv_done = sem("conv_done")
        rtap0 = sem("rtap0")
        rtaps = sem("rtaps")
        rgxh = sem("rgxh")
        rgxl = sem("rgxl")
        gwh = sem("gwh")
        gwl = sem("gwl")
        th_done = sem("th_done")
        a_done = sem("a_done")
        a2_done = sem("a2_done")
        ix_done = sem("ix_done")
        q_done = sem("q_done")
        root_done = sem("root_done")
        b_done = sem("b_done")
        h_done = sem("h_done")
        y_done = sem("y_done")
        st_saved = sem("st_saved")
        st_read = sem("st_read")
        sgc_out = sem("sgc_out")
        yr_out = sem("yr_out")
        mean_done = sem("mean_done")
        centred = sem("centred")
        squared = sem("squared")
        sq_used = sem("sq_used")
        var_done = sem("var_done")
        ln_rstd = sem("ln_rstd")
        z_done = sem("z_done")
        ln_silu = sem("ln_silu")
        v_hi = sem("v_hi")
        v_lo = sem("v_lo")
        st_turned = sem("st_turned")
        st_rows = sem("st_rows")
        st_out = sem("st_out")
        silu_loaded = [sem("silu_loaded0"), sem("silu_loaded1")]
        pw = sem("pw")
        yc = sem("yc")
        yr_in = sem("yr_in")
        yh = sem("yh")
        yl = sem("yl")
        oproj = sem("oproj")
        half_done = sem("half_done")
        o_copied = sem("o_copied")
        o_sq = sem("o_sq")
        o_ssq = sem("o_ssq")
        ss_done = sem("ss_done")
        ss_root = sem("ss_root")
        ss_rs = sem("ss_rs")
        o_turned = sem("o_turned")
        y_ready = sem("y_ready")
        xr_loaded = [sem("xr_loaded0"), sem("xr_loaded1")]
        y_stored = [sem("y_stored0"), sem("y_stored1")]

        w_in_v = w_in.rearrange("d (k p) e -> p (d k) e", p=P)
        w_pw_v = cv_w_pw2.rearrange("d (k p) e -> p (d k) e", p=P)
        w_out_v = w_out.rearrange("d (h k p) e -> p (d h k) e", h=2, p=P)
        xp_v = x_prompt.rearrange("b t d -> (b t) d")
        xs_v = x_sample.rearrange("b t d -> (b t) d")

        first = P - META
        x_tiles = [[(0, meta_tokens, 0, META), (META, xp_v, 0, first)]]
        for t in range(1, 8):
            x_tiles.append([(0, xp_v, first + (t - 1) * P, P)])
        x_tiles.append([(0, xp_v, SEQ - META, META), (META, xs_v, 0, DEC)])
        x_rows = [P] * 8 + [META + DEC]
        NX = len(x_tiles)
        x_dmas = [len(t) for t in x_tiles]
        assert first + 7 * P == SEQ - META

        def x_landed(t):
            return 16 * sum(x_dmas[u] for u in range(t % 4, t + 1, 4))

        out_tiles = [[(0, P), (128, P), (256, P)], [(384, P), (512, P), (640, P)],
                     [(768, P), (896, P), (1024, DEC)]]

        par_src = [(P_CW, cv_conv_w[0]), (P_RW, rg_conv_w[0]), (P_RB, rg_conv_b), (P_BA, rg_ba),
                   (P_BX, rg_bx), (P_LAM, rg_lambda), (P_CB, cv_conv_b), (P_LG, cv_ln_g),
                   (P_LB, cv_ln_b), (P_B2, cv_b_pw2), (P_PG, post_norm_g), (P_H0, state_rg_h[0]),
                   (P_RS, state_rg_conv[0, 0]), (P_CS, state_cv_conv[0, 0])]

        block = ctx.enter_context(nc.Block())

        @block.sync
        def _(sp):
            def load_x(t):
                for row, src, r0, n in x_tiles[t]:
                    if t >= 4:
                        sp.wait_ge(x_normed, t - 3)
                    sp.dma_start(x_in[row:row + n, t % 4, :], src[r0:r0 + n, :]).then_inc(x_loaded[t % 4], 16)

            def load_w(slot, src):
                sp.dma_start(wstage[:, slot], src).then_inc(w_loaded[slot], 16)

            def w_in_cols(s, c):
                return w_in_v[:, :, bass.ds(c * P + COLUMN[s] * D, P)]

            def after_reg_wait():
                sp.sem_inc(sp_steps, 1)

            for t in range(3):
                load_x(t)
            sp.dma_start(g_bcast[:, :], pre_norm_g.broadcast_to([P, D])).then_inc(g_loaded, 16)
            load_x(3)
            load_w(0, w_in_cols("g", 0))
            load_w(1, w_in_cols("v", 0))
            for t in range(4, NX):
                load_x(t)
            sp.wait_ge(w_los, 1)
            load_w(0, w_in_cols("x", 0))

            def loop_loads(c, fst, last):
                sp.wait_ge(w_los, c * NS + 2)
                after_reg_wait()
                load_w(1, w_in_cols("gc", c))
                sp.wait_ge(w_los, c * NS + 3)
                after_reg_wait()
                load_w(0, w_in_cols("gr", c))
                if not fst:
                    sp.wait_ge(y_done, 2 * c)
                    after_reg_wait()
                    sp.dma_start(yr_spill[bass.ds(c - 1, 1)], y_rg[:, :]).then_inc(yr_out, 16)
                sp.wait_ge(w_los, c * NS + 4)
                after_reg_wait()
                load_w(1, w_pw_v[:, :, P:2 * P] if last else w_in_cols("v", c + 1))
                sp.wait_ge(w_los, c * NS + 5)
                after_reg_wait()
                load_w(0, w_pw_v[:, :, 0:P] if last else w_in_cols("g", c + 1))
                sp.wait_ge(gc_read, c + 1)
                after_reg_wait()
                sp.dma_start(silu_spill[bass.ds(c, 1)], silu_gc[:, :]).then_inc(sgc_out, 16)
                if not last:
                    sp.wait_ge(w_los, c * NS + 6)
                    after_reg_wait()
                    load_w(0, w_in_cols("x", c + 1))

            loop_loads(0, True, False)
            with sp.Fori(1, KT - 1) as c:
                loop_loads(c, False, False)
            loop_loads(KT - 1, False, True)

            sp.wait_ge(y_done, 2 * KT)
            sp.dma_start(yr_spill[KT - 1], y_rg[:, :]).then_inc(yr_out, 16)
            sp.wait_ge(yr_out, 16 * KT)
            sp.wait_ge(sgc_out, 16 * KT)
            sp.wait_ge(ln_rstd, 2)
            for h in range(2):
                sp.dma_start(silu_l[:, h], silu_spill[h]).then_inc(silu_loaded[h], 16)
            sp.wait_ge(w_los, N_PW + 1)
            load_w(0, w_pw_v[:, :, 2 * P:3 * P])
            sp.wait_ge(w_los, N_PW + 2)
            load_w(1, w_pw_v[:, :, 3 * P:4 * P])
            sp.wait_ge(st_out, 16 * 6)
            sp.dma_start(yr[:, :, :], yr_spill.rearrange("k p t -> p k t")).then_inc(yr_in, 16)

            with sp.Fori(0, 2) as p:
                for h in range(2):
                    sp.wait_ge(yc, p * 2 + h + 1)
                    after_reg_wait()
                    sp.dma_start(silu_l[:, h], silu_spill[bass.ds(p * 2 + h + 2, 1)])\
                        .then_inc(silu_loaded[h], 16)
                    sp.wait_ge(w_los, p * 2 + N_PW + 3 + h)
                    after_reg_wait()
                    load_w(h, w_pw_v[:, :, bass.ds(p * (2 * P) + (h + 4) * P, P)])
            for h in range(2):
                sp.wait_ge(yc, 4 + h + 1)
                sp.dma_start(silu_l[:, h], silu_spill[6 + h]).then_inc(silu_loaded[h], 16)
                sp.wait_ge(w_los, N_PW + 7 + h)
                load_w(h, w_out_v[:, (1 - h) * KT:(2 - h) * KT, 0:P])
            with sp.Fori(1, KT) as e:
                for h in range(2):
                    sp.wait_ge(w_los, N_OUT + 2 * e - 1 + h)
                    after_reg_wait()
                    load_w(h, w_out_v[:, (1 - h) * KT:(2 - h) * KT, bass.ds(e * P, P)])
            sp.wait_ge(w_los, N_OUT + 2 * KT)
            flat = [t for j in out_tiles for t in j]
            for n, (c0, rows) in enumerate(flat[:2]):
                sp.dma_start(x_res[0:rows, n], xp_v[c0:c0 + rows, :]).then_inc(xr_loaded[n], 16)
            for n, (c0, rows) in enumerate(flat):
                dst, r0 = (y_prompt[0], c0) if c0 < SEQ else (y_sample[0], 0)
                sp.wait_ge(y_ready, n + 1)
                sp.dma_start(dst[r0:r0 + rows, :], y_out[0:rows, n % 2]).then_inc(y_stored[n % 2], 16)
                if n + 2 < len(flat):
                    c2, rows2 = flat[n + 2]
                    src, r2 = (xp_v, c2) if c2 < SEQ else (xs_v, 0)
                    sp.dma_start(x_res[0:rows2, n % 2], src[r2:r2 + rows2, :]).then_inc(xr_loaded[n % 2], 16)
            sp.wait_ge(y_stored[0], 16 * 5)
            sp.wait_ge(y_stored[1], 16 * 4)

        @block.gpsimd
        def _(pool):
            pool.memset(ident[:, :], 0.0).then_inc(consts, 1)
            pool.memset(mean_w[:, :], 1.0 / D).then_inc(consts, 1)
            pool.memset(eps_col[:, :], EPS).then_inc(consts, 1)
            pool.memset(gate_h[:, :, :].bitcast(F32), 0.0).then_inc(consts, 1)
            pool.memset(gate_l[:, :, :].bitcast(F32), 0.0).then_inc(consts, 1)
            pool.wait_ge(consts, 5)
            pool.affine_select(out=ident[:, :], in_=ident[:, :], compare_op=ALU.not_equal, fill=1.0,
                               base=0, pattern=[[-1, P]], channel_multiplier=1).then_inc(consts, 1)
            for row, src in par_src:
                n = src.shape[0]
                pool.dma_start(par_rows[row:row + n, :], src).then_inc(par_loaded, 16)
            for m, w in enumerate((rg_wa, rg_wx)):
                for b in range(2):
                    pool.dma_start(gate_w[64 * b:64 * b + 64, m],
                                   w[0].rearrange("(c b) i j -> b i c j", b=2)[b]).then_inc(gatew_loaded, 16)
            pool.wait_ge(par_turned, 1)
            pool.memset(rg_in[:, 0:RPAD], 0.0).then_inc(pads, 1)
            pool.memset(rg_in[:, R_SAMPLE_IN + DEC:R_IN + 1], 0.0).then_inc(pads, 1)
            pool.memset(cv_in[:, 0:CPAD], 0.0).then_inc(pads, 1)
            pool.wait_ge(st_rows, 2)
            for dst, row, n in ((rg_h_p[0], O_HP, 1), (rg_h_s[0], O_HS, 1), (rg_c_p[0, 0], O_RP, RPAD),
                                (rg_c_s[0, 0], O_RS, RPAD), (cv_c_p[0, 0], O_CP, CPAD),
                                (cv_c_s[0, 0], O_CS, CPAD)):
                pool.dma_start(dst, state_rows[row:row + n, :]).then_inc(st_out, 16)
            pool.wait_ge(st_out, 16 * 6)

        @block.tensor
        def _(pe):
            def product(out, wh, wl, xh, xl, start, stop):
                pe.matmul(out, wh, xh, start=start, stop=False)
                pe.matmul(out, wh, xl, start=False, stop=False)
                return pe.matmul(out, wl, xh, start=False, stop=stop)

            def chunk(s, j):
                bank = (BANK[s] + j) % 8
                c0, n = (META + j * OCH, OCH) if s in ("gr", "gc") else XCH[j]
                w = WSLOT[s]
                for k in range(KT):
                    mm = product(ps[:, bank, 0:n], WHI[w][:, k], WLO[w][:, k],
                                 act_hi[:, k, c0:c0 + n], act_lo[:, k, c0:c0 + n], k == 0, k == KT - 1)
                mm.then_inc(proj, 1)

            def turn_x(t):
                rows = x_rows[t]
                pe.wait_ge(x_normed, t + 1)
                if t >= 2:
                    pe.wait_ge(x_lo, t - 1)
                for k in range(KT):
                    mm = pe.transpose(ps[:, 2 * (t % 2) + k // 4, k % 4 * P:k % 4 * P + rows],
                                      x_norm[0:rows, t % 2, k * P:(k + 1) * P], ident[0:rows, 0:rows])
                mm.then_inc(x_turned, 1)

            def gate_chunk(j):
                for m, bank in ((0, GATE_R_BANK), (1, GATE_I_BANK)):
                    mm = product(ps[:, bank, 0:R_CH], gate_h[:, m], gate_l[:, m],
                                 rg_xh[:, j * R_CH:(j + 1) * R_CH], rg_xl[:, j * R_CH:(j + 1) * R_CH],
                                 True, True)
                    mm.then_inc(gates, 1)

            def tile(c, fst):
                if not fst:
                    pe.wait_ge(w_los, c * NS + 1)
                    pe.wait_ge(gc_read, c)
                    for j in range(3):
                        chunk("g", j)
                pe.wait_ge(w_los, c * NS + 2)
                if not fst:
                    pe.wait_ge(gates_read, 6 * c)
                    pe.wait_ge(gr_read, c)
                for j in range(3):
                    chunk("v", j)
                pe.wait_ge(w_los, c * NS + 3)
                pe.wait_ge(g_read, 2 * c + 2)
                for j in range(3):
                    if j == 2:
                        pe.wait_ge(v_read, 3 * c + 3)
                    chunk("x", j)
                pe.wait_ge(w_los, c * NS + 4)
                for j in range(3):
                    if j == 2:
                        pe.wait_ge(x_read, 3 * c + 1)
                    chunk("gc", j)
                pe.wait_ge(w_los, c * NS + 5)
                for j in range(3):
                    chunk("gr", j)
                    if j == 0:
                        pe.wait_ge(x_read, 3 * c + 3)
                        pe.wait_ge(rgxl, c + 1)
                        pe.wait_ge(gwl, 2 * c + 2)
                    if j > 0:
                        pe.wait_ge(gates_read, 6 * c + 2 * j)
                    gate_chunk(j)

            pe.wait_ge(consts, 6)
            for t in range(NX):
                turn_x(t)
                if t % 3 == 2:
                    pe.wait_ge(w_los, 1)
                    pe.wait_ge(x_lo, t + 1)
                    chunk("g", t // 3)
            pe.wait_ge(par_loaded, 16 * len(par_src))
            pe.wait_ge(x_lo, NX)
            for k in range(KT):
                mm = pe.transpose(ps[:, 2 + k // 4, k % 4 * P:k % 4 * P + PAR],
                                  par_rows[0:PAR, k * P:(k + 1) * P], ident[0:PAR, 0:PAR])
            mm.then_inc(par_turned, 1)
            pe.wait_ge(par_ready, 1)
            tile(0, True)
            with pe.Fori(1, KT) as c:
                tile(c, False)

            pe.wait_ge(gates_read, 6 * KT)
            pe.wait_ge(gr_read, KT)
            for c in range(KT):
                pe.wait_ge(conv_done, c + 1)
                for j in range(3):
                    mm = pe.matmul(ps[:, j, 0:C_CH], mean_w[:, :], conv_out[:, c, j * C_CH:(j + 1) * C_CH],
                                   start=(c == 0), stop=(c == KT - 1))
            mm.then_inc(mean_done, 1)
            pe.wait_ge(st_saved, 6 * KT)
            for k in range(KT):
                mm = pe.transpose(ps[0:NOUT, 3 + 4 * (k // 4), k % 4 * P:(k % 4 + 1) * P],
                                  states[:, k, :], ident[:, :])
            mm.then_inc(st_turned, 1)
            pe.wait_ge(gc_read, KT)
            for c in range(KT):
                pe.wait_ge(squared, c + 1)
                for j in range(3):
                    mm = pe.matmul(ps[:, 4 + j, 0:C_CH], mean_w[:, :], sqs[:, c % 2, j * C_CH:(j + 1) * C_CH],
                                   start=(c == 0), stop=(c == KT - 1))
                mm.then_inc(sq_used, 1)
            def pw_pair(p, fst):
                for h in range(2):
                    pe.wait_ge(w_los, p * 2 + N_PW + h + 1)
                    if fst:
                        pe.wait_ge(centred, KT)
                        pe.wait_ge(ln_rstd, 1)
                    else:
                        pe.wait_ge(yc, p * 2 + h - 1)
                    for k in range(KT):
                        pe.wait_ge(v_lo, 2 * k + 2)
                        for j in range(3):
                            mm = product(ps[:, 4 * h + j, 0:OCH], WHI[h][:, k], WLO[h][:, k],
                                         act_hi[:, k, j * OCH:(j + 1) * OCH],
                                         act_lo[:, k, j * OCH:(j + 1) * OCH], k == 0, k == KT - 1)
                    mm.then_inc(pw, 1)

            pw_pair(0, True)
            with pe.Fori(1, KT // 2) as p:
                pw_pair(p, False)

            halves = [(act_hi, yc_lo), (act_lo, yr_lo)]

            def o_steps(h, k, j, start, stop):
                hi, lo = halves[h]
                c0, n = YCH[j]
                return product(ps[:, j, 0:n], WHI[h][:, k], WLO[h][:, k],
                               hi[:, k, c0:c0 + n], lo[:, k, c0:c0 + n], start, stop)

            pe.wait_ge(yc, KT)
            for h in range(2):
                pe.wait_ge(w_los, N_OUT + 1 + h)
                for k in range(KT):
                    pe.wait_ge(yl, h * KT + k + 1)
                    for j in range(3):
                        mm = o_steps(h, k, j, h == 0 and k == 0, h == 1 and k == KT - 1)
                        if h == 1 and k == KT - 1:
                            mm.then_inc(oproj, 1)
                if h == 0:
                    mm.then_inc(half_done, 1)
            with pe.Fori(1, KT - 1) as e:
                for h in range(2):
                    pe.wait_ge(w_los, e * 2 + N_OUT + 1 + h)
                    for j in range(3):
                        if h == 0:
                            pe.wait_ge(o_sq, e * 3 - 2 + j)
                        for k in range(KT):
                            mm = o_steps(h, k, j, h == 0 and k == 0, h == 1 and k == KT - 1)
                        if h == 1:
                            mm.then_inc(oproj, 1)
                    if h == 0:
                        mm.then_inc(half_done, 1)

            e = KT - 1

            def turn_out(j):
                pe.wait_ge(o_ssq, 3 * e + j + 1)
                for i, (c0, rows) in enumerate(out_tiles[j]):
                    mm = pe.matmul(ps[0:rows, 3, i:i + 1], ssq[:, c0:c0 + rows], mean_w[:, 0:1],
                                   start=(i == 0), stop=True, skip_group_check=True)
                mm.then_inc(ss_done, 1)
                for i, (c0, rows) in enumerate(out_tiles[j]):
                    n = 3 * j + i
                    if n >= 2:
                        pe.wait_ge(y_ready, n - 1)
                    for k in range(KT):
                        mm = pe.transpose(ps[0:rows, 4 + 2 * (n % 2) + k // 4, k % 4 * P:(k % 4 + 1) * P],
                                          o_t[:, k, c0:c0 + rows], ident[:, :])
                    mm.then_inc(o_turned, 1)

            pe.wait_ge(w_los, N_OUT + 2 * KT)
            for j in range(3):
                pe.wait_ge(o_sq, 3 * e - 2 + j)
                for h in range(2):
                    for k in range(KT):
                        mm = o_steps(h, k, j, h == 0 and k == 0, h == 1 and k == KT - 1)
                mm.then_inc(oproj, 1)
                if j > 0:
                    turn_out(j - 1)
            turn_out(2)

        @block.scalar
        def _(act):
            A = act.activation

            def w_hi_part(slot, stage):
                A(WHI[slot], wstage[:, stage], ACT.Copy).then_inc(w_his, 1)

            act.preload_act_table(ACT.Sqrt)
            act.wait_ge(consts, 6)

            def x_stats(t):
                rows = x_rows[t]
                act.wait_ge(x_loaded[t % 4], x_landed(t))
                if t >= 1:
                    act.wait_ge(x_ss, t)
                A(sq_junk[0:rows, :], x_in[0:rows, t % 4, :], ACT.Square,
                  accum_out=sums[0:rows, t:t + 1]).then_inc(x_ss, 1)
                act.wait_ge(x_ss, t + 1)
                A(sums[0:rows, t:t + 1], sums[0:rows, t:t + 1], ACT.Sqrt, scale=1.0 / D,
                  bias=eps_col[0:rows, :]).then_inc(x_rt, 1)

            def x_hi_part(t):
                rows = x_rows[t]
                b = 2 * (t % 2)
                act.wait_ge(x_turned, t + 1)
                A(act_hi[:, :, t * P:t * P + rows].rearrange("p (b k) t -> p b k t", b=2),
                  ps[:, b:b + 2, :].rearrange("p b (k t) -> p b k t", t=P)[:, :, :, 0:rows],
                  ACT.Copy).then_inc(x_hi, 1)

            for t in range(NX + 1):
                if t < NX:
                    x_stats(t)
                if t == 2:
                    act.wait_ge(w_loaded[0], 16)
                    w_hi_part(0, 0)
                if t >= 1:
                    x_hi_part(t - 1)
            act.wait_ge(w_loaded[1], 16)
            w_hi_part(1, 1)
            act.wait_ge(par_turned, 1)
            A(par[:, :, 0:PAR].rearrange("p (b k) n -> p b k n", b=2),
              ps[:, 2:4, :].rearrange("p b (k n) -> p b k n", n=P)[:, :, :, 0:PAR],
              ACT.Copy).then_inc(par_ready, 1)
            act.wait_ge(der, 2)
            A(small[:, 1, :], small[:, 1, :], ACT.Exp, scale=-1.0).then_inc(der_exp, 1)
            act.wait_ge(w_loaded[0], 32)
            w_hi_part(2, 0)
            act.wait_ge(pads, 3)

            def tile(c, fst, last):
                act.preload_act_table(ACT.Silu)
                act.wait_ge(proj, c * (3 * NS) + 2)
                if not fst:
                    act.wait_ge(v_read, 3 * c)
                A(tanh_g[:, 0:716].rearrange("p (j n) -> p j n", j=2), ps[:, 4:6, 0:358], ACT.Tanh,
                  scale=0.5).then_inc(g_read, 1)
                act.wait_ge(proj, c * (3 * NS) + 3)
                A(tanh_g[:, 716:T], ps[:, 6, 0:356], ACT.Tanh, scale=0.5).then_inc(g_read, 1)
                act.wait_ge(w_loaded[1], c * 32 + 32)
                w_hi_part(0, 1)
                if not fst:
                    act.wait_ge(a_done, c)
                act.wait_ge(par_ready, 1)
                act.wait_ge(der, DER_STEPS)
                A(par_a[:, :], par[:, bass.ds(c, 1), :], ACT.Copy).then_inc(para, 1)
                act.wait_ge(para, c + 1)
                act.wait_ge(proj, c * (3 * NS) + 6)
                act.wait_ge(w_loaded[0], c * 48 + 48)
                w_hi_part(1, 0)
                if not fst:
                    act.wait_ge(gates, 6 * c)
                act.wait_ge(gatew_loaded, 64)
                for b in range(2):
                    r = slice(64 * b, 64 * b + 64)
                    act.wait_ge(gatew_loaded, 64)
                    A(gate_h[r, :, 64 * b:64 * b + 64], gate_w[r, :, bass.ds(c, 1), :], ACT.Copy)\
                        .then_inc(gwh, 1)
                act.wait_ge(v_read, 3 * c + 3)
                if not fst:
                    act.wait_ge(conv_done, c)
                A(acc[:, :], cv_in[:, META:META + C_LEN], ACT.Identity, scale=par_a[:, Q_CW:Q_CW + 1],
                  bias=par_a[:, P_CB:P_CB + 1]).then_inc(tap0, 1)
                if not fst:
                    act.wait_ge(st_saved, 6 * c)
                    act.wait_ge(rtaps, 3 * c)
                A(rg_in[:, RPAD + META + SEQ:R_SAMPLE_IN], par_a[:, P_RS:P_RS + RPAD], ACT.Copy).then_inc(st_read, 1)
                act.wait_ge(proj, c * (3 * NS) + 8)
                A(rg_in[:, RPAD:RPAD + 716].rearrange("p (j n) -> p j n", j=2), ps[:, 6:8, 0:358],
                  ACT.Copy).then_inc(x_read, 1)
                act.wait_ge(proj, c * (3 * NS) + 9)
                A(rg_in[:, RPAD + 716:RPAD + META + SEQ], ps[:, 0, 0:324], ACT.Copy).then_inc(x_read, 1)
                A(rg_in[:, R_SAMPLE_IN:R_SAMPLE_IN + DEC], ps[:, 0, 324:356], ACT.Copy).then_inc(x_read, 1)
                act.wait_ge(st_read, c + 1)
                act.wait_ge(x_read, 3 * c + 3)
                if not fst:
                    act.wait_ge(ix_done, c)
                A(rg_x[:, :], rg_in[:, 0:R_LEN], ACT.Identity, scale=par_a[:, P_RW:P_RW + 1],
                  bias=par_a[:, P_RB:P_RB + 1]).then_inc(rtap0, 1)
                act.wait_ge(rtaps, 3 * c + 3)
                A(rg_xh[:, :], rg_x[:, :], ACT.Copy).then_inc(rgxh, 1)
                act.wait_ge(proj, c * (3 * NS) + 12)
                if not fst:
                    act.wait_ge(sgc_out, 16 * c)
                A(silu_gc[:, :].rearrange("p (j n) -> p j n", j=3), ps[:, 4:7, 0:OCH], ACT.Silu)\
                    .then_inc(gc_read, 1)
                act.wait_ge(w_loaded[0], c * 48 + 64)
                w_hi_part(0, 0)
                if not fst:
                    act.wait_ge(h_done, 2 * c)
                for j in range(3):
                    cols = slice(j * R_CH, (j + 1) * R_CH)
                    act.wait_ge(gates, 6 * c + 2 * j + 1)
                    A(ra[:, cols], ps[:, GATE_R_BANK, 0:R_CH], ACT.Tanh, scale=0.5,
                      bias=par_a[:, Q_BA:Q_BA + 1]).then_inc(gates_read, 1)
                    act.wait_ge(gates, 6 * c + 2 * j + 2)
                    A(rd[:, cols], ps[:, GATE_I_BANK, 0:R_CH], ACT.Tanh, scale=0.5,
                      bias=par_a[:, Q_BX:Q_BX + 1]).then_inc(gates_read, 1)
                act.wait_ge(proj, c * (3 * NS) + 15)
                if not fst:
                    act.wait_ge(y_done, 2 * c)
                A(silu_gr[:, :].rearrange("p (j n) -> p j n", j=3), ps[:, 1:4, 0:OCH], ACT.Silu)\
                    .then_inc(gr_read, 1)
                act.wait_ge(gates_read, 6 * c + 6)
                if not fst:
                    act.wait_ge(st_saved, 6 * c)
                A(rb[:, :], ra[:, :], ACT.Tanh, scale=par_a[:, Q_SP:Q_SP + 1],
                  bias=par_a[:, Q_SP:Q_SP + 1]).then_inc(th_done, 1)
                act.wait_ge(th_done, c + 1)
                A(ra[:, :], ra[:, :], ACT.Exp, scale=par_a[:, Q_NSP:Q_NSP + 1],
                  bias=par_a[:, Q_NSP:Q_NSP + 1]).then_inc(a_done, 1)
                act.wait_ge(a_done, c + 1)
                A(rc[:, :], ra[:, :], ACT.Square).then_inc(a2_done, 1)
                act.wait_ge(w_loaded[1], c * 32 + 48)
                w_hi_part(1, 1)
                if not last:
                    act.wait_ge(w_loaded[0], c * 48 + 80)
                    w_hi_part(2, 0)
                act.wait_ge(q_done, c + 1)
                A(rc[:, :], rc[:, :], ACT.Sqrt, scale=0.25).then_inc(root_done, 1)

            tile(0, True, False)
            with act.Fori(1, KT - 1) as c:
                tile(c, False, False)
            tile(KT - 1, False, True)

            act.wait_ge(st_turned, 1)
            act.wait_ge(b_done, KT)
            for i in range(2):
                A(state_rows[0:NOUT, i * 512:(i + 1) * 512], ps[0:NOUT, 3 + 4 * i, :], ACT.Copy)\
                    .then_inc(st_rows, 1)
            act.wait_ge(sgc_out, 16 * KT)
            act.wait_ge(y_done, 2 * KT)
            for c in range(KT):
                act.wait_ge(centred, c + 1)
                if c >= 2:
                    act.wait_ge(sq_used, c - 1)
                A(sqs[:, c % 2, :], conv_out[:, c, :], ACT.Square).then_inc(squared, 1)
            act.wait_ge(sq_used, KT)
            A(rstd_b[:, :].rearrange("p (j n) -> p j n", j=3), ps[:, 4:7, 0:C_CH], ACT.Ln,
              bias=eps_col[:, :]).then_inc(ln_rstd, 1)
            act.wait_ge(ln_rstd, 1)
            A(rstd_b[:, :], rstd_b[:, :], ACT.Exp, scale=-0.5).then_inc(ln_rstd, 1)
            act.preload_act_table(ACT.Silu)
            for c in range(KT + 1):
                if c < KT:
                    act.wait_ge(z_done, c + 1)
                    if c >= 2:
                        act.wait_ge(v_lo, 2 * c - 2)
                    A(silu_v[:, c % 2, :], conv_out[:, c, :], ACT.Silu, scale=par[:, c, P_LG:P_LG + 1],
                      bias=par[:, c, P_LB:P_LB + 1]).then_inc(ln_silu, 1)
                if c >= 1:
                    act.wait_ge(ln_silu, c)
                    A(act_hi[:, c - 1, 0:SEQ], silu_v[:, (c - 1) % 2, 0:SEQ], ACT.Copy).then_inc(v_hi, 1)
                    A(act_hi[:, c - 1, SEQ:TO], silu_v[:, (c - 1) % 2, C_SAMPLE:C_LEN], ACT.Copy)\
                        .then_inc(v_hi, 1)
            with act.Fori(0, KT // 2) as p:
                for h in range(2):
                    act.wait_ge(pw, p * 2 + h + 1)
                    act.wait_ge(w_loaded[h], p * 16 + 16 * ((3 if h == 0 else 2) * KT + 2))
                    w_hi_part(h, h)
            act.wait_ge(pw, KT)
            for k in range(KT):
                act.wait_ge(yc, k + 1)
                A(act_hi[:, k, 0:TO], conv_out[:, k, 0:TO], ACT.Copy).then_inc(yh, 1)
            act.wait_ge(yr_in, 16)
            for k in range(KT):
                A(act_lo[:, k, 0:TO], yr[:, k, :], ACT.Copy).then_inc(yh, 1)

            def o_chunk(e, j, fst, tokens=0):
                c0, n = YCH[j]
                act.wait_ge(oproj, e * 3 + j + 1)
                act.wait_ge(par_ready, 1)
                A(o_t[:, bass.ds(e, 1), c0:c0 + n], ps[:, j, 0:n], ACT.Copy,
                  scale=par[:, bass.ds(e, 1), P_PG:P_PG + 1].rearrange("p a n -> p (a n)"))\
                    .then_inc(o_copied, 1)
                if not (fst and j == 0):
                    act.wait_ge(o_ssq, e * 3 + j)
                if tokens:
                    act.wait_ge(ss_root, tokens)
                A(ps[:, 3, 0:n], ps[:, j, 0:n], ACT.Square).then_inc(o_sq, 1)

            n_loads = [3 * KT + 1 + KT // 2, 2 * KT + 1 + KT // 2]

            def o_tile(e, fst):
                act.wait_ge(half_done, e + 1)
                act.wait_ge(w_loaded[0], e * 16 + 16 * (n_loads[0] + 1))
                w_hi_part(0, 0)
                for j in range(3):
                    o_chunk(e, j, fst)
                act.wait_ge(w_loaded[1], e * 16 + 16 * (n_loads[1] + 1))
                w_hi_part(1, 1)

            o_tile(0, True)
            with act.Fori(1, KT - 1) as e:
                o_tile(e, False)
            e = KT - 1
            act.preload_act_table(ACT.Sqrt)
            for j in range(3):
                o_chunk(e, j, False, tokens=3 * j)
                act.wait_ge(ss_done, j + 1)
                for i, (c0, rows) in enumerate(out_tiles[j]):
                    A(rs_o[0:rows, 0, 3 * j + i:3 * j + i + 1], ps[0:rows, 3, i:i + 1], ACT.Sqrt,
                      bias=eps_col[0:rows, :]).then_inc(ss_root, 1)

        @block.vector
        def _(dve):
            STT, TT, TS = dve.scalar_tensor_tensor, dve.tensor_tensor, dve.tensor_scalar

            def w_lo_part(slot, stage, hi_count):
                dve.wait_ge(w_his, hi_count)
                TT(WLO[slot], wstage[:, stage], WHI[slot], ALU.subtract).then_inc(w_los, 1)

            def x_norm_part(t):
                rows = x_rows[t]
                dve.wait_ge(x_rt, t + 1)
                dve.reciprocal(sums[0:rows, t:t + 1], sums[0:rows, t:t + 1]).then_inc(x_rs, 1)
                dve.wait_ge(x_rs, t + 1)
                if t == 0:
                    dve.wait_ge(g_loaded, 16)
                if t >= 2:
                    dve.wait_ge(x_turned, t - 1)
                STT(out=x_norm[0:rows, t % 2, :], in0=x_in[0:rows, t % 4, :], scalar=sums[0:rows, t:t + 1],
                    in1=g_bcast[0:rows, :], op0=ALU.mult, op1=ALU.mult).then_inc(x_normed, 1)

            def x_lo_part(t):
                rows = x_rows[t]
                b = 2 * (t % 2)
                dve.wait_ge(x_hi, t + 1)
                src = ps[:, b:b + 2, :].rearrange("p b (k t) -> p (b k) t", t=P)[:, :, 0:rows]
                TT(act_lo[:, :, t * P:t * P + rows], src, act_hi[:, :, t * P:t * P + rows],
                   ALU.subtract).then_inc(x_lo, 1)

            for t in range(NX + 1):
                if t < NX:
                    x_norm_part(t)
                if t == 2:
                    w_lo_part(0, 0, 1)
                if t >= 1:
                    x_lo_part(t - 1)
            w_lo_part(1, 1, 2)

            step = [0]

            def chain(ins):
                step[0] += 1
                ins.then_inc(der, 1)
                dve.wait_ge(der, step[0])

            dve.wait_ge(par_ready, 1)
            lam = par[:, :, P_LAM]
            neg, z, s, s2 = (small[:, i, :] for i in range(4))
            poly = prm[:, 0, :]
            chain(TS(neg, lam, -1.0, None, ALU.mult))
            TT(z, lam, neg, ALU.max).then_inc(der, 1)
            step[0] += 1
            dve.wait_ge(der_exp, 1)
            chain(TS(s, z, 2.0, None, ALU.add))
            chain(dve.reciprocal(s2, s))
            chain(TT(s, s2, z, ALU.mult))
            chain(TT(s2, s, s, ALU.mult))
            chain(TS(poly, s2, 1.0 / 17.0, None, ALU.mult))
            for d in (15, 13, 11, 9, 7, 5, 3):
                chain(STT(out=poly, in0=poly, scalar=1.0 / d, in1=s2, op0=ALU.add, op1=ALU.mult))
            chain(STT(out=poly, in0=poly, scalar=1.0, in1=s, op0=ALU.add, op1=ALU.mult))
            chain(TS(neg, neg, 0.0, None, ALU.max))
            chain(TS(neg, neg, 0.5, None, ALU.mult))
            chain(TT(poly, poly, neg, ALU.add))
            chain(TS(par[:, :, Q_SP], poly, 8.0, None, ALU.mult))
            TS(par[:, :, Q_NSP], poly, -8.0, None, ALU.mult).then_inc(der, 1)
            TS(par[:, :, Q_CW:Q_CW + CW], par[:, :, P_CW:P_CW + CW], 0.5, None, ALU.mult).then_inc(der, 1)
            TS(par[:, :, Q_BA:Q_BA + 2], par[:, :, P_BA:P_BA + 2], 0.5, None, ALU.mult).then_inc(der, 1)
            step[0] += 3
            dve.wait_ge(der, step[0])
            assert step[0] == DER_STEPS
            w_lo_part(2, 0, 3)
            dve.wait_ge(pads, 3)

            def tile(c, fst, last):
                def tap(k):
                    if k == 1:
                        dve.wait_ge(tap0, c + 1)
                    else:
                        dve.wait_ge(taps, c * (CPAD - 1) + k - 1)
                    if k < CPAD:
                        STT(out=acc[:, :], in0=cv_in[:, META + k:META + k + C_LEN],
                            scalar=par_v[:, Q_CW + k:Q_CW + k + 1], in1=acc[:, :], op0=ALU.mult,
                            op1=ALU.add).then_inc(taps, 1)
                    else:
                        STT(out=conv_out[:, bass.ds(c, 1), :].rearrange("p a n -> p (a n)"),
                            in0=cv_in[:, META + k:META + k + C_LEN],
                            scalar=par_v[:, Q_CW + k:Q_CW + k + 1], in1=acc[:, :], op0=ALU.mult,
                            op1=ALU.add).then_inc(conv_done, 1)

                def rtap(k):
                    if k == 1:
                        dve.wait_ge(rtap0, c + 1)
                    else:
                        dve.wait_ge(rtaps, 3 * c + k - 1)
                    STT(out=rg_x[:, :], in0=rg_in[:, k:k + R_LEN], scalar=par_v[:, P_RW + k:P_RW + k + 1],
                        in1=rg_x[:, :], op0=ALU.mult, op1=ALU.add).then_inc(rtaps, 1)

                if not fst:
                    dve.wait_ge(conv_done, c)
                    dve.wait_ge(h_done, 2 * c)
                dve.tensor_copy(par_v[:, :], par[:, bass.ds(c, 1), :].rearrange("p a n -> p (a n)")).then_inc(parv, 1)
                dve.wait_ge(parv, c + 1)
                if not fst:
                    dve.wait_ge(st_saved, 6 * c)
                TS(cv_in[:, CPAD + META + SEQ:V_SAMPLE_IN], par_v[:, P_CS:P_CS + CPAD], 2.0, None,
                   ALU.mult).then_inc(parv2, 1)
                dve.wait_ge(g_read, 2 * c + 2)
                dve.wait_ge(proj, c * (3 * NS) + 6)
                STT(out=cv_in[:, CPAD:CPAD + 716].rearrange("p (j n) -> p j n", j=2),
                    in0=tanh_g[:, 0:716].rearrange("p (j n) -> p j n", j=2), scalar=1.0,
                    in1=ps[:, 0:2, 0:358], op0=ALU.add, op1=ALU.mult).then_inc(v_read, 1)
                STT(out=cv_in[:, CPAD + 716:CPAD + META + SEQ], in0=tanh_g[:, 716:META + SEQ], scalar=1.0,
                    in1=ps[:, 2, 0:324], op0=ALU.add, op1=ALU.mult).then_inc(v_read, 1)
                dve.wait_ge(parv2, c + 1)
                STT(out=cv_in[:, V_SAMPLE_IN:V_IN], in0=tanh_g[:, META + SEQ:T], scalar=1.0,
                    in1=ps[:, 2, 324:356], op0=ALU.add, op1=ALU.mult).then_inc(v_read, 1)
                w_lo_part(0, 1, c * NS + 4)
                dve.wait_ge(v_read, 3 * c + 3)
                for k in range(1, 4):
                    tap(k)
                w_lo_part(1, 0, c * NS + 5)
                for b in range(2):
                    r = slice(64 * b, 64 * b + 64)
                    dve.wait_ge(gwh, 2 * c + b + 1)
                    TT(gate_l[r, :, 64 * b:64 * b + 64],
                       gate_w[r, :, bass.ds(c, 1), :].rearrange("p m a j -> p m (a j)"),
                       gate_h[r, :, 64 * b:64 * b + 64], ALU.subtract).then_inc(gwl, 1)
                TS(states[:, bass.ds(c, 1), O_CP:O_CP + CPAD], cv_in[:, META + SEQ:META + SEQ + CPAD].rearrange("p (a n) -> p a n", a=1),
                   0.5, None, ALU.mult).then_inc(st_saved, 1)
                TS(states[:, bass.ds(c, 1), O_CS:O_CS + CPAD], cv_in[:, V_IN - CPAD:V_IN].rearrange("p (a n) -> p a n", a=1),
                   0.5, None, ALU.mult).then_inc(st_saved, 1)
                for k in range(4, 7):
                    tap(k)
                rtap(1)
                tap(7)
                rtap(2)
                tap(8)
                rtap(3)
                dve.tensor_copy(states[:, bass.ds(c, 1), O_RP:O_RP + RPAD],
                                rg_in[:, META + SEQ:META + SEQ + RPAD].rearrange("p (a n) -> p a n", a=1)).then_inc(st_saved, 1)
                dve.tensor_copy(states[:, bass.ds(c, 1), O_RS:O_RS + RPAD],
                                rg_in[:, R_SAMPLE_IN + DEC - RPAD:R_SAMPLE_IN + DEC].rearrange("p (a n) -> p a n", a=1)).then_inc(st_saved, 1)
                tap(9)
                tap(10)
                dve.wait_ge(rgxh, c + 1)
                TT(rg_xl[:, :], rg_x[:, :], rg_xh[:, :], ALU.subtract).then_inc(rgxl, 1)
                for k in range(11, 15):
                    tap(k)
                w_lo_part(0, 0, c * NS + 6)
                for k in range(15, 21):
                    tap(k)
                dve.wait_ge(gates_read, 6 * c + 6)
                STT(out=rd[:, :], in0=rd[:, :], scalar=1.0, in1=rg_x[:, :], op0=ALU.add,
                    op1=ALU.mult).then_inc(ix_done, 1)
                for k in range(21, 24):
                    tap(k)
                dve.wait_ge(a2_done, c + 1)
                STT(out=rc[:, :], in0=rc[:, :], scalar=1.0, in1=rb[:, :], op0=ALU.add,
                    op1=ALU.mult).then_inc(q_done, 1)
                tap(24)
                w_lo_part(1, 1, c * NS + 7)
                tap(25)
                if not last:
                    w_lo_part(2, 0, c * NS + 8)
                dve.wait_ge(root_done, c + 1)
                dve.wait_ge(ix_done, c + 1)
                TT(rc[:, :], rc[:, :], rd[:, :], ALU.mult).then_inc(b_done, 1)
                tap(26)
                dve.wait_ge(b_done, c + 1)
                dve.tensor_tensor_scan(rb[:, 0:META + SEQ], ra[:, 0:META + SEQ], rc[:, 0:META + SEQ], 0.0,
                                       ALU.mult, ALU.add).then_inc(h_done, 1)
                dve.tensor_tensor_scan(rb[:, R_SAMPLE:R_SAMPLE + DEC], ra[:, R_SAMPLE:R_SAMPLE + DEC],
                                       rc[:, R_SAMPLE:R_SAMPLE + DEC], par_v[:, P_H0:P_H0 + 1],
                                       ALU.mult, ALU.add).then_inc(h_done, 1)
                tap(27)
                dve.wait_ge(h_done, 2 * c + 2)
                dve.wait_ge(gr_read, c + 1)
                if not fst:
                    dve.wait_ge(yr_out, 16 * c)
                TT(y_rg[:, 0:SEQ], rb[:, META:META + SEQ], silu_gr[:, 0:SEQ], ALU.mult).then_inc(y_done, 1)
                TT(y_rg[:, SEQ:TO], rb[:, R_SAMPLE:R_SAMPLE + DEC], silu_gr[:, SEQ:TO], ALU.mult)\
                    .then_inc(y_done, 1)
                dve.tensor_copy(states[:, bass.ds(c, 1), O_HP:O_HP + 1], rb[:, META + SEQ - 1:META + SEQ].rearrange("p (a n) -> p a n", a=1))\
                    .then_inc(st_saved, 1)
                dve.tensor_copy(states[:, bass.ds(c, 1), O_HS:O_HS + 1], rb[:, R_SAMPLE + DEC - 1:R_SAMPLE + DEC].rearrange("p (a n) -> p a n", a=1))\
                    .then_inc(st_saved, 1)
                for k in range(28, CW):
                    tap(k)

            tile(0, True, False)
            with dve.Fori(1, KT - 1) as c:
                tile(c, False, False)
            tile(KT - 1, False, True)

            dve.wait_ge(mean_done, 1)
            for c in range(KT):
                t = conv_out[:, c, :].rearrange("p (j n) -> p j n", j=3)
                TT(t, t, ps[:, 0:3, 0:C_CH], ALU.subtract).then_inc(centred, 1)
            dve.wait_ge(ln_rstd, 2)

            def ln_lo(c):
                dve.wait_ge(v_hi, 2 * c + 2)
                TT(act_lo[:, c, 0:SEQ], silu_v[:, c % 2, 0:SEQ], act_hi[:, c, 0:SEQ],
                   ALU.subtract).then_inc(v_lo, 1)
                TT(act_lo[:, c, SEQ:TO], silu_v[:, c % 2, C_SAMPLE:C_LEN], act_hi[:, c, SEQ:TO],
                   ALU.subtract).then_inc(v_lo, 1)

            for c in range(KT + 2):
                if c < KT:
                    dve.wait_ge(squared, c + 1)
                    TT(conv_out[:, c, :], conv_out[:, c, :], rstd_b[:, :], ALU.mult).then_inc(z_done, 1)
                if c >= 2:
                    ln_lo(c - 2)
            with dve.Fori(0, KT // 2) as p:
                for h in range(2):
                    c = p * 2 + h
                    dve.wait_ge(pw, c + 1)
                    dve.wait_ge(silu_loaded[h], p * 16 + 16)
                    STT(out=conv_out[:, bass.ds(c, 1), 0:TO].rearrange("p a (j n) -> p (a j) n", j=3),
                        in0=ps[:, 4 * h:4 * h + 3, 0:OCH], scalar=par[:, bass.ds(c, 1), P_B2:P_B2 + 1].rearrange("p a n -> p (a n)"),
                        in1=silu_l[:, h].rearrange("p (j n) -> p j n", j=3), op0=ALU.add,
                        op1=ALU.mult).then_inc(yc, 1)
                    w_lo_part(h, h, p * 2 + N_PW + 3 + h)
            for k in range(KT):
                dve.wait_ge(yh, k + 1)
                TT(yc_lo[:, k, 0:TO], conv_out[:, k, 0:TO], act_hi[:, k, 0:TO], ALU.subtract).then_inc(yl, 1)
            for k in range(KT):
                dve.wait_ge(yh, KT + k + 1)
                TT(yr_lo[:, k, :], yr[:, k, :], act_lo[:, k, 0:TO], ALU.subtract).then_inc(yl, 1)

            def add_squares(e, j, fst):
                c0, n = YCH[j]
                dve.wait_ge(o_sq, e * 3 + j + 1)
                if fst:
                    dve.tensor_copy(ssq[:, c0:c0 + n], ps[:, 3, 0:n]).then_inc(o_ssq, 1)
                else:
                    dve.wait_ge(o_ssq, e * 3 + j - 2)
                    TT(ssq[:, c0:c0 + n], ssq[:, c0:c0 + n], ps[:, 3, 0:n], ALU.add).then_inc(o_ssq, 1)

            def o_tile(e, fst):
                w_lo_part(0, 0, e * 2 + N_OUT + 3)
                for j in range(3):
                    add_squares(e, j, fst)
                w_lo_part(1, 1, e * 2 + N_OUT + 4)

            o_tile(0, True)
            with dve.Fori(1, KT - 1) as e:
                o_tile(e, False)
            e = KT - 1

            def finish(j):
                for i, (c0, rows) in enumerate(out_tiles[j]):
                    n = 3 * j + i
                    dve.wait_ge(ss_root, n + 1)
                    dve.reciprocal(rs_o[0:rows, 1, n:n + 1], rs_o[0:rows, 0, n:n + 1]).then_inc(ss_rs, 1)
                    dve.wait_ge(ss_rs, n + 1)
                    dve.wait_ge(o_turned, n + 1)
                    dve.wait_ge(xr_loaded[n % 2], 16 * (n // 2 + 1))
                    if n >= 2:
                        dve.wait_ge(y_stored[n % 2], 16 * (n // 2))
                    b = 4 + 2 * (n % 2)
                    STT(out=y_out[0:rows, n % 2].rearrange("p (b n) -> p b n", b=2), in0=ps[0:rows, b:b + 2, :],
                        scalar=rs_o[0:rows, 1, n:n + 1],
                        in1=x_res[0:rows, n % 2].rearrange("p (b n) -> p b n", b=2), op0=ALU.mult,
                        op1=ALU.add).then_inc(y_ready, 1)

            for j in range(3):
                add_squares(e, j, False)
                if j > 0:
                    finish(j - 1)
            finish(2)


_INS = ["x_prompt", "x_sample", "state_rg_h", "state_rg_conv", "state_cv_conv", "meta_tokens", "pre_norm_g",
        "w_in", "rg_conv_w", "rg_conv_b", "rg_wa", "rg_ba", "rg_wx", "rg_bx", "rg_lambda", "cv_conv_w",
        "cv_conv_b", "cv_ln_g", "cv_ln_b", "cv_w_pw2", "cv_b_pw2", "w_out", "post_norm_g"]
_OUTS = [(1, SEQ, D), (1, DEC, D), (1, 1, D), (1, 1, RPAD, D), (1, 1, CPAD, D),
         (1, 1, D), (1, 1, RPAD, D), (1, 1, CPAD, D)]


def kernel(**inputs):
    import concourse.bacc as bacc
    from concourse.bass_utils import run_bass_kernel_spmd

    nc = bacc.Bacc("TRN2", target_bir_lowering=False, num_devices=1)
    arrays, args = {}, []
    for name in _INS:
        a = np.ascontiguousarray(inputs[name])
        arrays[f"in_{name}"] = a
        args.append(nc.dram_tensor(f"in_{name}", a.shape, mybir.dt.from_np(a.dtype), kind="ExternalInput").ap())
    for i, shape in enumerate(_OUTS):
        args.append(nc.dram_tensor(f"out_{i}", shape, F32, kind="ExternalOutput").ap())
    build(nc, *args)
    r = run_bass_kernel_spmd(nc, [arrays], core_ids=[0])
    return tuple(r.results[0][f"out_{i}"] for i in range(len(_OUTS)))
```

```python
from contextlib import ExitStack

import numpy as np

import concourse.bass as bass
from concourse import mybir
from concourse.alu_op_type import AluOpType as ALU

F32 = mybir.dt.float32
F32R = mybir.dt.float32r
ACT = mybir.ActivationFunctionType

P = 128
D = 1024
KT = D // P
META, SEQ, DEC = 16, 1024, 32
T = META + SEQ + DEC
TO = SEQ + DEC
EPS = 1e-6

XCH = [(0, 358), (358, 358), (716, 356)]
OCH = 352
assert sum(n for _, n in XCH) == T and 3 * OCH == TO

RW = 4
RPAD = RW - 1
R_SAMPLE_IN = RPAD + META + SEQ + RPAD
R_LEN = 1080
R_CH = R_LEN // 3
R_SAMPLE = R_SAMPLE_IN - RPAD
R_IN = R_LEN + RPAD
assert R_SAMPLE + DEC <= R_LEN

CW = 31
CPAD = CW - 1
V_SAMPLE_IN = CPAD + META + SEQ + CPAD
V_IN = V_SAMPLE_IN + DEC
C_LEN = SEQ + CPAD + DEC
C_SAMPLE = SEQ + CPAD
C_CH = C_LEN // 3
assert 3 * C_CH == C_LEN and META + C_LEN + CPAD == V_IN

P_CW, P_RW, P_RB, P_BA, P_BX, P_LAM, P_CB, P_LG, P_LB, P_B2, P_PG, P_H0, P_RS, P_CS = (
    0, 31, 35, 36, 37, 38, 39, 40, 41, 42, 43, 44, 45, 48)
PAR = P_CS + CPAD
Q_CW, Q_BA, Q_BX, Q_SP, Q_NSP = PAR, PAR + CW, PAR + CW + 1, PAR + CW + 2, PAR + CW + 3
PARQ = Q_NSP + 1

O_HP, O_HS, O_RP, O_RS, O_CP, O_CS = 0, 1, 2, 5, 8, 38
NOUT = O_CS + CPAD

SECTIONS = ["g", "v", "x", "gc", "gr"]
COLUMN = {"x": 0, "gr": 1, "v": 2, "g": 3, "gc": 4}
NS = len(SECTIONS)
ORDER = {s: i for i, s in enumerate(SECTIONS)}
WSLOT = {"g": 0, "v": 1, "x": 2, "gc": 0, "gr": 1}
BANK = {"g": 4, "v": 0, "x": 6, "gc": 4, "gr": 1}
GATE_R_BANK, GATE_I_BANK = 7, 0
X_BANK = [0, 2, 6]
LAST_GR_BANK = [7, 3, 7]

N_IN = NS * KT
N_PW = N_IN
N_OUT = N_IN + KT
SQ_TILES = [0, 1, 2, 3, 4, 6]
LO_POOL = [1, 3, 6]
LO_DVE = [0, 2, 4, 5, 7]
DER_STEPS = 22
YCH = [(0, 384), (384, 384), (768, 288)]


def build(nc, x_prompt, x_sample, state_rg_h, state_rg_conv, state_cv_conv, meta_tokens, pre_norm_g,
          w_in, rg_conv_w, rg_conv_b, rg_wa, rg_ba, rg_wx, rg_bx, rg_lambda, cv_conv_w, cv_conv_b,
          cv_ln_g, cv_ln_b, cv_w_pw2, cv_b_pw2, w_out, post_norm_g,
          y_prompt, y_sample, rg_h_p, rg_c_p, cv_c_p, rg_h_s, rg_c_s, cv_c_s):
    top = [(nc.sbuf_base + 31) // 32 * 32]

    def take(nbytes):
        at = top[0]
        top[0] = at + (nbytes + 31) // 32 * 32
        assert top[0] <= nc.sbuf_usable_end, (top[0], nc.sbuf_usable_end)
        return at

    def at(name, shape, dt, offset):
        return nc.alloc_sbuf_tensor_at(name, [P] + shape, dt, offset=offset)

    def new(name, shape, dt=F32):
        return at(name, shape, dt, take(4 * int(np.prod(shape))))

    act_hi = new("act_hi", [KT, T], F32R)
    act_lo = new("act_lo", [KT, T], F32R)
    conv_at = take(4 * KT * C_LEN)
    conv_out = at("conv_out", [KT, C_LEN], F32, conv_at)
    yc_lo = at("yc_lo", [KT, C_LEN], F32R, conv_at)
    wstage_at = take(2 * 4 * D)
    wstage = at("wstage", [2, KT, P], F32, wstage_at)
    w_hi = new("w_hi", [2, KT, P], F32R)
    w_lo = new("w_lo", [2, KT, P], F32R)
    w2_at = take(2 * 4 * D)
    w2_hi = at("w2_hi", [KT, P], F32R, w2_at)
    w2_lo = at("w2_lo", [KT, P], F32R, w2_at + 4 * D)
    par = new("par", [KT, PARQ])
    ident = new("ident", [P])
    mean_w = new("mean_w", [P])
    eps_col = new("eps_col", [1])
    WHI = [w_hi[:, 0], w_hi[:, 1], w2_hi[:, :, :]]
    WLO = [w_lo[:, 0], w_lo[:, 1], w2_lo[:, :, :]]
    arena = top[0]

    def phase(start):
        spot = [start]

        def put(name, shape, dt=F32):
            o = spot[0]
            spot[0] = (o + 4 * int(np.prod(shape)) + 31) // 32 * 32
            assert spot[0] <= nc.sbuf_usable_end, (name, spot[0], nc.sbuf_usable_end)
            return at(name, shape, dt, o)
        return put, spot

    put, spot = phase(conv_at)
    x_in = put("x_in", [4, D])
    x_norm = put("x_norm", [2, D])
    g_bcast = put("g_bcast", [D])
    sq_junk = put("sq_junk", [D])
    assert spot[0] <= conv_at + 4 * KT * C_LEN

    put, spot = phase(arena)
    ra = put("ra", [R_LEN])
    rb = put("rb", [R_LEN])
    rc = put("rc", [R_LEN])
    rd = put("rd", [R_LEN])
    rg_xl = at("rg_xl", [R_LEN], F32R, arena + 2 * 4 * R_LEN)
    rg_in = put("rg_in", [R_IN + 1])
    rg_x = put("rg_x", [R_LEN])
    rg_xh = put("rg_xh", [R_LEN], F32R)
    y_rg = put("y_rg", [TO])
    silu_gc = put("silu_gc", [TO])
    gate_w = put("gate_w", [2, KT, 64])
    gate_h = put("gate_h", [2, P], F32R)
    gate_l = put("gate_l", [2, P], F32R)
    par_cv = put("par_cv", [2, PARQ])
    par_rg = put("par_rg", [2, PARQ])
    states = put("states", [KT, NOUT])
    prm = put("prm", [KT])
    small = put("small", [4, KT])
    sums = put("sums", [16])
    cv_bufs = spot[0]
    tanh_g = put("tanh_g", [T])
    cv_in = put("cv_in", [2, V_IN])
    acc = put("acc", [C_LEN])
    csum = put("csum", [C_LEN])
    assert 4 * D <= 4 * R_LEN
    par_rows = at("par_rows", [D], F32, arena)

    put2, spot2 = phase(cv_bufs)
    sqs = put2("sqs", [4, C_LEN])
    rstd_at = spot2[0]
    rstd_b = put2("rstd_b", [C_LEN])
    silu_l = at("silu_l", [2, TO], F32, cv_bufs)
    state_rows = at("state_rows", [D], F32, rstd_at)
    assert arena + 4 * KT * TO <= cv_bufs
    yr = at("yr", [KT, TO], F32, arena)
    yr_lo = at("yr_lo", [KT, TO], F32R, arena)

    put3, _ = phase(arena + 4 * KT * TO)
    o_t = put3("o_t", [KT, TO])
    ssq = put3("ssq", [TO])
    rs_o = put3("rs_o", [3, 9])
    x_res = at("x_res", [2, D], F32, wstage_at)
    y_out = at("y_out", [2, D], F32, w2_at)

    ps = nc.alloc_psum_tensor("ps", [P, 8, 512], F32)
    silu_spill = nc.dram_tensor("silu_spill", [KT, P, TO], F32, kind="Internal").ap()
    yr_spill = nc.dram_tensor("yr_spill", [KT, P, TO], F32, kind="Internal").ap()

    ctx = ExitStack()
    with ctx:
        def sem(name):
            return ctx.enter_context(nc.semaphore(name))

        x_loaded = [sem(f"x_loaded{i}") for i in range(4)]
        g_loaded = sem("g_loaded")
        par_loaded = sem("par_loaded")
        gatew_loaded = sem("gatew_loaded")
        consts = sem("consts")
        x_ss = sem("x_ss")
        x_rt = sem("x_rt")
        x_rs = sem("x_rs")
        x_normed = sem("x_normed")
        x_turned = sem("x_turned")
        x_hi = sem("x_hi")
        x_lo = sem("x_lo")
        par_turned = sem("par_turned")
        par_ready = sem("par_ready")
        der = sem("der")
        der_exp = sem("der_exp")
        pads = sem("pads")
        w_loaded = [sem("w_loaded0"), sem("w_loaded1")]
        sp_steps = sem("sp_steps")
        w_his = sem("w_his")
        w_los = sem("w_los")
        late_los = sem("late_los")
        proj = sem("proj")
        g_read = sem("g_read")
        v_copied = sem("v_copied")
        one_added = sem("one_added")
        glu_done = sem("glu_done")
        x_read = sem("x_read")
        gc_read = sem("gc_read")
        gr_read = sem("gr_read")
        gates = sem("gates")
        gates_read = sem("gates_read")
        par_cv_set = sem("par_cv_set")
        par_rg_set = sem("par_rg_set")
        cv_state_set = sem("cv_state_set")
        pool_steps = sem("pool_steps")
        act_steps = sem("act_steps")
        taps = sem("taps")
        conv_done = sem("conv_done")
        rtap0 = sem("rtap0")
        rtaps = sem("rtaps")
        rgxh = sem("rgxh")
        rgxl = sem("rgxl")
        gwh = sem("gwh")
        gwl = sem("gwl")
        th_done = sem("th_done")
        a_done = sem("a_done")
        a2_done = sem("a2_done")
        ix_done = sem("ix_done")
        q_done = sem("q_done")
        root_done = sem("root_done")
        b_done = sem("b_done")
        h_done = sem("h_done")
        y_done = sem("y_done")
        cv_saved = sem("cv_saved")
        rg_saved = sem("rg_saved")
        h_saved = sem("h_saved")
        csummed = sem("csummed")
        st_read = sem("st_read")
        sgc_out = sem("sgc_out")
        yr_out = sem("yr_out")
        mean_done = sem("mean_done")
        centred = sem("centred")
        squared = sem("squared")
        sq_used = sem("sq_used")
        sq_paired = sem("sq_paired")
        var_done = sem("var_done")
        ln_rstd = sem("ln_rstd")
        z_done = sem("z_done")
        ln_silu = sem("ln_silu")
        v_hi = sem("v_hi")
        v_lo = [sem("v_lo0"), sem("v_lo1")]
        st_turned = sem("st_turned")
        st_rows = sem("st_rows")
        st_out = sem("st_out")
        silu_loaded = [sem("silu_loaded0"), sem("silu_loaded1")]
        pw = sem("pw")
        yc = sem("yc")
        yr_in = sem("yr_in")
        yh = sem("yh")
        yl = sem("yl")
        oproj = sem("oproj")
        half_done = sem("half_done")
        o_copied = sem("o_copied")
        o_sq = sem("o_sq")
        o_ssq = sem("o_ssq")
        ss_done = sem("ss_done")
        ss_root = sem("ss_root")
        ss_rs = sem("ss_rs")
        o_turned = sem("o_turned")
        y_ready = sem("y_ready")
        xr_loaded = [sem("xr_loaded0"), sem("xr_loaded1")]
        y_stored = [sem("y_stored0"), sem("y_stored1")]

        w_in_v = w_in.rearrange("d (k p) e -> p (d k) e", p=P)
        w_pw_v = cv_w_pw2.rearrange("d (k p) e -> p (d k) e", p=P)
        w_out_v = w_out.rearrange("d (h k p) e -> p (d h k) e", h=2, p=P)
        xp_v = x_prompt.rearrange("b t d -> (b t) d")
        xs_v = x_sample.rearrange("b t d -> (b t) d")

        first = P - META
        x_tiles = [[(0, meta_tokens, 0, META), (META, xp_v, 0, first)]]
        for t in range(1, 8):
            x_tiles.append([(0, xp_v, first + (t - 1) * P, P)])
        x_tiles.append([(0, xp_v, SEQ - META, META), (META, xs_v, 0, DEC)])
        x_rows = [P] * 8 + [META + DEC]
        NX = len(x_tiles)
        x_dmas = [len(t) for t in x_tiles]
        assert first + 7 * P == SEQ - META

        def x_landed(t):
            return 16 * sum(x_dmas[u] for u in range(t % 4, t + 1, 4))

        out_tiles = [[(0, P), (128, P), (256, P)], [(384, P), (512, P), (640, P)],
                     [(768, P), (896, P), (1024, DEC)]]

        par_src = [(P_CW, cv_conv_w[0]), (P_RW, rg_conv_w[0]), (P_RB, rg_conv_b), (P_BA, rg_ba),
                   (P_BX, rg_bx), (P_LAM, rg_lambda), (P_CB, cv_conv_b), (P_LG, cv_ln_g),
                   (P_LB, cv_ln_b), (P_B2, cv_b_pw2), (P_PG, post_norm_g), (P_H0, state_rg_h[0]),
                   (P_RS, state_rg_conv[0, 0]), (P_CS, state_cv_conv[0, 0])]

        block = ctx.enter_context(nc.Block())

        @block.sync
        def _(sp):
            def load_x(t):
                for row, src, r0, n in x_tiles[t]:
                    if t >= 4:
                        sp.wait_ge(x_normed, t - 3)
                    sp.dma_start(x_in[row:row + n, t % 4, :], src[r0:r0 + n, :]).then_inc(x_loaded[t % 4], 16)

            def load_w(slot, src):
                sp.dma_start(wstage[:, slot], src).then_inc(w_loaded[slot], 16)

            def w_in_cols(s, c):
                return w_in_v[:, :, bass.ds(c * P + COLUMN[s] * D, P)]

            def after_reg_wait():
                sp.sem_inc(sp_steps, 1)

            load_x(0)
            sp.dma_start(g_bcast[:, :], pre_norm_g.broadcast_to([P, D])).then_inc(g_loaded, 16)
            for t in range(1, 4):
                load_x(t)
            load_w(0, w_in_cols("g", 0))
            load_w(1, w_in_cols("v", 0))
            for t in range(4, NX):
                load_x(t)
            sp.wait_ge(w_los, 1)
            load_w(0, w_in_cols("x", 0))
            sp.wait_ge(w_los, 2)
            load_w(1, w_in_cols("v", 1))
            sp.wait_ge(w_los, 3)
            load_w(0, w_in_cols("g", 1))

            def loop_loads(c, fst, last):
                sp.wait_ge(w_los, c * NS + 4)
                after_reg_wait()
                load_w(0, w_in_cols("gr", c))
                sp.wait_ge(w_los, c * NS + 5)
                after_reg_wait()
                load_w(1, w_in_cols("gc", c))
                sp.wait_ge(w_los, c * NS + 6)
                after_reg_wait()
                load_w(1, w_in_cols("gr", KT - 1) if last else w_in_cols("v", c + 2))
                sp.wait_ge(w_los, c * NS + 7)
                after_reg_wait()
                load_w(0, w_in_cols("x", c + 1))
                sp.wait_ge(w_los, c * NS + 8)
                after_reg_wait()
                load_w(0, w_in_cols("gc", KT - 1) if last else w_in_cols("g", c + 2))
                sp.wait_ge(gc_read, c + 1)
                after_reg_wait()
                sp.dma_start(silu_spill[bass.ds(c, 1)], silu_gc[:, :]).then_inc(sgc_out, 16)
                if not fst:
                    sp.wait_ge(y_done, 2 * c)
                    after_reg_wait()
                    sp.dma_start(yr_spill[bass.ds(c - 1, 1)], y_rg[:, :]).then_inc(yr_out, 16)

            loop_loads(0, True, False)
            with sp.Fori(1, KT - 2) as c:
                loop_loads(c, False, False)
            loop_loads(KT - 2, False, True)
            sp.wait_ge(w_los, N_IN - 1)
            load_w(0, w_pw_v[:, :, 0:P])
            sp.wait_ge(w_los, N_IN)
            load_w(1, w_pw_v[:, :, P:2 * P])
            sp.wait_ge(y_done, 2 * (KT - 1))
            sp.dma_start(yr_spill[KT - 2], y_rg[:, :]).then_inc(yr_out, 16)
            sp.wait_ge(gc_read, KT)
            sp.dma_start(silu_spill[KT - 1], silu_gc[:, :]).then_inc(sgc_out, 16)

            sp.wait_ge(sgc_out, 16 * KT)
            sp.wait_ge(ln_rstd, 1)
            for h in range(2):
                sp.dma_start(silu_l[:, h], silu_spill[h]).then_inc(silu_loaded[h], 16)
            sp.wait_ge(late_los, N_PW - N_IN + 1)
            load_w(0, w_pw_v[:, :, 2 * P:3 * P])
            sp.wait_ge(late_los, N_PW - N_IN + 2)
            load_w(1, w_pw_v[:, :, 3 * P:4 * P])

            with sp.Fori(0, 2) as p:
                for h in range(2):
                    sp.wait_ge(yc, p * 2 + h + 1)
                    after_reg_wait()
                    sp.dma_start(silu_l[:, h], silu_spill[bass.ds(p * 2 + h + 2, 1)])\
                        .then_inc(silu_loaded[h], 16)
                    sp.wait_ge(late_los, p * 2 + N_PW - N_IN + 3 + h)
                    after_reg_wait()
                    load_w(h, w_pw_v[:, :, bass.ds(p * (2 * P) + (h + 4) * P, P)])
            sp.wait_ge(y_done, 2 * KT)
            sp.dma_start(yr_spill[KT - 1], y_rg[:, :]).then_inc(yr_out, 16)
            sp.wait_ge(yr_out, 16 * KT)
            sp.wait_ge(h_saved, 2 * KT)
            sp.dma_start(yr[:, :, :], yr_spill.rearrange("k p t -> p k t")).then_inc(yr_in, 16)
            for h in range(2):
                sp.wait_ge(yc, 4 + h + 1)
                sp.dma_start(silu_l[:, h], silu_spill[6 + h]).then_inc(silu_loaded[h], 16)
                sp.wait_ge(late_los, N_PW - N_IN + 7 + h)
                load_w(h, w_out_v[:, (1 - h) * KT:(2 - h) * KT, 0:P])
            with sp.Fori(1, KT) as e:
                for h in range(2):
                    sp.wait_ge(late_los, N_OUT - N_IN + 2 * e - 1 + h)
                    after_reg_wait()
                    load_w(h, w_out_v[:, (1 - h) * KT:(2 - h) * KT, bass.ds(e * P, P)])
            sp.wait_ge(late_los, N_OUT - N_IN + 2 * KT)
            flat = [t for j in out_tiles for t in j]
            for n, (c0, rows) in enumerate(flat[:2]):
                sp.dma_start(x_res[0:rows, n], xp_v[c0:c0 + rows, :]).then_inc(xr_loaded[n], 16)
            for n, (c0, rows) in enumerate(flat):
                dst, r0 = (y_prompt[0], c0) if c0 < SEQ else (y_sample[0], 0)
                sp.wait_ge(y_ready, n + 1)
                sp.dma_start(dst[r0:r0 + rows, :], y_out[0:rows, n % 2]).then_inc(y_stored[n % 2], 16)
                if n + 2 < len(flat):
                    c2, rows2 = flat[n + 2]
                    src, r2 = (xp_v, c2) if c2 < SEQ else (xs_v, 0)
                    sp.dma_start(x_res[0:rows2, n % 2], src[r2:r2 + rows2, :]).then_inc(xr_loaded[n % 2], 16)
            sp.wait_ge(y_stored[0], 16 * 5)
            sp.wait_ge(y_stored[1], 16 * 4)

        @block.gpsimd
        def _(pool):
            pool.memset(ident[:, :], 0.0).then_inc(consts, 1)
            pool.memset(mean_w[:, :], 1.0 / D).then_inc(consts, 1)
            pool.memset(eps_col[:, :], EPS).then_inc(consts, 1)
            pool.memset(gate_h[:, :, :].bitcast(F32), 0.0).then_inc(consts, 1)
            pool.memset(gate_l[:, :, :].bitcast(F32), 0.0).then_inc(consts, 1)
            pool.wait_ge(consts, 5)
            pool.affine_select(out=ident[:, :], in_=ident[:, :], compare_op=ALU.not_equal, fill=1.0,
                               base=0, pattern=[[-1, P]], channel_multiplier=1).then_inc(consts, 1)
            for row, src in par_src:
                n = src.shape[0]
                pool.dma_start(par_rows[row:row + n, :], src).then_inc(par_loaded, 16)
            for m, w in enumerate((rg_wa, rg_wx)):
                for b in range(2):
                    pool.dma_start(gate_w[64 * b:64 * b + 64, m],
                                   w[0].rearrange("(c b) i j -> b i c j", b=2)[b]).then_inc(gatew_loaded, 16)
            TT = pool.tensor_tensor

            def take_wait():
                pool.sem_inc(pool_steps, 1)

            def w_lo_part(slot, stage, n):
                pool.wait_ge(w_his, n)
                TT(WLO[slot], wstage[:, stage], WHI[slot], ALU.subtract).then_inc(w_los, 1)

            def add_one(d):
                pool.wait_ge(g_read, 2 * d + 2)
                take_wait()
                pool.tensor_scalar(tanh_g[:, :], tanh_g[:, :], 1.0, None, ALU.add).then_inc(one_added, 1)

            def conv_input(d, b):
                pool.wait_ge(v_copied, 3 * d + 3)
                pool.wait_ge(one_added, d + 1)
                for lo, hi, src in ((CPAD, CPAD + META + SEQ, tanh_g[:, 0:META + SEQ]),
                                    (V_SAMPLE_IN, V_IN, tanh_g[:, META + SEQ:T])):
                    TT(cv_in[:, b, lo:hi], src, cv_in[:, b, lo:hi], ALU.mult).then_inc(glu_done, 1)

            def rg_low(c):
                pool.wait_ge(rgxh, c + 1)
                if not (isinstance(c, int) and c == 0):
                    pool.wait_ge(h_done, 2 * c)
                TT(rg_xl[:, :], rg_x[:, :], rg_xh[:, :], ALU.subtract).then_inc(rgxl, 1)

            def y_part(c, gr_reads):
                pool.wait_ge(h_done, 2 * c + 2)
                pool.wait_ge(gr_read, gr_reads)
                TT(y_rg[:, 0:SEQ], rb[:, META:META + SEQ], y_rg[:, 0:SEQ], ALU.mult).then_inc(y_done, 1)
                TT(y_rg[:, SEQ:TO], rb[:, R_SAMPLE:R_SAMPLE + DEC], y_rg[:, SEQ:TO], ALU.mult)\
                    .then_inc(y_done, 1)

            def tile(c, b, fst, second):
                add_one(c + 1)
                w_lo_part(0, 1, c * NS + 6)
                conv_input(c + 1, 1 - b)
                w_lo_part(1, 0, c * NS + 7)
                w_lo_part(2, 0, c * NS + 8)
                rg_low(c)
                if not fst:
                    y_part(c - 1, c)
                w_lo_part(0, 0, c * NS + 9)
                w_lo_part(1, 1, c * NS + 10)
                if not fst:
                    pool.wait_ge(conv_done, c + 1)
                    if second:
                        TT(csum[:, :], conv_out[:, 0, :], conv_out[:, 1, :], ALU.add).then_inc(csummed, 1)
                    else:
                        pool.wait_ge(csummed, c - 1)
                        take_wait()
                        TT(csum[:, :].rearrange("p (a n) -> p a n", a=1), csum[:, :].rearrange("p (a n) -> p a n", a=1),
                           conv_out[:, bass.ds(c, 1), :], ALU.add).then_inc(csummed, 1)

            w_lo_part(0, 0, 1)
            w_lo_part(1, 1, 2)
            w_lo_part(2, 0, 3)
            pool.wait_ge(par_turned, 1)
            pool.memset(rg_in[:, 0:RPAD], 0.0).then_inc(pads, 1)
            pool.memset(rg_in[:, R_SAMPLE_IN + DEC:R_IN + 1], 0.0).then_inc(pads, 1)
            pool.memset(cv_in[:, :, 0:CPAD], 0.0).then_inc(pads, 1)
            pool.wait_ge(pads, 3)
            add_one(0)
            w_lo_part(0, 0, 4)
            conv_input(0, 0)
            w_lo_part(1, 1, 5)
            tile(0, 0, True, False)
            tile(1, 1, False, True)
            tile(2, 0, False, False)
            with pool.Fori(1, KT // 2 - 1) as i:
                tile(i * 2 + 1, 1, False, False)
                tile(i * 2 + 2, 0, False, False)
            rg_low(KT - 1)
            y_part(KT - 2, KT - 1)
            for i, k in enumerate(LO_POOL):
                pool.wait_ge(v_hi, 2 * k + 2)
                TT(act_lo[:, k, 0:SEQ], conv_out[:, k, 0:SEQ], act_hi[:, k, 0:SEQ],
                   ALU.subtract).then_inc(v_lo[0], 1)
                TT(act_lo[:, k, SEQ:TO], conv_out[:, k, C_SAMPLE:C_LEN], act_hi[:, k, SEQ:TO],
                   ALU.subtract).then_inc(v_lo[0], 1)
            y_part(KT - 1, KT - 1 + 3)
            pool.wait_ge(st_rows, 2)
            for dst, row, n in ((rg_h_p[0], O_HP, 1), (rg_h_s[0], O_HS, 1), (rg_c_p[0, 0], O_RP, RPAD),
                                (rg_c_s[0, 0], O_RS, RPAD), (cv_c_p[0, 0], O_CP, CPAD),
                                (cv_c_s[0, 0], O_CS, CPAD)):
                pool.dma_start(dst, state_rows[row:row + n, :]).then_inc(st_out, 16)
            pool.wait_ge(st_out, 16 * 6)

        @block.tensor
        def _(pe):
            def product(out, wh, wl, xh, xl, start, stop):
                pe.matmul(out, wh, xh, start=start, stop=False)
                pe.matmul(out, wh, xl, start=False, stop=False)
                return pe.matmul(out, wl, xh, start=False, stop=stop)

            def chunk(s, j, bank=None):
                bank = (BANK[s] + j) % 8 if bank is None else bank
                c0, n = (META + j * OCH, OCH) if s in ("gr", "gc") else XCH[j]
                w = WSLOT[s]
                for k in range(KT):
                    mm = product(ps[:, bank, 0:n], WHI[w][:, k], WLO[w][:, k],
                                 act_hi[:, k, c0:c0 + n], act_lo[:, k, c0:c0 + n], k == 0, k == KT - 1)
                mm.then_inc(proj, 1)

            def turn_x(t):
                rows = x_rows[t]
                pe.wait_ge(x_normed, t + 1)
                if t >= 3:
                    pe.wait_ge(x_lo, t - 2)
                for k in range(KT):
                    mm = pe.transpose(ps[:, X_BANK[t % 3] + k // 4, k % 4 * P:k % 4 * P + rows],
                                      x_norm[0:rows, t % 2, k * P:(k + 1) * P], ident[0:rows, 0:rows])
                mm.then_inc(x_turned, 1)

            def gate_chunk(j, banks=(GATE_R_BANK, GATE_I_BANK)):
                for m, bank in enumerate(banks):
                    mm = product(ps[:, bank, 0:R_CH], gate_h[:, m], gate_l[:, m],
                                 rg_xh[:, j * R_CH:(j + 1) * R_CH], rg_xl[:, j * R_CH:(j + 1) * R_CH],
                                 True, True)
                    mm.then_inc(gates, 1)

            def tile(c, fst):
                d = c + 1
                pe.wait_ge(w_los, c * NS + 4)
                if fst:
                    pe.wait_ge(g_read, 2)
                else:
                    pe.wait_ge(gc_read, c)
                for j in range(3):
                    if j == 1 and not fst:
                        pe.wait_ge(gates_read, 6 * c)
                    chunk("g", j)
                pe.wait_ge(w_los, c * NS + 5)
                if fst:
                    pe.wait_ge(v_copied, 3)
                else:
                    pe.wait_ge(gr_read, c)
                for j in range(3):
                    chunk("v", j)
                pe.wait_ge(g_read, 2 * d + 2)
                for j in range(3):
                    if j == 2:
                        pe.wait_ge(v_copied, 3 * d + 3)
                    chunk("x", j)
                pe.wait_ge(w_los, c * NS + 6)
                for j in range(3):
                    if j == 2:
                        pe.wait_ge(x_read, 3 * c + 1)
                    chunk("gc", j)
                pe.wait_ge(w_los, c * NS + 7)
                chunk("gr", 0)
                chunk("gr", 1)
                pe.wait_ge(x_read, 3 * c + 3)
                pe.wait_ge(rgxl, c + 1)
                pe.wait_ge(gwl, 2 * c + 2)
                gate_chunk(0)
                chunk("gr", 2)
                pe.wait_ge(gates_read, 6 * c + 2)
                gate_chunk(1)
                pe.wait_ge(gc_read, c + 1)
                gate_chunk(2, (5, 6))

            pe.wait_ge(consts, 6)
            for j, (t0, t1) in enumerate(((0, 5), (5, 8), (8, NX))):
                for t in range(t0, t1):
                    turn_x(t)
                pe.wait_ge(w_los, 1)
                pe.wait_ge(x_lo, 3 * j + 3)
                chunk("g", j)
            pe.wait_ge(par_loaded, 16 * len(par_src))
            for k in range(KT):
                mm = pe.transpose(ps[:, 3 + 4 * (k // 4), k % 4 * P:k % 4 * P + PAR],
                                  par_rows[0:PAR, k * P:(k + 1) * P], ident[0:PAR, 0:PAR])
            mm.then_inc(par_turned, 1)
            pe.wait_ge(w_los, 2)
            for j in range(3):
                chunk("v", j)
            pe.wait_ge(par_ready, 1)
            tile(0, True)
            with pe.Fori(1, KT - 1) as c:
                tile(c, False)

            c = KT - 1
            pe.wait_ge(w_los, c * NS + 3)
            pe.wait_ge(gates_read, 6 * c)
            for j in range(3):
                chunk("x", j)
            pe.wait_ge(w_los, N_IN - 1)
            pe.wait_ge(x_read, 3 * c + 1)
            for j in range(3):
                chunk("gc", j)
            pe.wait_ge(gr_read, c)
            pe.wait_ge(csummed, KT - 1)
            for j in range(3):
                mm = pe.matmul(ps[:, 1 + j, 0:C_CH], mean_w[:, :], csum[:, j * C_CH:(j + 1) * C_CH],
                               start=True, stop=True)
            mm.then_inc(mean_done, 1)
            pe.wait_ge(w_los, N_IN)
            pe.wait_ge(x_read, 3 * c + 3)
            chunk("gr", 0, LAST_GR_BANK[0])
            pe.wait_ge(gc_read, KT)
            for k in SQ_TILES:
                if k < 4:
                    pe.wait_ge(squared, k + 1)
                else:
                    pe.wait_ge(sq_paired, k // 2 - 1)
                for j in range(3):
                    mm = pe.matmul(ps[:, 4 + j, 0:C_CH], mean_w[:, :], sqs[:, k % 4, j * C_CH:(j + 1) * C_CH],
                                   start=(k == 0), stop=(k == SQ_TILES[-1]))
                mm.then_inc(sq_used, 1)
            pe.wait_ge(centred, KT)
            chunk("gr", 1, LAST_GR_BANK[1])
            pe.wait_ge(gr_read, c + 1)
            chunk("gr", 2, LAST_GR_BANK[2])
            pe.wait_ge(ln_rstd, 1)
            pe.wait_ge(rgxl, c + 1)
            pe.wait_ge(gwl, 2 * c + 2)
            gate_chunk(0, (4, 5))
            def pw_pair(p, fst):
                for h in range(2):
                    pe.wait_ge(late_los, p * 2 + N_PW - N_IN + h + 1)
                    if fst:
                        pe.wait_ge(centred, KT)
                        if h == 1:
                            pe.wait_ge(gates_read, 6 * KT - 4)
                    else:
                        pe.wait_ge(yc, p * 2 + h - 1)
                    for k in range(KT):
                        if fst:
                            if k in LO_POOL:
                                pe.wait_ge(v_lo[0], 2 * LO_POOL.index(k) + 2)
                            else:
                                pe.wait_ge(v_lo[1], 2 * LO_DVE.index(k) + 2)
                        for j in range(3):
                            mm = product(ps[:, 4 * h + j, 0:OCH], WHI[h][:, k], WLO[h][:, k],
                                         act_hi[:, k, j * OCH:(j + 1) * OCH],
                                         act_lo[:, k, j * OCH:(j + 1) * OCH], k == 0, k == KT - 1)
                    mm.then_inc(pw, 1)
                    if fst:
                        pe.wait_ge(gr_read, KT - 1 + 3)
                        pe.wait_ge(gates_read, 6 * KT - 4 + 2 * h)
                        gate_chunk(1 + h, (7, 3))

            pw_pair(0, True)
            with pe.Fori(1, KT // 2) as p:
                pw_pair(p, False)
            pe.wait_ge(gates_read, 6 * KT)
            pe.wait_ge(cv_saved, 2 * KT)
            pe.wait_ge(rg_saved, 2 * KT)
            pe.wait_ge(h_saved, 2 * KT)
            for k in range(KT):
                mm = pe.transpose(ps[0:NOUT, 3 + 4 * (k // 4), k % 4 * P:(k % 4 + 1) * P],
                                  states[:, k, :], ident[:, :])
            mm.then_inc(st_turned, 1)

            halves = [(act_hi, yc_lo), (act_lo, yr_lo)]

            def o_steps(h, k, j, start, stop):
                hi, lo = halves[h]
                c0, n = YCH[j]
                return product(ps[:, j, 0:n], WHI[h][:, k], WLO[h][:, k],
                               hi[:, k, c0:c0 + n], lo[:, k, c0:c0 + n], start, stop)

            pe.wait_ge(yc, KT)
            for h in range(2):
                pe.wait_ge(late_los, N_OUT - N_IN + 1 + h)
                for k in range(KT):
                    pe.wait_ge(yl, h * KT + k + 1)
                    for j in range(3):
                        mm = o_steps(h, k, j, h == 0 and k == 0, h == 1 and k == KT - 1)
                        if h == 1 and k == KT - 1:
                            mm.then_inc(oproj, 1)
                if h == 0:
                    mm.then_inc(half_done, 1)
            with pe.Fori(1, KT - 1) as e:
                for h in range(2):
                    pe.wait_ge(late_los, e * 2 + N_OUT - N_IN + 1 + h)
                    for j in range(3):
                        if h == 0:
                            pe.wait_ge(o_sq, e * 3 - 2 + j)
                        for k in range(KT):
                            mm = o_steps(h, k, j, h == 0 and k == 0, h == 1 and k == KT - 1)
                        if h == 1:
                            mm.then_inc(oproj, 1)
                    if h == 0:
                        mm.then_inc(half_done, 1)

            e = KT - 1

            def turn_out(j):
                pe.wait_ge(o_ssq, 3 * e + j + 1)
                for i, (c0, rows) in enumerate(out_tiles[j]):
                    mm = pe.matmul(ps[0:rows, 3, i:i + 1], ssq[:, c0:c0 + rows], mean_w[:, 0:1],
                                   start=(i == 0), stop=True, skip_group_check=True)
                mm.then_inc(ss_done, 1)
                for i, (c0, rows) in enumerate(out_tiles[j]):
                    n = 3 * j + i
                    if n >= 2:
                        pe.wait_ge(y_ready, n - 1)
                    for k in range(KT):
                        mm = pe.transpose(ps[0:rows, 4 + 2 * (n % 2) + k // 4, k % 4 * P:(k % 4 + 1) * P],
                                          o_t[:, k, c0:c0 + rows], ident[:, :])
                    mm.then_inc(o_turned, 1)

            pe.wait_ge(late_los, N_OUT - N_IN + 2 * KT)
            for j in range(3):
                pe.wait_ge(o_sq, 3 * e - 2 + j)
                for h in range(2):
                    for k in range(KT):
                        mm = o_steps(h, k, j, h == 0 and k == 0, h == 1 and k == KT - 1)
                mm.then_inc(oproj, 1)
                if j > 0:
                    turn_out(j - 1)
            turn_out(2)

        @block.scalar
        def _(act):
            A = act.activation

            def take_wait():
                act.sem_inc(act_steps, 1)

            def w_hi_part(slot, stage):
                A(WHI[slot], wstage[:, stage], ACT.Copy).then_inc(w_his, 1)

            act.preload_act_table(ACT.Sqrt)
            act.wait_ge(consts, 6)

            def x_stats(t):
                rows = x_rows[t]
                act.wait_ge(x_loaded[t % 4], x_landed(t))
                if t >= 1:
                    act.wait_ge(x_ss, t)
                A(sq_junk[0:rows, :], x_in[0:rows, t % 4, :], ACT.Square,
                  accum_out=sums[0:rows, t:t + 1]).then_inc(x_ss, 1)
                act.wait_ge(x_ss, t + 1)
                A(sums[0:rows, t:t + 1], sums[0:rows, t:t + 1], ACT.Sqrt, scale=1.0 / D,
                  bias=eps_col[0:rows, :]).then_inc(x_rt, 1)

            def x_hi_part(t):
                rows = x_rows[t]
                b = X_BANK[t % 3]
                act.wait_ge(x_turned, t + 1)
                A(act_hi[:, :, t * P:t * P + rows].rearrange("p (b k) t -> p b k t", b=2),
                  ps[:, b:b + 2, :].rearrange("p b (k t) -> p b k t", t=P)[:, :, :, 0:rows],
                  ACT.Copy).then_inc(x_hi, 1)

            for t in range(NX + 2):
                if t < NX:
                    x_stats(t)
                if t >= 2:
                    x_hi_part(t - 2)
                if t == 2:
                    act.wait_ge(w_loaded[0], 16)
                    w_hi_part(0, 0)
            act.wait_ge(w_loaded[1], 16)
            w_hi_part(1, 1)
            act.wait_ge(w_loaded[0], 32)
            w_hi_part(2, 0)
            act.wait_ge(par_turned, 1)
            A(par[:, :, 0:PAR].rearrange("p (b k) n -> p b k n", b=2),
              ps[:, 3:8:4, :].rearrange("p b (k n) -> p b k n", n=P)[:, :, :, 0:PAR],
              ACT.Copy).then_inc(par_ready, 1)
            act.wait_ge(der, 2)
            A(small[:, 1, :], small[:, 1, :], ACT.Exp, scale=-1.0).then_inc(der_exp, 1)
            def gate_tanh(d):
                n = 0 if isinstance(d, int) and d == 0 else d * (3 * NS) - 9
                act.wait_ge(proj, n + 2)
                if not (isinstance(d, int) and d == 0):
                    act.wait_ge(glu_done, 2 * d)
                A(tanh_g[:, 0:716].rearrange("p (j n) -> p j n", j=2), ps[:, 4:6, 0:358], ACT.Tanh,
                  scale=0.5).then_inc(g_read, 1)
                act.wait_ge(proj, n + 3)
                A(tanh_g[:, 716:T], ps[:, 6, 0:356], ACT.Tanh, scale=0.5).then_inc(g_read, 1)

            def cv_setup(d, b, reuse):
                if reuse:
                    act.wait_ge(conv_done, d - 1)
                    act.wait_ge(cv_saved, 2 * d - 2)
                    take_wait()
                A(par_cv[:, b:b + 1, :], par[:, bass.ds(d, 1), :], ACT.Copy).then_inc(par_cv_set, 1)
                A(cv_in[:, b:b + 1, CPAD + META + SEQ:V_SAMPLE_IN],
                  par[:, bass.ds(d, 1), P_CS:P_CS + CPAD], ACT.Copy, scale=2.0).then_inc(cv_state_set, 1)

            def copy_v(d, b):
                act.wait_ge(proj, 6 if isinstance(d, int) and d == 0 else d * (3 * NS) - 3)
                A(cv_in[:, b, CPAD:CPAD + 716].rearrange("p (j n) -> p j n", j=2), ps[:, 0:2, 0:358],
                  ACT.Copy).then_inc(v_copied, 1)
                A(cv_in[:, b, CPAD + 716:CPAD + META + SEQ], ps[:, 2, 0:324], ACT.Copy).then_inc(v_copied, 1)
                A(cv_in[:, b, V_SAMPLE_IN:V_IN], ps[:, 2, 324:356], ACT.Copy).then_inc(v_copied, 1)

            def rg_setup(c, b, fst, reuse):
                if reuse:
                    act.wait_ge(h_done, 2 * c - 2)
                    take_wait()
                A(par_rg[:, b:b + 1, :], par[:, bass.ds(c, 1), :], ACT.Copy).then_inc(par_rg_set, 1)
                act.wait_ge(par_rg_set, c + 1)
                if not fst:
                    act.wait_ge(gates, 6 * c)
                for i in range(2):
                    r = slice(64 * i, 64 * i + 64)
                    act.wait_ge(gatew_loaded, 64)
                    A(gate_h[r, :, 64 * i:64 * i + 64], gate_w[r, :, bass.ds(c, 1), :], ACT.Copy)\
                        .then_inc(gwh, 1)
                if not fst:
                    act.wait_ge(rg_saved, 2 * c)
                    act.wait_ge(rtaps, 3 * c)
                A(rg_in[:, RPAD + META + SEQ:R_SAMPLE_IN], par_rg[:, b, P_RS:P_RS + RPAD], ACT.Copy)\
                    .then_inc(st_read, 1)

            def root(c):
                act.wait_ge(q_done, c + 1)
                A(rc[:, :], rc[:, :], ACT.Sqrt, scale=0.25).then_inc(root_done, 1)

            def rg_input(c, b, n, fst):
                act.wait_ge(proj, n + 2)
                A(rg_in[:, RPAD:RPAD + 716].rearrange("p (j n) -> p j n", j=2), ps[:, 6:8, 0:358],
                  ACT.Copy).then_inc(x_read, 1)
                act.wait_ge(proj, n + 3)
                A(rg_in[:, RPAD + 716:RPAD + META + SEQ], ps[:, 0, 0:324], ACT.Copy).then_inc(x_read, 1)
                A(rg_in[:, R_SAMPLE_IN:R_SAMPLE_IN + DEC], ps[:, 0, 324:356], ACT.Copy).then_inc(x_read, 1)
                act.wait_ge(st_read, c + 1)
                act.wait_ge(x_read, 3 * c + 3)
                if not fst:
                    act.wait_ge(ix_done, c)
                A(rg_x[:, :], rg_in[:, 0:R_LEN], ACT.Identity, scale=par_rg[:, b, P_RW:P_RW + 1],
                  bias=par_rg[:, b, P_RB:P_RB + 1]).then_inc(rtap0, 1)

            def rg_high(c):
                act.wait_ge(rtaps, 3 * c + 3)
                A(rg_xh[:, :], rg_x[:, :], ACT.Copy).then_inc(rgxh, 1)

            def silu_of_gc(c, n, fst):
                act.wait_ge(proj, n + 3)
                if not fst:
                    act.wait_ge(sgc_out, 16 * c)
                A(silu_gc[:, :].rearrange("p (j n) -> p j n", j=3), ps[:, 4:7, 0:OCH], ACT.Silu)\
                    .then_inc(gc_read, 1)

            def gates_chunk(c, b, j, banks=(GATE_R_BANK, GATE_I_BANK)):
                cols = slice(j * R_CH, (j + 1) * R_CH)
                for m, (bank, dst, bias) in enumerate(zip(banks, (ra, rd), (Q_BA, Q_BX))):
                    act.wait_ge(gates, 6 * c + 2 * j + m + 1)
                    A(dst[:, cols], ps[:, bank, 0:R_CH], ACT.Tanh, scale=0.5,
                      bias=par_rg[:, b, bias:bias + 1]).then_inc(gates_read, 1)

            def decay(c, b, fst):
                act.wait_ge(gates_read, 6 * c + 6)
                if not fst:
                    act.wait_ge(h_saved, 2 * c)
                    act.wait_ge(y_done, 2 * c)
                A(rb[:, :], ra[:, :], ACT.Tanh, scale=par_rg[:, b, Q_SP:Q_SP + 1],
                  bias=par_rg[:, b, Q_SP:Q_SP + 1]).then_inc(th_done, 1)
                act.wait_ge(th_done, c + 1)
                A(ra[:, :], ra[:, :], ACT.Exp, scale=par_rg[:, b, Q_NSP:Q_NSP + 1],
                  bias=par_rg[:, b, Q_NSP:Q_NSP + 1]).then_inc(a_done, 1)
                act.wait_ge(a_done, c + 1)
                A(rc[:, :], ra[:, :], ACT.Square).then_inc(a2_done, 1)

            def tile(c, b, fst, last):
                n = c * (3 * NS) + 6
                act.preload_act_table(ACT.Silu)
                gate_tanh(c + 1)
                act.wait_ge(w_loaded[1], c * 32 + 48)
                w_hi_part(0, 1)
                cv_setup(c + 1, 1 - b, not fst)
                rg_setup(c, b, fst, not fst)
                copy_v(c + 1, 1 - b)
                act.wait_ge(w_loaded[0], c * 48 + 64)
                w_hi_part(1, 0)
                rg_input(c, b, n + 6, fst)
                if not fst:
                    root(c - 1)
                act.wait_ge(w_loaded[0], c * 48 + 80)
                w_hi_part(2, 0)
                rg_high(c)
                silu_of_gc(c, n + 9, fst)
                act.wait_ge(w_loaded[0], c * 48 + 96)
                w_hi_part(0, 0)
                if not fst:
                    act.wait_ge(h_done, 2 * c)
                    act.wait_ge(b_done, c)
                gates_chunk(c, b, 0)
                act.wait_ge(proj, n + 15)
                if not fst:
                    act.wait_ge(yr_out, 16 * c)
                act.wait_ge(w_loaded[1], c * 32 + 64)
                w_hi_part(1, 1)
                gates_chunk(c, b, 1)
                gates_chunk(c, b, 2, (5, 6))
                A(y_rg[:, :].rearrange("p (j n) -> p j n", j=3), ps[:, 1:4, 0:OCH], ACT.Silu)\
                    .then_inc(gr_read, 1)
                decay(c, b, fst)

            gate_tanh(0)
            act.wait_ge(w_loaded[0], 48)
            w_hi_part(0, 0)
            act.wait_ge(pads, 3)
            act.wait_ge(der, DER_STEPS)
            cv_setup(0, 0, False)
            copy_v(0, 0)
            act.wait_ge(w_loaded[1], 32)
            w_hi_part(1, 1)
            tile(0, 0, True, False)
            with act.Fori(0, KT // 2 - 1) as i:
                tile(i * 2 + 1, 1, False, False)
                tile(i * 2 + 2, 0, False, False)

            c = KT - 1
            n = c * (3 * NS) + 6
            rg_setup(c, 1, False, True)
            rg_input(c, 1, n, False)
            silu_of_gc(c, n + 3, False)
            rg_high(c)
            root(c - 1)
            act.preload_act_table(ACT.Silu)
            act.wait_ge(w_loaded[0], 16 * (3 * KT + 1))
            w_hi_part(0, 0)

            def last_silu(j):
                act.wait_ge(proj, n + 7 + j)
                act.wait_ge(yr_out, 16 * c)
                A(y_rg[:, j * OCH:(j + 1) * OCH], ps[:, LAST_GR_BANK[j], 0:OCH], ACT.Silu)\
                    .then_inc(gr_read, 1)

            for k in range(KT):
                act.wait_ge(centred, k + 1)
                if k >= 4:
                    act.wait_ge(sq_used, k - 3)
                A(sqs[:, k % 4, :], conv_out[:, k, :], ACT.Square).then_inc(squared, 1)
                if k == 1:
                    last_silu(0)
            act.wait_ge(sq_used, len(SQ_TILES))
            A(rstd_b[:, :].rearrange("p (j n) -> p j n", j=3), ps[:, 4:7, 0:C_CH], ACT.Ln,
              bias=eps_col[:, :]).then_inc(ln_rstd, 1)
            act.wait_ge(ln_rstd, 1)
            A(rstd_b[:, :], rstd_b[:, :], ACT.Exp, scale=-0.5).then_inc(ln_rstd, 1)
            act.preload_act_table(ACT.Silu)
            for k in range(KT + 1):
                if k < KT:
                    act.wait_ge(z_done, k + 1)
                    A(conv_out[:, k, :], conv_out[:, k, :], ACT.Silu, scale=par[:, k, P_LG:P_LG + 1],
                      bias=par[:, k, P_LB:P_LB + 1]).then_inc(ln_silu, 1)
                if k == 0:
                    last_silu(1)
                    last_silu(2)
                    act.wait_ge(proj, 3 * N_IN)
                if k >= 1:
                    act.wait_ge(ln_silu, k)
                    A(act_hi[:, k - 1, 0:SEQ], conv_out[:, k - 1, 0:SEQ], ACT.Copy).then_inc(v_hi, 1)
                    A(act_hi[:, k - 1, SEQ:TO], conv_out[:, k - 1, C_SAMPLE:C_LEN], ACT.Copy)\
                        .then_inc(v_hi, 1)
            act.wait_ge(w_loaded[1], 16 * (2 * KT + 1))
            w_hi_part(1, 1)
            act.wait_ge(h_done, 2 * c)
            act.wait_ge(b_done, c)
            gates_chunk(c, 1, 0, (4, 5))

            def pw_weights(p):
                for h in range(2):
                    act.wait_ge(pw, p * 2 + h + 1)
                    act.wait_ge(w_loaded[h], p * 16 + 16 * ((3 if h == 0 else 2) * KT + 2))
                    w_hi_part(h, h)
                    if isinstance(p, int):
                        gates_chunk(c, 1, 1 + h, (7, 3))
                if isinstance(p, int):
                    decay(c, 1, False)
                    root(c)

            pw_weights(0)
            with act.Fori(1, KT // 2) as p:
                pw_weights(p)
            act.wait_ge(st_turned, 1)
            for i in range(2):
                A(state_rows[0:NOUT, i * 512:(i + 1) * 512], ps[0:NOUT, 3 + 4 * i, :], ACT.Copy)\
                    .then_inc(st_rows, 1)
            act.wait_ge(pw, KT)
            for k in range(KT):
                act.wait_ge(yc, k + 1)
                A(act_hi[:, k, 0:TO], conv_out[:, k, 0:TO], ACT.Copy).then_inc(yh, 1)
            act.wait_ge(yr_in, 16)
            for k in range(KT):
                A(act_lo[:, k, 0:TO], yr[:, k, :], ACT.Copy).then_inc(yh, 1)

            def o_chunk(e, j, fst, tokens=0):
                c0, n = YCH[j]
                act.wait_ge(oproj, e * 3 + j + 1)
                act.wait_ge(par_ready, 1)
                A(o_t[:, bass.ds(e, 1), c0:c0 + n], ps[:, j, 0:n], ACT.Copy,
                  scale=par[:, bass.ds(e, 1), P_PG:P_PG + 1].rearrange("p a n -> p (a n)"))\
                    .then_inc(o_copied, 1)
                if not (fst and j == 0):
                    act.wait_ge(o_ssq, e * 3 + j)
                if tokens:
                    act.wait_ge(ss_root, tokens)
                A(ps[:, 3, 0:n], ps[:, j, 0:n], ACT.Square).then_inc(o_sq, 1)

            act.wait_ge(st_rows, 2)
            act.wait_ge(st_out, 16 * 6)

            n_loads = [3 * KT + 1 + KT // 2, 2 * KT + 1 + KT // 2]

            def o_tile(e, fst):
                act.wait_ge(half_done, e + 1)
                act.wait_ge(w_loaded[0], e * 16 + 16 * (n_loads[0] + 1))
                w_hi_part(0, 0)
                for j in range(3):
                    o_chunk(e, j, fst)
                act.wait_ge(w_loaded[1], e * 16 + 16 * (n_loads[1] + 1))
                w_hi_part(1, 1)

            o_tile(0, True)
            with act.Fori(1, KT - 1) as e:
                o_tile(e, False)
            e = KT - 1
            act.preload_act_table(ACT.Sqrt)
            for j in range(3):
                o_chunk(e, j, False, tokens=3 * j)
                act.wait_ge(ss_done, j + 1)
                for i, (c0, rows) in enumerate(out_tiles[j]):
                    A(rs_o[0:rows, 0, 3 * j + i:3 * j + i + 1], ps[0:rows, 3, i:i + 1], ACT.Sqrt,
                      bias=eps_col[0:rows, :]).then_inc(ss_root, 1)

        @block.vector
        def _(dve):
            STT, TT, TS = dve.scalar_tensor_tensor, dve.tensor_tensor, dve.tensor_scalar

            def w_lo_part(slot, stage, hi_count):
                dve.wait_ge(w_his, hi_count)
                TT(WLO[slot], wstage[:, stage], WHI[slot], ALU.subtract).then_inc(late_los, 1)

            def x_norm_part(t):
                rows = x_rows[t]
                dve.wait_ge(x_rt, t + 1)
                dve.reciprocal(sums[0:rows, t:t + 1], sums[0:rows, t:t + 1]).then_inc(x_rs, 1)
                dve.wait_ge(x_rs, t + 1)
                if t == 0:
                    dve.wait_ge(g_loaded, 16)
                if t >= 2:
                    dve.wait_ge(x_turned, t - 1)
                STT(out=x_norm[0:rows, t % 2, :], in0=x_in[0:rows, t % 4, :], scalar=sums[0:rows, t:t + 1],
                    in1=g_bcast[0:rows, :], op0=ALU.mult, op1=ALU.mult).then_inc(x_normed, 1)

            def x_lo_part(t):
                rows = x_rows[t]
                b = X_BANK[t % 3]
                dve.wait_ge(x_hi, t + 1)
                src = ps[:, b:b + 2, :].rearrange("p b (k t) -> p (b k) t", t=P)[:, :, 0:rows]
                TT(act_lo[:, :, t * P:t * P + rows], src, act_hi[:, :, t * P:t * P + rows],
                   ALU.subtract).then_inc(x_lo, 1)

            for t in range(NX + 2):
                if t < NX:
                    x_norm_part(t)
                if t >= 2:
                    x_lo_part(t - 2)

            step = [0]

            def chain(ins):
                step[0] += 1
                ins.then_inc(der, 1)
                dve.wait_ge(der, step[0])

            dve.wait_ge(par_ready, 1)
            lam = par[:, :, P_LAM]
            neg, z, s, s2 = (small[:, i, :] for i in range(4))
            poly = prm[:, :]
            chain(TS(neg, lam, -1.0, None, ALU.mult))
            TT(z, lam, neg, ALU.max).then_inc(der, 1)
            step[0] += 1
            dve.wait_ge(der_exp, 1)
            chain(TS(s, z, 2.0, None, ALU.add))
            chain(dve.reciprocal(s2, s))
            chain(TT(s, s2, z, ALU.mult))
            chain(TT(s2, s, s, ALU.mult))
            chain(TS(poly, s2, 1.0 / 17.0, None, ALU.mult))
            for d in (15, 13, 11, 9, 7, 5, 3):
                chain(STT(out=poly, in0=poly, scalar=1.0 / d, in1=s2, op0=ALU.add, op1=ALU.mult))
            chain(STT(out=poly, in0=poly, scalar=1.0, in1=s, op0=ALU.add, op1=ALU.mult))
            chain(TS(neg, neg, 0.0, None, ALU.max))
            chain(TS(neg, neg, 0.5, None, ALU.mult))
            chain(TT(poly, poly, neg, ALU.add))
            chain(TS(par[:, :, Q_SP], poly, 8.0, None, ALU.mult))
            TS(par[:, :, Q_NSP], poly, -8.0, None, ALU.mult).then_inc(der, 1)
            TS(par[:, :, Q_CW:Q_CW + CW], par[:, :, P_CW:P_CW + CW], 0.5, None, ALU.mult).then_inc(der, 1)
            TS(par[:, :, Q_BA:Q_BA + 2], par[:, :, P_BA:P_BA + 2], 0.5, None, ALU.mult).then_inc(der, 1)
            step[0] += 3
            dve.wait_ge(der, step[0])
            assert step[0] == DER_STEPS

            def tap(d, b, k):
                src, w = cv_in[:, b, META + k:META + k + C_LEN], par_cv[:, b, Q_CW + k:Q_CW + k + 1]
                if k > 0:
                    dve.wait_ge(taps, d * CPAD + k)
                if k == 0:
                    TS(acc[:, :], src, w, par_cv[:, b, P_CB:P_CB + 1], ALU.mult, ALU.add).then_inc(taps, 1)
                elif k < CPAD:
                    STT(out=acc[:, :], in0=src, scalar=w, in1=acc[:, :], op0=ALU.mult,
                        op1=ALU.add).then_inc(taps, 1)
                else:
                    STT(out=conv_out[:, bass.ds(d, 1), :].rearrange("p a n -> p (a n)"), in0=src, scalar=w,
                        in1=acc[:, :], op0=ALU.mult, op1=ALU.add).then_inc(conv_done, 1)

            def some_taps(d, b, first, end):
                for k in range(first, end):
                    tap(d, b, k)

            def conv_start(d, b, fst):
                if not fst:
                    dve.wait_ge(conv_done, d)
                dve.wait_ge(par_cv_set, d + 1)
                dve.wait_ge(cv_state_set, d + 1)
                dve.wait_ge(glu_done, 2 * d + 2)
                some_taps(d, b, 0, 2)
                for o, i in ((O_CP, META + SEQ), (O_CS, V_IN - CPAD)):
                    TS(states[:, bass.ds(d, 1), o:o + CPAD], cv_in[:, b:b + 1, i:i + CPAD],
                       0.5, None, ALU.mult).then_inc(cv_saved, 1)
                tap(d, b, 2)

            def gate_low(c):
                for i in range(2):
                    r = slice(64 * i, 64 * i + 64)
                    dve.wait_ge(gwh, 2 * c + i + 1)
                    TT(gate_l[r, :, 64 * i:64 * i + 64],
                       gate_w[r, :, bass.ds(c, 1), :].rearrange("p m a j -> p m (a j)"),
                       gate_h[r, :, 64 * i:64 * i + 64], ALU.subtract).then_inc(gwl, 1)

            def rtap(c, b, k):
                if k == 1:
                    dve.wait_ge(rtap0, c + 1)
                else:
                    dve.wait_ge(rtaps, 3 * c + k - 1)
                STT(out=rg_x[:, :], in0=rg_in[:, k:k + R_LEN], scalar=par_rg[:, b, P_RW + k:P_RW + k + 1],
                    in1=rg_x[:, :], op0=ALU.mult, op1=ALU.add).then_inc(rtaps, 1)

            def b_part(c):
                dve.wait_ge(root_done, c + 1)
                TT(rc[:, :], rc[:, :], rd[:, :], ALU.mult).then_inc(b_done, 1)

            def scan(c, b):
                dve.wait_ge(b_done, c + 1)
                dve.tensor_tensor_scan(rb[:, 0:META + SEQ], ra[:, 0:META + SEQ], rc[:, 0:META + SEQ], 0.0,
                                       ALU.mult, ALU.add).then_inc(h_done, 1)
                dve.tensor_tensor_scan(rb[:, R_SAMPLE:R_SAMPLE + DEC], ra[:, R_SAMPLE:R_SAMPLE + DEC],
                                       rc[:, R_SAMPLE:R_SAMPLE + DEC], par_rg[:, b, P_H0:P_H0 + 1],
                                       ALU.mult, ALU.add).then_inc(h_done, 1)

            def save_h(c):
                dve.wait_ge(h_done, 2 * c + 2)
                for o, i in ((O_HP, META + SEQ - 1), (O_HS, R_SAMPLE + DEC - 1)):
                    dve.tensor_copy(states[:, bass.ds(c, 1), o:o + 1],
                                    rb[:, i:i + 1].rearrange("p (a n) -> p a n", a=1)).then_inc(h_saved, 1)

            def save_rg(c):
                dve.wait_ge(x_read, 3 * c + 3)
                for o, i in ((O_RP, META + SEQ), (O_RS, R_SAMPLE_IN + DEC - RPAD)):
                    dve.tensor_copy(states[:, bass.ds(c, 1), o:o + RPAD],
                                    rg_in[:, i:i + RPAD].rearrange("p (a n) -> p a n", a=1)).then_inc(rg_saved, 1)

            def ix_part(c):
                dve.wait_ge(gates_read, 6 * c + 6)
                STT(out=rd[:, :], in0=rd[:, :], scalar=1.0, in1=rg_x[:, :], op0=ALU.add,
                    op1=ALU.mult).then_inc(ix_done, 1)

            def q_part(c):
                dve.wait_ge(a2_done, c + 1)
                dve.wait_ge(ix_done, c + 1)
                STT(out=rc[:, :], in0=rc[:, :], scalar=1.0, in1=rb[:, :], op0=ALU.add,
                    op1=ALU.mult).then_inc(q_done, 1)

            def tile(c, b, fst, at):
                d, o = c + 1, 1 - b
                conv_start(d, o, False)
                gate_low(c)
                tap(d, o, 3)
                for k in range(4, CW):
                    if not fst and k == at + 3:
                        b_part(c - 1)
                    if not fst and k == at + 4:
                        scan(c - 1, 1 - b)
                    if not fst and k == at + 5:
                        save_h(c - 1)
                    if not fst and at <= k < at + 3:
                        rtap(c, b, k - at + 1)
                    if k == at + 3:
                        save_rg(c)
                    if k == 26:
                        ix_part(c)
                    if k == 28:
                        q_part(c)
                    tap(d, o, k)

            conv_start(0, 0, True)
            some_taps(0, 0, 3, 26)
            for k in range(1, RW):
                rtap(0, 0, k)
                tap(0, 0, 25 + k)
            some_taps(0, 0, 29, CW)
            tile(0, 0, True, 4)
            tile(1, 1, False, 6)
            tile(2, 0, False, 7)
            with dve.Fori(1, KT // 2 - 1) as i:
                tile(i * 2 + 1, 1, False, 8)
                tile(i * 2 + 2, 0, False, 8)

            c = KT - 1
            dve.wait_ge(cv_saved, 2 * KT)
            dve.wait_ge(conv_done, KT)
            dve.wait_ge(csummed, KT - 2)
            TT(csum[:, :], csum[:, :], conv_out[:, c, :], ALU.add).then_inc(csummed, 1)
            gate_low(c)
            for k in range(1, RW):
                rtap(c, 1, k)
            save_rg(c)
            b_part(c - 1)
            scan(c - 1, 0)
            save_h(c - 1)
            dve.wait_ge(mean_done, 1)
            for k in range(KT):
                t = conv_out[:, k, :].rearrange("p (j n) -> p j n", j=3)
                TT(t, t, ps[:, 1:4, 0:C_CH], ALU.subtract).then_inc(centred, 1)
            for i, k in enumerate((4, 6)):
                dve.wait_ge(squared, k + 2)
                TT(sqs[:, k % 4, :], sqs[:, k % 4, :], sqs[:, k % 4 + 1, :], ALU.add).then_inc(sq_paired, 1)
            w_lo_part(0, 0, N_PW + 1)
            dve.wait_ge(ln_rstd, 2)

            def ln_lo(k):
                dve.wait_ge(v_hi, 2 * k + 2)
                TT(act_lo[:, k, 0:SEQ], conv_out[:, k, 0:SEQ], act_hi[:, k, 0:SEQ],
                   ALU.subtract).then_inc(v_lo[1], 1)
                TT(act_lo[:, k, SEQ:TO], conv_out[:, k, C_SAMPLE:C_LEN], act_hi[:, k, SEQ:TO],
                   ALU.subtract).then_inc(v_lo[1], 1)

            for k in range(KT + 3):
                if k < KT:
                    TT(conv_out[:, k, :], conv_out[:, k, :], rstd_b[:, :], ALU.mult).then_inc(z_done, 1)
                if k - 3 in LO_DVE:
                    ln_lo(k - 3)
            w_lo_part(1, 1, N_PW + 2)
            def pw_out(p):
                for h in range(2):
                    k = p * 2 + h
                    dve.wait_ge(pw, k + 1)
                    dve.wait_ge(silu_loaded[h], p * 16 + 16)
                    STT(out=conv_out[:, bass.ds(k, 1), 0:TO].rearrange("p a (j n) -> p (a j) n", j=3),
                        in0=ps[:, 4 * h:4 * h + 3, 0:OCH], scalar=par[:, bass.ds(k, 1), P_B2:P_B2 + 1].rearrange("p a n -> p (a n)"),
                        in1=silu_l[:, h].rearrange("p (j n) -> p j n", j=3), op0=ALU.add,
                        op1=ALU.mult).then_inc(yc, 1)
                    w_lo_part(h, h, p * 2 + N_PW + 3 + h)

            pw_out(0)
            ix_part(c)
            q_part(c)
            b_part(c)
            scan(c, 1)
            save_h(c)
            with dve.Fori(1, KT // 2) as p:
                pw_out(p)
            for k in range(KT):
                dve.wait_ge(yh, k + 1)
                TT(yc_lo[:, k, 0:TO], conv_out[:, k, 0:TO], act_hi[:, k, 0:TO], ALU.subtract).then_inc(yl, 1)
            for k in range(KT):
                dve.wait_ge(yh, KT + k + 1)
                TT(yr_lo[:, k, :], yr[:, k, :], act_lo[:, k, 0:TO], ALU.subtract).then_inc(yl, 1)

            def add_squares(e, j, fst):
                c0, n = YCH[j]
                dve.wait_ge(o_sq, e * 3 + j + 1)
                if fst:
                    dve.tensor_copy(ssq[:, c0:c0 + n], ps[:, 3, 0:n]).then_inc(o_ssq, 1)
                else:
                    dve.wait_ge(o_ssq, e * 3 + j - 2)
                    TT(ssq[:, c0:c0 + n], ssq[:, c0:c0 + n], ps[:, 3, 0:n], ALU.add).then_inc(o_ssq, 1)

            def o_tile(e, fst):
                w_lo_part(0, 0, e * 2 + N_OUT + 3)
                for j in range(3):
                    add_squares(e, j, fst)
                w_lo_part(1, 1, e * 2 + N_OUT + 4)

            o_tile(0, True)
            with dve.Fori(1, KT - 1) as e:
                o_tile(e, False)
            e = KT - 1

            def finish(j):
                for i, (c0, rows) in enumerate(out_tiles[j]):
                    n = 3 * j + i
                    dve.wait_ge(ss_root, n + 1)
                    dve.reciprocal(rs_o[0:rows, 1, n:n + 1], rs_o[0:rows, 0, n:n + 1]).then_inc(ss_rs, 1)
                    dve.wait_ge(ss_rs, n + 1)
                    dve.wait_ge(o_turned, n + 1)
                    dve.wait_ge(xr_loaded[n % 2], 16 * (n // 2 + 1))
                    if n >= 2:
                        dve.wait_ge(y_stored[n % 2], 16 * (n // 2))
                    b = 4 + 2 * (n % 2)
                    STT(out=y_out[0:rows, n % 2].rearrange("p (b n) -> p b n", b=2), in0=ps[0:rows, b:b + 2, :],
                        scalar=rs_o[0:rows, 1, n:n + 1],
                        in1=x_res[0:rows, n % 2].rearrange("p (b n) -> p b n", b=2), op0=ALU.mult,
                        op1=ALU.add).then_inc(y_ready, 1)

            for j in range(3):
                add_squares(e, j, False)
                if j > 0:
                    finish(j - 1)
            finish(2)


_INS = ["x_prompt", "x_sample", "state_rg_h", "state_rg_conv", "state_cv_conv", "meta_tokens", "pre_norm_g",
        "w_in", "rg_conv_w", "rg_conv_b", "rg_wa", "rg_ba", "rg_wx", "rg_bx", "rg_lambda", "cv_conv_w",
        "cv_conv_b", "cv_ln_g", "cv_ln_b", "cv_w_pw2", "cv_b_pw2", "w_out", "post_norm_g"]
_OUTS = [(1, SEQ, D), (1, DEC, D), (1, 1, D), (1, 1, RPAD, D), (1, 1, CPAD, D),
         (1, 1, D), (1, 1, RPAD, D), (1, 1, CPAD, D)]


def kernel(**inputs):
    import concourse.bacc as bacc
    from concourse.bass_utils import run_bass_kernel_spmd

    nc = bacc.Bacc("TRN2", target_bir_lowering=False, num_devices=1)
    arrays, args = {}, []
    for name in _INS:
        a = np.ascontiguousarray(inputs[name])
        arrays[f"in_{name}"] = a
        args.append(nc.dram_tensor(f"in_{name}", a.shape, mybir.dt.from_np(a.dtype), kind="ExternalInput").ap())
    for i, shape in enumerate(_OUTS):
        args.append(nc.dram_tensor(f"out_{i}", shape, F32, kind="ExternalOutput").ap())
    build(nc, *args)
    r = run_bass_kernel_spmd(nc, [arrays], core_ids=[0])
    return tuple(r.results[0][f"out_{i}"] for i in range(len(_OUTS)))
```

```python
from contextlib import ExitStack

import numpy as np

import concourse.bass as bass
from concourse import mybir
from concourse.alu_op_type import AluOpType as ALU

F32 = mybir.dt.float32
F32R = mybir.dt.float32r
ACT = mybir.ActivationFunctionType

P = 128
D = 1024
KT = D // P
META, SEQ, DEC = 16, 1024, 32
T = META + SEQ + DEC
TO = SEQ + DEC
EPS = 1e-6

XCH = [(0, 358), (358, 358), (716, 356)]
OCH = 352
assert sum(n for _, n in XCH) == T and 3 * OCH == TO

RW = 4
RPAD = RW - 1
R_SAMPLE_IN = RPAD + META + SEQ + RPAD
R_LEN = 1080
R_CH = R_LEN // 3
R_SAMPLE = R_SAMPLE_IN - RPAD
R_IN = R_LEN + RPAD
assert R_SAMPLE + DEC <= R_LEN

CW = 31
CPAD = CW - 1
V_SAMPLE_IN = CPAD + META + SEQ + CPAD
V_IN = V_SAMPLE_IN + DEC
C_LEN = SEQ + CPAD + DEC
C_SAMPLE = SEQ + CPAD
C_CH = C_LEN // 3
assert 3 * C_CH == C_LEN and META + C_LEN + CPAD == V_IN

P_CW, P_RW, P_RB, P_BA, P_BX, P_LAM, P_CB, P_LG, P_LB, P_B2, P_PG, P_H0, P_RS, P_CS = (
    0, 31, 35, 36, 37, 38, 39, 40, 41, 42, 43, 44, 45, 48)
PAR = P_CS + CPAD
Q_CW, Q_BA, Q_BX, Q_SP, Q_NSP = PAR, PAR + CW, PAR + CW + 1, PAR + CW + 2, PAR + CW + 3
PARQ = Q_NSP + 1

O_HP, O_HS, O_RP, O_RS, O_CP, O_CS = 0, 1, 2, 5, 8, 38
NOUT = O_CS + CPAD

SECTIONS = ["g", "v", "x", "gc", "gr"]
COLUMN = {"x": 0, "gr": 1, "v": 2, "g": 3, "gc": 4}
NS = len(SECTIONS)
WSLOT = {"g": 0, "v": 1, "x": 2, "gc": 0, "gr": 1}
BANK = {"g": 4, "v": 0, "x": 6, "gc": 4, "gr": 1}
GATE_R_BANK, GATE_I_BANK = 7, 0
X_BANK = [0, 2, 6]
LAST_GR_BANK = [7, 0, 3]

PW_BANK = [4, 0]

N_IN = NS * KT
N_PW = N_IN
N_OUT = N_IN + KT
LATE_PW, LATE_OUT = 0, KT
SQ_TILES = [0, 1, 2, 3, 4, 6]
SQ_SLOT = {0: 0, 1: 1, 2: 2, 3: 3, 4: 0, 6: 1, 7: 2}
HI_ACT, HI_DVE = [0, 1, 2, 4, 5, 7], [3, 6]
LO_POOL, LO_DVE = [1, 4, 6], [0, 2, 3, 5, 7]
DER_STEPS = 22
YCH = [(0, 384), (384, 384), (768, 288)]


def build(nc, x_prompt, x_sample, state_rg_h, state_rg_conv, state_cv_conv, meta_tokens, pre_norm_g,
          w_in, rg_conv_w, rg_conv_b, rg_wa, rg_ba, rg_wx, rg_bx, rg_lambda, cv_conv_w, cv_conv_b,
          cv_ln_g, cv_ln_b, cv_w_pw2, cv_b_pw2, w_out, post_norm_g,
          y_prompt, y_sample, rg_h_p, rg_c_p, cv_c_p, rg_h_s, rg_c_s, cv_c_s):
    top = [(nc.sbuf_base + 31) // 32 * 32]

    def take(nbytes):
        at = top[0]
        top[0] = at + (nbytes + 31) // 32 * 32
        assert top[0] <= nc.sbuf_usable_end, (top[0], nc.sbuf_usable_end)
        return at

    def at(name, shape, dt, offset):
        return nc.alloc_sbuf_tensor_at(name, [P] + shape, dt, offset=offset)

    def new(name, shape, dt=F32):
        return at(name, shape, dt, take(4 * int(np.prod(shape))))

    act_hi_at = top[0]
    act_hi = new("act_hi", [KT, T], F32R)
    act_lo = new("act_lo", [KT, T], F32R)
    conv_at = take(4 * KT * C_LEN)
    conv_out = at("conv_out", [KT, C_LEN], F32, conv_at)
    yc_lo = at("yc_lo", [KT, C_LEN], F32R, conv_at)
    wstage_at = take(2 * 4 * D)
    wstage = at("wstage", [2, KT, P], F32, wstage_at)
    w_hi = new("w_hi", [2, KT, P], F32R)
    w_lo = new("w_lo", [2, KT, P], F32R)
    w2_at = take(2 * 4 * D)
    w2_hi = at("w2_hi", [KT, P], F32R, w2_at)
    w2_lo = at("w2_lo", [KT, P], F32R, w2_at + 4 * D)
    par = new("par", [KT, PARQ])
    ident = new("ident", [P])
    mean_w = new("mean_w", [P])
    eps_col = new("eps_col", [1])
    WHI = [w_hi[:, 0], w_hi[:, 1], w2_hi[:, :, :]]
    WLO = [w_lo[:, 0], w_lo[:, 1], w2_lo[:, :, :]]
    arena = top[0]

    def phase(start):
        spot = [start]

        def put(name, shape, dt=F32):
            o = spot[0]
            spot[0] = (o + 4 * int(np.prod(shape)) + 31) // 32 * 32
            assert spot[0] <= nc.sbuf_usable_end, (name, spot[0], nc.sbuf_usable_end)
            return at(name, shape, dt, o)
        return put, spot

    put, spot = phase(conv_at)
    x_in = put("x_in", [4, D])
    x_norm = put("x_norm", [2, D])
    g_bcast = put("g_bcast", [D])
    sq_junk = put("sq_junk", [D])
    assert spot[0] <= conv_at + 4 * KT * C_LEN

    put, spot = phase(arena)
    ra = put("ra", [R_LEN])
    rb = put("rb", [R_LEN])
    rc = put("rc", [R_LEN])
    rd = put("rd", [R_LEN])
    rg_xl = at("rg_xl", [R_LEN], F32R, arena + 2 * 4 * R_LEN)
    rg_in = put("rg_in", [R_IN + 1])
    rg_x = put("rg_x", [R_LEN])
    rg_xh = put("rg_xh", [R_LEN], F32R)
    y_rg = put("y_rg", [TO])
    silu_gc = put("silu_gc", [TO])
    gate_w = put("gate_w", [2, KT, 64])
    gate_h = put("gate_h", [2, P], F32R)
    gate_l = put("gate_l", [2, P], F32R)
    par_cv = put("par_cv", [2, PARQ])
    par_rg = put("par_rg", [2, PARQ])
    states = put("states", [KT, NOUT])
    prm = put("prm", [KT])
    small = put("small", [4, KT])
    sums = put("sums", [16])
    cv_bufs = spot[0]
    tanh_g = put("tanh_g", [T])
    cv_in = put("cv_in", [2, V_IN])
    acc = put("acc", [C_LEN])
    csum = put("csum", [C_LEN])
    assert 4 * D <= 4 * R_LEN
    par_rows = at("par_rows", [D], F32, arena)

    put2, spot = phase(cv_bufs)
    sqs = put2("sqs", [4, C_LEN])
    sq5 = at("sq5", [C_LEN], F32, w2_at)
    rstd_at = spot[0]
    rstd_b = put2("rstd_b", [C_LEN])
    silu_l = at("silu_l", [2, TO], F32, cv_bufs)
    state_rows = at("state_rows", [D], F32, rstd_at)
    assert arena + 4 * KT * TO <= cv_bufs
    yr = at("yr", [KT, TO], F32, arena)
    yr_lo = at("yr_lo", [KT, TO], F32R, arena)

    put3, _ = phase(arena + 4 * KT * TO)
    o_tok = put3("o_tok", [9, D])
    rs_o = put3("rs_o", [2, 9])
    put4, spot = phase(w2_at)
    o_c = put4("o_c", [2, YCH[0][1]])
    ssq = put4("ssq", [TO])
    assert spot[0] <= w2_at + 2 * 4 * D
    y0_hi = at("y0_hi", [TO], F32R, w2_at)
    x_res0 = at("x_res0", [2, D], F32, wstage_at)
    x_res2 = at("x_res2", [7, D], F32, act_hi_at)

    ps = nc.alloc_psum_tensor("ps", [P, 8, 512], F32)
    silu_spill = nc.dram_tensor("silu_spill", [KT, P, TO], F32, kind="Internal").ap()
    yr_spill = nc.dram_tensor("yr_spill", [KT, P, TO], F32, kind="Internal").ap()

    ctx = ExitStack()
    with ctx:
        def sem(name):
            return ctx.enter_context(nc.semaphore(name))

        x_loaded = [sem(f"x_loaded{i}") for i in range(4)]
        g_loaded = sem("g_loaded")
        par_loaded = sem("par_loaded")
        gatew_loaded = sem("gatew_loaded")
        consts = sem("consts")
        x_ss = sem("x_ss")
        x_rt = sem("x_rt")
        x_rs = sem("x_rs")
        x_normed = sem("x_normed")
        x_turned = sem("x_turned")
        x_hi = sem("x_hi")
        x_lo = sem("x_lo")
        par_turned = sem("par_turned")
        par_ready = sem("par_ready")
        der = sem("der")
        der_exp = sem("der_exp")
        pads = sem("pads")
        w_loaded = [sem("w_loaded0"), sem("w_loaded1")]
        sp_steps = sem("sp_steps")
        w_his = sem("w_his")
        w_los = sem("w_los")
        late_los = sem("late_los")
        proj = sem("proj")
        g_read = sem("g_read")
        v_copied = sem("v_copied")
        one_added = sem("one_added")
        glu_done = sem("glu_done")
        x_read = sem("x_read")
        gc_read = sem("gc_read")
        gr_read = sem("gr_read")
        gates = sem("gates")
        gates_read = sem("gates_read")
        par_cv_set = sem("par_cv_set")
        par_rg_set = sem("par_rg_set")
        cv_state_set = sem("cv_state_set")
        pool_steps = sem("pool_steps")
        act_steps = sem("act_steps")
        taps = sem("taps")
        conv_done = sem("conv_done")
        rtap0 = sem("rtap0")
        rtaps = sem("rtaps")
        rgxh = sem("rgxh")
        rgxl = sem("rgxl")
        gwh = sem("gwh")
        gwl = sem("gwl")
        th_done = sem("th_done")
        a_done = sem("a_done")
        a2_done = sem("a2_done")
        ix_done = sem("ix_done")
        q_done = sem("q_done")
        root_done = sem("root_done")
        b_done = sem("b_done")
        h_done = sem("h_done")
        y_done = sem("y_done")
        cv_saved = sem("cv_saved")
        rg_saved = sem("rg_saved")
        h_saved = sem("h_saved")
        csummed = sem("csummed")
        st_read = sem("st_read")
        sgc_out = sem("sgc_out")
        yr_out = sem("yr_out")
        mean_done = sem("mean_done")
        centred = sem("centred")
        squared = sem("squared")
        sq_used = sem("sq_used")
        sq_paired = sem("sq_paired")
        ln_rstd = sem("ln_rstd")
        z_done = sem("z_done")
        ln_silu = sem("ln_silu")
        v_hi = sem("v_hi")
        v_hi_dve = sem("v_hi_dve")
        v_lo = [sem("v_lo0"), sem("v_lo1")]
        st_turned = sem("st_turned")
        st_rows = sem("st_rows")
        st_out = sem("st_out")
        silu_loaded = [sem("silu_loaded0"), sem("silu_loaded1")]
        pw = sem("pw")
        yc = sem("yc")
        yr_in = sem("yr_in")
        yh = sem("yh")
        y0_placed = sem("y0_placed")
        yl = sem("yl")
        oproj = sem("oproj")
        half_done = sem("half_done")
        o_copied = sem("o_copied")
        o_sq = sem("o_sq")
        o_ssq = sem("o_ssq")
        ss_done = sem("ss_done")
        o_turned = sem("o_turned")
        o_placed = sem("o_placed")
        ss_root = sem("ss_root")
        ss_rs = sem("ss_rs")
        o_scaled = sem("o_scaled")
        y_ready = [sem("y_ready_dve"), sem("y_ready_pool")]
        xr_loaded = [sem(f"xr_loaded{j}") for j in range(3)]
        y_stored = sem("y_stored")

        w_in_v = w_in.rearrange("d (k p) e -> p (d k) e", p=P)
        w_pw_v = cv_w_pw2.rearrange("d (k p) e -> p (d k) e", p=P)
        w_out_v = w_out.rearrange("d (h k p) e -> p (d h k) e", h=2, p=P)
        xp_v = x_prompt.rearrange("b t d -> (b t) d")
        xs_v = x_sample.rearrange("b t d -> (b t) d")

        first = P - META
        x_tiles = [[(0, meta_tokens, 0, META), (META, xp_v, 0, first)]]
        for t in range(1, 8):
            x_tiles.append([(0, xp_v, first + (t - 1) * P, P)])
        x_tiles.append([(0, xp_v, SEQ - META, META), (META, xs_v, 0, DEC)])
        x_rows = [P] * 8 + [META + DEC]
        NX = len(x_tiles)
        x_dmas = [len(t) for t in x_tiles]
        assert first + 7 * P == SEQ - META

        def x_landed(t):
            return 16 * sum(x_dmas[u] for u in range(t % 4, t + 1, 4))

        out_tiles = [[(0, P), (128, P), (256, P)], [(384, P), (512, P), (640, P)],
                     [(768, P), (896, P), (1024, DEC)]]

        par_src = [(P_CW, cv_conv_w[0]), (P_RW, rg_conv_w[0]), (P_RB, rg_conv_b), (P_BA, rg_ba),
                   (P_BX, rg_bx), (P_LAM, rg_lambda), (P_CB, cv_conv_b), (P_LG, cv_ln_g),
                   (P_LB, cv_ln_b), (P_B2, cv_b_pw2), (P_PG, post_norm_g), (P_H0, state_rg_h[0]),
                   (P_RS, state_rg_conv[0, 0]), (P_CS, state_cv_conv[0, 0])]

        def hi_done(engine, k):
            if k in HI_DVE:
                engine.wait_ge(v_hi_dve, 2 * HI_DVE.index(k) + 2)
            else:
                engine.wait_ge(v_hi, 2 * HI_ACT.index(k) + 2)

        block = ctx.enter_context(nc.Block())

        @block.sync
        def _(sp):
            def load_x(t):
                for row, src, r0, n in x_tiles[t]:
                    if t >= 4:
                        sp.wait_ge(x_normed, t - 3)
                    sp.dma_start(x_in[row:row + n, t % 4, :], src[r0:r0 + n, :]).then_inc(x_loaded[t % 4], 16)

            def load_w(slot, src):
                sp.dma_start(wstage[:, slot], src).then_inc(w_loaded[slot], 16)

            def w_in_cols(s, c):
                return w_in_v[:, :, bass.ds(c * P + COLUMN[s] * D, P)]

            def after_reg_wait():
                sp.sem_inc(sp_steps, 1)

            load_x(0)
            sp.dma_start(g_bcast[:, :], pre_norm_g.broadcast_to([P, D])).then_inc(g_loaded, 16)
            for t in range(1, 4):
                load_x(t)
            load_w(0, w_in_cols("g", 0))
            load_w(1, w_in_cols("v", 0))
            for t in range(4, NX):
                load_x(t)
            sp.wait_ge(w_los, 1)
            load_w(0, w_in_cols("x", 0))
            sp.wait_ge(w_los, 2)
            load_w(1, w_in_cols("v", 1))
            sp.wait_ge(w_los, 3)
            load_w(0, w_in_cols("g", 1))

            def loop_loads(c, fst, last):
                sp.wait_ge(w_los, c * NS + 4)
                after_reg_wait()
                load_w(0, w_in_cols("gr", c))
                sp.wait_ge(w_los, c * NS + 5)
                after_reg_wait()
                load_w(1, w_in_cols("gc", c))
                sp.wait_ge(w_los, c * NS + 6)
                after_reg_wait()
                load_w(1, w_in_cols("gr", KT - 1) if last else w_in_cols("v", c + 2))
                sp.wait_ge(w_los, c * NS + 7)
                after_reg_wait()
                load_w(0, w_in_cols("x", c + 1))
                sp.wait_ge(w_los, c * NS + 8)
                after_reg_wait()
                load_w(0, w_in_cols("gc", KT - 1) if last else w_in_cols("g", c + 2))
                sp.wait_ge(gc_read, c + 1)
                after_reg_wait()
                sp.dma_start(silu_spill[bass.ds(c, 1)], silu_gc[:, :]).then_inc(sgc_out, 16)
                if not fst:
                    sp.wait_ge(y_done, 2 * c)
                    after_reg_wait()
                    sp.dma_start(yr_spill[bass.ds(c - 1, 1)], y_rg[:, :]).then_inc(yr_out, 16)

            loop_loads(0, True, False)
            with sp.Fori(1, KT - 2) as c:
                loop_loads(c, False, False)
            loop_loads(KT - 2, False, True)
            sp.wait_ge(w_los, N_IN - 1)
            load_w(0, w_pw_v[:, :, 0:P])
            sp.wait_ge(w_los, N_IN)
            load_w(1, w_pw_v[:, :, P:2 * P])
            sp.wait_ge(y_done, 2 * (KT - 1))
            sp.dma_start(yr_spill[KT - 2], y_rg[:, :]).then_inc(yr_out, 16)
            sp.wait_ge(gc_read, KT)
            sp.dma_start(silu_spill[KT - 1], silu_gc[:, :]).then_inc(sgc_out, 16)

            sp.wait_ge(sgc_out, 16 * KT)
            sp.wait_ge(ln_rstd, 1)
            for h in range(2):
                sp.dma_start(silu_l[:, h], silu_spill[h]).then_inc(silu_loaded[h], 16)
            sp.wait_ge(late_los, LATE_PW + 1)
            load_w(0, w_pw_v[:, :, 2 * P:3 * P])
            sp.wait_ge(late_los, LATE_PW + 2)
            load_w(1, w_pw_v[:, :, 3 * P:4 * P])

            with sp.Fori(0, 2) as p:
                for h in range(2):
                    sp.wait_ge(yc, p * 2 + h + 1)
                    after_reg_wait()
                    sp.dma_start(silu_l[:, h], silu_spill[bass.ds(p * 2 + h + 2, 1)])\
                        .then_inc(silu_loaded[h], 16)
                    sp.wait_ge(late_los, p * 2 + LATE_PW + 3 + h)
                    after_reg_wait()
                    load_w(h, w_pw_v[:, :, bass.ds(p * (2 * P) + (h + 4) * P, P)])
            sp.wait_ge(y_done, 2 * KT)
            sp.dma_start(yr_spill[KT - 1], y_rg[:, :]).then_inc(yr_out, 16)
            sp.wait_ge(yr_out, 16 * KT)
            sp.wait_ge(h_saved, 2 * KT)
            sp.dma_start(yr[:, :, :], yr_spill.rearrange("k p t -> p k t")).then_inc(yr_in, 16)
            for h in range(2):
                sp.wait_ge(yc, 4 + h + 1)
                sp.dma_start(silu_l[:, h], silu_spill[6 + h]).then_inc(silu_loaded[h], 16)
                sp.wait_ge(late_los, LATE_PW + 7 + h)
                load_w(h, w_out_v[:, (1 - h) * KT:(2 - h) * KT, 0:P])
            with sp.Fori(1, KT) as e:
                for h in range(2):
                    sp.wait_ge(late_los, LATE_OUT + 2 * e - 1 + h)
                    after_reg_wait()
                    load_w(h, w_out_v[:, (1 - h) * KT:(2 - h) * KT, bass.ds(e * P, P)])
            flat = [t for j in out_tiles for t in j]
            sp.wait_ge(late_los, LATE_OUT + 2 * KT)
            for n in range(2):
                c0, rows = flat[n]
                sp.dma_start(x_res0[0:rows, n], xp_v[c0:c0 + rows, :]).then_inc(xr_loaded[0], 16)
            sp.wait_ge(half_done, KT)
            for n in range(2, 9):
                c0, rows = flat[n]
                src, r0 = (xp_v, c0) if c0 < SEQ else (xs_v, 0)
                sp.dma_start(x_res2[0:rows, n - 2], src[r0:r0 + rows, :]).then_inc(xr_loaded[n // 3], 16)
            for n, (c0, rows) in enumerate(flat):
                dst, r0 = (y_prompt[0], c0) if c0 < SEQ else (y_sample[0], 0)
                if n % 3 < 2:
                    sp.wait_ge(y_ready[0], n // 3 * 2 + n % 3 + 1)
                else:
                    sp.wait_ge(y_ready[1], n // 3 + 1)
                sp.dma_start(dst[r0:r0 + rows, :], o_tok[0:rows, n]).then_inc(y_stored, 16)
            sp.wait_ge(y_stored, 16 * len(flat))

        @block.gpsimd
        def _(pool):
            pool.memset(ident[:, :], 0.0).then_inc(consts, 1)
            pool.memset(mean_w[:, :], 1.0 / D).then_inc(consts, 1)
            pool.memset(eps_col[:, :], EPS).then_inc(consts, 1)
            pool.memset(gate_h[:, :, :].bitcast(F32), 0.0).then_inc(consts, 1)
            pool.memset(gate_l[:, :, :].bitcast(F32), 0.0).then_inc(consts, 1)
            pool.wait_ge(consts, 5)
            pool.affine_select(out=ident[:, :], in_=ident[:, :], compare_op=ALU.not_equal, fill=1.0,
                               base=0, pattern=[[-1, P]], channel_multiplier=1).then_inc(consts, 1)
            TT = pool.tensor_tensor

            def take_wait():
                pool.sem_inc(pool_steps, 1)

            def w_lo_part(slot, stage, n):
                pool.wait_ge(w_his, n)
                TT(WLO[slot], wstage[:, stage], WHI[slot], ALU.subtract).then_inc(w_los, 1)

            def add_one(d):
                pool.wait_ge(g_read, 2 * d + 2)
                take_wait()
                pool.tensor_scalar(tanh_g[:, :], tanh_g[:, :], 1.0, None, ALU.add).then_inc(one_added, 1)

            def conv_input(d, b):
                pool.wait_ge(v_copied, 3 * d + 3)
                pool.wait_ge(one_added, d + 1)
                for lo, hi, src in ((CPAD, CPAD + META + SEQ, tanh_g[:, 0:META + SEQ]),
                                    (V_SAMPLE_IN, V_IN, tanh_g[:, META + SEQ:T])):
                    TT(cv_in[:, b, lo:hi], src, cv_in[:, b, lo:hi], ALU.mult).then_inc(glu_done, 1)

            def rg_low(c):
                pool.wait_ge(rgxh, c + 1)
                if not (isinstance(c, int) and c == 0):
                    pool.wait_ge(h_done, 2 * c)
                TT(rg_xl[:, :], rg_x[:, :], rg_xh[:, :], ALU.subtract).then_inc(rgxl, 1)

            def y_part(c, gr_reads):
                pool.wait_ge(h_done, 2 * c + 2)
                pool.wait_ge(gr_read, gr_reads)
                TT(y_rg[:, 0:SEQ], rb[:, META:META + SEQ], y_rg[:, 0:SEQ], ALU.mult).then_inc(y_done, 1)
                TT(y_rg[:, SEQ:TO], rb[:, R_SAMPLE:R_SAMPLE + DEC], y_rg[:, SEQ:TO], ALU.mult)\
                    .then_inc(y_done, 1)

            def tile(c, b, fst=False, second=False):
                add_one(c + 1)
                w_lo_part(0, 1, c * NS + 6)
                conv_input(c + 1, 1 - b)
                w_lo_part(1, 0, c * NS + 7)
                w_lo_part(2, 0, c * NS + 8)
                rg_low(c)
                if not fst:
                    y_part(c - 1, c)
                w_lo_part(0, 0, c * NS + 9)
                w_lo_part(1, 1, c * NS + 10)
                if not fst:
                    pool.wait_ge(conv_done, c + 1)
                    if second:
                        TT(csum[:, :], conv_out[:, 0, :], conv_out[:, 1, :], ALU.add).then_inc(csummed, 1)
                    else:
                        pool.wait_ge(csummed, c - 1)
                        take_wait()
                        total = csum[:, :].rearrange("p (a n) -> p a n", a=1)
                        TT(total, total, conv_out[:, bass.ds(c, 1), :], ALU.add).then_inc(csummed, 1)

            def load_par(rows):
                for row, src in rows:
                    pool.dma_start(par_rows[row:row + src.shape[0], :], src).then_inc(par_loaded, 16)

            load_par(par_src[:7])
            w_lo_part(0, 0, 1)
            load_par(par_src[7:])
            for m, w in enumerate((rg_wa, rg_wx)):
                for b in range(2):
                    pool.dma_start(gate_w[64 * b:64 * b + 64, m],
                                   w[0].rearrange("(c b) i j -> b i c j", b=2)[b]).then_inc(gatew_loaded, 16)
            w_lo_part(1, 1, 2)
            w_lo_part(2, 0, 3)
            pool.wait_ge(par_turned, 1)
            pool.memset(rg_in[:, 0:RPAD], 0.0).then_inc(pads, 1)
            pool.memset(rg_in[:, R_SAMPLE_IN + DEC:R_IN + 1], 0.0).then_inc(pads, 1)
            pool.memset(cv_in[:, :, 0:CPAD], 0.0).then_inc(pads, 1)
            pool.wait_ge(pads, 3)
            add_one(0)
            w_lo_part(0, 0, 4)
            conv_input(0, 0)
            w_lo_part(1, 1, 5)
            tile(0, 0, fst=True)
            tile(1, 1, second=True)
            tile(2, 0)
            with pool.Fori(1, KT // 2 - 1) as i:
                tile(i * 2 + 1, 1)
                tile(i * 2 + 2, 0)
            rg_low(KT - 1)
            y_part(KT - 2, KT - 1)
            pool.wait_ge(proj, 3 * N_IN)
            for k in LO_POOL:
                hi_done(pool, k)
                TT(act_lo[:, k, 0:SEQ], conv_out[:, k, 0:SEQ], act_hi[:, k, 0:SEQ],
                   ALU.subtract).then_inc(v_lo[0], 1)
                TT(act_lo[:, k, SEQ:TO], conv_out[:, k, C_SAMPLE:C_LEN], act_hi[:, k, SEQ:TO],
                   ALU.subtract).then_inc(v_lo[0], 1)
            y_part(KT - 1, KT - 1 + 3)
            pool.wait_ge(st_rows, 2)
            for dst, row, n in ((rg_h_p[0], O_HP, 1), (rg_h_s[0], O_HS, 1), (rg_c_p[0, 0], O_RP, RPAD),
                                (rg_c_s[0, 0], O_RS, RPAD), (cv_c_p[0, 0], O_CP, CPAD),
                                (cv_c_s[0, 0], O_CS, CPAD)):
                pool.dma_start(dst, state_rows[row:row + n, :]).then_inc(st_out, 16)
            pool.wait_ge(st_out, 16 * 6)
            for j in range(3):
                n, rows = 3 * j + 2, out_tiles[j][2][1]
                pool.wait_ge(xr_loaded[j], 16 * 3)
                pool.wait_ge(o_scaled, j + 1)
                TT(o_tok[0:rows, n], o_tok[0:rows, n], x_res2[0:rows, n - 2], ALU.add).then_inc(y_ready[1], 1)

        @block.tensor
        def _(pe):
            def product(out, wh, wl, xh, xl, start, stop):
                pe.matmul(out, wh, xh, start=start, stop=False)
                pe.matmul(out, wh, xl, start=False, stop=False)
                return pe.matmul(out, wl, xh, start=False, stop=stop)

            def chunk(s, j, bank=None, between={}):
                bank = (BANK[s] + j) % 8 if bank is None else bank
                c0, n = (META + j * OCH, OCH) if s in ("gr", "gc") else XCH[j]
                w = WSLOT[s]
                for k in range(KT):
                    mm = product(ps[:, bank, 0:n], WHI[w][:, k], WLO[w][:, k],
                                 act_hi[:, k, c0:c0 + n], act_lo[:, k, c0:c0 + n], k == 0, k == KT - 1)
                    if k in between:
                        turn_x(between[k])
                mm.then_inc(proj, 1)

            def turn_x(t):
                rows = x_rows[t]
                pe.wait_ge(x_normed, t + 1)
                if t >= 3:
                    pe.wait_ge(x_lo, t - 2)
                for k in range(KT):
                    mm = pe.transpose(ps[:, X_BANK[t % 3] + k // 4, k % 4 * P:k % 4 * P + rows],
                                      x_norm[0:rows, t % 2, k * P:(k + 1) * P], ident[0:rows, 0:rows])
                mm.then_inc(x_turned, 1)

            def gate_chunk(j, banks=(GATE_R_BANK, GATE_I_BANK)):
                for m, bank in enumerate(banks):
                    mm = product(ps[:, bank, 0:R_CH], gate_h[:, m], gate_l[:, m],
                                 rg_xh[:, j * R_CH:(j + 1) * R_CH], rg_xl[:, j * R_CH:(j + 1) * R_CH],
                                 True, True)
                    mm.then_inc(gates, 1)

            def tile(c, fst):
                d = c + 1
                pe.wait_ge(w_los, c * NS + 4)
                if fst:
                    pe.wait_ge(g_read, 2)
                else:
                    pe.wait_ge(gc_read, c)
                for j in range(3):
                    if j == 1 and not fst:
                        pe.wait_ge(gates_read, 6 * c)
                    chunk("g", j)
                pe.wait_ge(w_los, c * NS + 5)
                if fst:
                    pe.wait_ge(v_copied, 3)
                else:
                    pe.wait_ge(gr_read, c)
                for j in range(3):
                    chunk("v", j)
                pe.wait_ge(g_read, 2 * d + 2)
                for j in range(3):
                    if j == 2:
                        pe.wait_ge(v_copied, 3 * d + 3)
                    chunk("x", j)
                pe.wait_ge(w_los, c * NS + 6)
                for j in range(3):
                    if j == 2:
                        pe.wait_ge(x_read, 3 * c + 1)
                    chunk("gc", j)
                pe.wait_ge(w_los, c * NS + 7)
                chunk("gr", 0)
                chunk("gr", 1)
                pe.wait_ge(x_read, 3 * c + 3)
                pe.wait_ge(rgxl, c + 1)
                pe.wait_ge(gwl, 2 * c + 2)
                gate_chunk(0)
                chunk("gr", 2)
                pe.wait_ge(gates_read, 6 * c + 2)
                gate_chunk(1)
                pe.wait_ge(gc_read, c + 1)
                gate_chunk(2, (5, 6))

            pe.wait_ge(consts, 6)
            for t in range(5):
                turn_x(t)
            pe.wait_ge(w_los, 1)
            for j, between in enumerate(({1: 5, 3: 6, 6: 7}, {2: 8}, {})):
                pe.wait_ge(x_lo, 3 * j + 3)
                chunk("g", j, between=between)
            pe.wait_ge(par_loaded, 16 * len(par_src))
            for k in range(KT):
                mm = pe.transpose(ps[:, 3 + 4 * (k // 4), k % 4 * P:k % 4 * P + PAR],
                                  par_rows[0:PAR, k * P:(k + 1) * P], ident[0:PAR, 0:PAR])
            mm.then_inc(par_turned, 1)
            pe.wait_ge(w_los, 2)
            for j in range(3):
                chunk("v", j)
            pe.wait_ge(par_ready, 1)
            tile(0, True)
            with pe.Fori(1, KT - 1) as c:
                tile(c, False)

            c = KT - 1
            pe.wait_ge(w_los, c * NS + 3)
            pe.wait_ge(gates_read, 6 * c - 2)
            for j in (1, 2, 0):
                if j == 0:
                    pe.wait_ge(gates_read, 6 * c)
                chunk("x", j)
            pe.wait_ge(w_los, N_IN - 1)
            pe.wait_ge(x_read, 3 * c + 1)
            for j in range(3):
                chunk("gc", j)
            pe.wait_ge(gr_read, c)
            pe.wait_ge(csummed, KT - 1)
            for j in range(3):
                mm = pe.matmul(ps[:, 1 + j, 0:C_CH], mean_w[:, :], csum[:, j * C_CH:(j + 1) * C_CH],
                               start=True, stop=True)
            mm.then_inc(mean_done, 1)
            pe.wait_ge(w_los, N_IN)
            pe.wait_ge(x_read, 3 * c + 3)
            chunk("gr", 0, LAST_GR_BANK[0])
            pe.wait_ge(gc_read, KT)
            for k in SQ_TILES:
                if k < 4:
                    pe.wait_ge(squared, k + 1)
                else:
                    pe.wait_ge(sq_paired, k // 2 - 1)
                for j in range(3):
                    mm = pe.matmul(ps[:, 4 + j, 0:C_CH], mean_w[:, :], sqs[:, SQ_SLOT[k], j * C_CH:(j + 1) * C_CH],
                                   start=(k == 0), stop=(k == SQ_TILES[-1]))
                mm.then_inc(sq_used, 1)
            chunk("gr", 1, LAST_GR_BANK[1])
            pe.wait_ge(centred, KT)
            chunk("gr", 2, LAST_GR_BANK[2])
            pe.wait_ge(ln_rstd, 1)
            pe.wait_ge(rgxl, c + 1)
            pe.wait_ge(gwl, 2 * c + 2)
            gate_chunk(0, (1, 2))

            def pw_pair(p, fst):
                for h in range(2):
                    pe.wait_ge(late_los, p * 2 + LATE_PW + h + 1)
                    if fst:
                        if h == 1:
                            pe.wait_ge(gr_read, KT - 1 + 2)
                            pe.wait_ge(gates_read, 6 * KT - 4)
                    else:
                        pe.wait_ge(yc, p * 2 + h - 1)
                    for k in range(KT):
                        if fst:
                            if k in LO_POOL:
                                pe.wait_ge(v_lo[0], 2 * LO_POOL.index(k) + 2)
                            else:
                                pe.wait_ge(v_lo[1], 2 * LO_DVE.index(k) + 2)
                        for j in range(3):
                            mm = product(ps[:, PW_BANK[h] + j, 0:OCH], WHI[h][:, k], WLO[h][:, k],
                                         act_hi[:, k, j * OCH:(j + 1) * OCH],
                                         act_lo[:, k, j * OCH:(j + 1) * OCH], k == 0, k == KT - 1)
                    mm.then_inc(pw, 1)
                    if fst:
                        pe.wait_ge(gr_read, KT - 1 + 3)
                        pe.wait_ge(gates_read, 6 * KT - 4 + 2 * h)
                        gate_chunk(1 + h, (7, 3))

            pw_pair(0, True)
            with pe.Fori(1, KT // 2) as p:
                pw_pair(p, False)
            pe.wait_ge(gates_read, 6 * KT)
            pe.wait_ge(cv_saved, 2 * KT)
            pe.wait_ge(rg_saved, 2 * KT)
            pe.wait_ge(h_saved, 2 * KT)
            for k in range(KT):
                mm = pe.transpose(ps[0:NOUT, 3 + 4 * (k // 4), k % 4 * P:(k % 4 + 1) * P],
                                  states[:, k, :], ident[:, :])
            mm.then_inc(st_turned, 1)

            halves = [(act_hi, yc_lo), (act_lo, yr_lo)]

            def o_steps(h, k, j, start, stop, aside=False):
                hi, lo = halves[h]
                c0, n = YCH[j]
                return product(ps[:, j, 0:n], WHI[h][:, k], WLO[h][:, k],
                               y0_hi[:, c0:c0 + n] if aside else hi[:, k, c0:c0 + n],
                               lo[:, k, c0:c0 + n], start, stop)

            def turn_out(e, j, fst):
                pe.wait_ge(o_copied, e * 3 + j + 1)
                if not fst:
                    pe.wait_ge(o_placed, e * 3 + j - 2)
                for i, (c0, rows) in enumerate(out_tiles[j]):
                    mm = pe.transpose(ps[0:rows, 4 + j, i * P:(i + 1) * P],
                                      o_c[:, j % 2, i * P:i * P + rows], ident[:, :])
                mm.then_inc(o_turned, 1)

            def token_sums(j):
                pe.wait_ge(o_ssq, 3 * (KT - 1) + j + 1)
                if j > 0:
                    pe.wait_ge(ss_root, 3 * j)
                for i, (c0, rows) in enumerate(out_tiles[j]):
                    mm = pe.matmul(ps[0:rows, 7, i:i + 1], ssq[:, c0:c0 + rows], mean_w[:, 0:1],
                                   start=(i == 0), stop=True, skip_group_check=True)
                mm.then_inc(ss_done, 1)

            def o_tile(e, first, last):
                for h in range(2):
                    pe.wait_ge(late_los, e * 2 + LATE_OUT + 1 + h)
                    for j in range(3):
                        if h == 0:
                            pe.wait_ge(o_sq, e * 3 - 2 + j)
                        for k in range(KT):
                            mm = o_steps(h, k, j, h == 0 and k == 0, h == 1 and k == KT - 1)
                            if h == 1 and j > 0 and k == 2:
                                turn_out(e, j - 1, False)
                            if h == 1 and j > 0 and k == 3 and last:
                                token_sums(j - 1)
                        if h == 0 and j == 2:
                            mm.then_inc(half_done, 1)
                        if h == 0 and j == 0:
                            turn_out(e - 1, 2, first)
                        if h == 1:
                            mm.then_inc(oproj, 1)

            pe.wait_ge(yc, KT)
            for h in range(2):
                pe.wait_ge(late_los, LATE_OUT + 1 + h)
                for k in range(KT):
                    pe.wait_ge(yl, h * KT + k + 1)
                    for j in range(3):
                        mm = o_steps(h, k, j, h == 0 and k == 0, h == 1 and k == KT - 1,
                                     aside=(h == 0 and k == 0))
                        if h == 1 and k == KT - 1:
                            mm.then_inc(oproj, 1)
                if h == 0:
                    mm.then_inc(half_done, 1)
            pe.wait_ge(st_rows, 2)
            for j in range(2):
                turn_out(0, j, True)
            pe.wait_ge(y0_placed, 1)
            o_tile(1, True, False)
            with pe.Fori(2, KT - 1) as e:
                o_tile(e, False, False)
            o_tile(KT - 1, False, True)
            turn_out(KT - 1, 2, False)
            token_sums(2)

        @block.scalar
        def _(act):
            A = act.activation

            def take_wait():
                act.sem_inc(act_steps, 1)

            def w_hi_part(slot, stage):
                A(WHI[slot], wstage[:, stage], ACT.Copy).then_inc(w_his, 1)

            act.preload_act_table(ACT.Sqrt)
            act.wait_ge(consts, 6)

            def x_stats(t):
                rows = x_rows[t]
                act.wait_ge(x_loaded[t % 4], x_landed(t))
                if t >= 1:
                    act.wait_ge(x_ss, t)
                A(sq_junk[0:rows, :], x_in[0:rows, t % 4, :], ACT.Square,
                  accum_out=sums[0:rows, t:t + 1]).then_inc(x_ss, 1)
                act.wait_ge(x_ss, t + 1)
                A(sums[0:rows, t:t + 1], sums[0:rows, t:t + 1], ACT.Sqrt, scale=1.0 / D,
                  bias=eps_col[0:rows, :]).then_inc(x_rt, 1)

            def x_hi_part(t):
                rows = x_rows[t]
                b = X_BANK[t % 3]
                act.wait_ge(x_turned, t + 1)
                A(act_hi[:, :, t * P:t * P + rows].rearrange("p (b k) t -> p b k t", b=2),
                  ps[:, b:b + 2, :].rearrange("p b (k t) -> p b k t", t=P)[:, :, :, 0:rows],
                  ACT.Copy).then_inc(x_hi, 1)

            for t in range(NX + 2):
                if t < NX:
                    x_stats(t)
                if t >= 2:
                    x_hi_part(t - 2)
                if t == 2:
                    act.wait_ge(w_loaded[0], 16)
                    w_hi_part(0, 0)
            act.wait_ge(w_loaded[1], 16)
            w_hi_part(1, 1)
            act.wait_ge(w_loaded[0], 32)
            w_hi_part(2, 0)
            act.wait_ge(par_turned, 1)
            A(par[:, :, 0:PAR].rearrange("p (b k) n -> p b k n", b=2),
              ps[:, 3:8:4, :].rearrange("p b (k n) -> p b k n", n=P)[:, :, :, 0:PAR],
              ACT.Copy).then_inc(par_ready, 1)
            act.wait_ge(der, 2)
            A(small[:, 1, :], small[:, 1, :], ACT.Exp, scale=-1.0).then_inc(der_exp, 1)

            def gate_tanh(d):
                n = 0 if isinstance(d, int) and d == 0 else d * (3 * NS) - 9
                act.wait_ge(proj, n + 2)
                if not (isinstance(d, int) and d == 0):
                    act.wait_ge(glu_done, 2 * d)
                A(tanh_g[:, 0:716].rearrange("p (j n) -> p j n", j=2), ps[:, 4:6, 0:358], ACT.Tanh,
                  scale=0.5).then_inc(g_read, 1)
                act.wait_ge(proj, n + 3)
                A(tanh_g[:, 716:T], ps[:, 6, 0:356], ACT.Tanh, scale=0.5).then_inc(g_read, 1)

            def cv_setup(d, b, reuse):
                if reuse:
                    act.wait_ge(conv_done, d - 1)
                    act.wait_ge(cv_saved, 2 * d - 2)
                    take_wait()
                A(par_cv[:, b:b + 1, :], par[:, bass.ds(d, 1), :], ACT.Copy).then_inc(par_cv_set, 1)
                A(cv_in[:, b:b + 1, CPAD + META + SEQ:V_SAMPLE_IN],
                  par[:, bass.ds(d, 1), P_CS:P_CS + CPAD], ACT.Copy, scale=2.0).then_inc(cv_state_set, 1)

            def copy_v(d, b):
                act.wait_ge(proj, 6 if isinstance(d, int) and d == 0 else d * (3 * NS) - 3)
                A(cv_in[:, b, CPAD:CPAD + 716].rearrange("p (j n) -> p j n", j=2), ps[:, 0:2, 0:358],
                  ACT.Copy).then_inc(v_copied, 1)
                A(cv_in[:, b, CPAD + 716:CPAD + META + SEQ], ps[:, 2, 0:324], ACT.Copy).then_inc(v_copied, 1)
                A(cv_in[:, b, V_SAMPLE_IN:V_IN], ps[:, 2, 324:356], ACT.Copy).then_inc(v_copied, 1)

            def rg_setup(c, b, fst, reuse):
                if reuse:
                    act.wait_ge(h_done, 2 * c - 2)
                    take_wait()
                A(par_rg[:, b:b + 1, :], par[:, bass.ds(c, 1), :], ACT.Copy).then_inc(par_rg_set, 1)
                act.wait_ge(par_rg_set, c + 1)
                if not fst:
                    act.wait_ge(gates, 6 * c)
                for i in range(2):
                    r = slice(64 * i, 64 * i + 64)
                    act.wait_ge(gatew_loaded, 64)
                    A(gate_h[r, :, 64 * i:64 * i + 64], gate_w[r, :, bass.ds(c, 1), :], ACT.Copy)\
                        .then_inc(gwh, 1)
                if not fst:
                    act.wait_ge(rg_saved, 2 * c)
                    act.wait_ge(rtaps, 3 * c)
                A(rg_in[:, RPAD + META + SEQ:R_SAMPLE_IN], par_rg[:, b, P_RS:P_RS + RPAD], ACT.Copy)\
                    .then_inc(st_read, 1)

            def root(c):
                act.wait_ge(q_done, c + 1)
                A(rc[:, :], rc[:, :], ACT.Sqrt, scale=0.25).then_inc(root_done, 1)

            def rg_input(c, b, n, fst):
                act.wait_ge(proj, n + (3 if isinstance(c, int) and c == KT - 1 else 2))
                A(rg_in[:, RPAD:RPAD + 716].rearrange("p (j n) -> p j n", j=2), ps[:, 6:8, 0:358],
                  ACT.Copy).then_inc(x_read, 1)
                act.wait_ge(proj, n + 3)
                A(rg_in[:, RPAD + 716:RPAD + META + SEQ], ps[:, 0, 0:324], ACT.Copy).then_inc(x_read, 1)
                A(rg_in[:, R_SAMPLE_IN:R_SAMPLE_IN + DEC], ps[:, 0, 324:356], ACT.Copy).then_inc(x_read, 1)
                act.wait_ge(st_read, c + 1)
                act.wait_ge(x_read, 3 * c + 3)
                if not fst:
                    act.wait_ge(ix_done, c)
                A(rg_x[:, :], rg_in[:, 0:R_LEN], ACT.Identity, scale=par_rg[:, b, P_RW:P_RW + 1],
                  bias=par_rg[:, b, P_RB:P_RB + 1]).then_inc(rtap0, 1)

            def rg_high(c):
                act.wait_ge(rtaps, 3 * c + 3)
                A(rg_xh[:, :], rg_x[:, :], ACT.Copy).then_inc(rgxh, 1)

            def silu_of_gc(c, n, fst):
                act.wait_ge(proj, n + 3)
                if not fst:
                    act.wait_ge(sgc_out, 16 * c)
                A(silu_gc[:, :].rearrange("p (j n) -> p j n", j=3), ps[:, 4:7, 0:OCH], ACT.Silu)\
                    .then_inc(gc_read, 1)

            def gates_chunk(c, b, j, banks=(GATE_R_BANK, GATE_I_BANK)):
                cols = slice(j * R_CH, (j + 1) * R_CH)
                for m, (bank, dst, bias) in enumerate(zip(banks, (ra, rd), (Q_BA, Q_BX))):
                    act.wait_ge(gates, 6 * c + 2 * j + m + 1)
                    A(dst[:, cols], ps[:, bank, 0:R_CH], ACT.Tanh, scale=0.5,
                      bias=par_rg[:, b, bias:bias + 1]).then_inc(gates_read, 1)

            def decay(c, b, fst):
                act.wait_ge(gates_read, 6 * c + 6)
                if not fst:
                    act.wait_ge(h_saved, 2 * c)
                    act.wait_ge(y_done, 2 * c)
                A(rb[:, :], ra[:, :], ACT.Tanh, scale=par_rg[:, b, Q_SP:Q_SP + 1],
                  bias=par_rg[:, b, Q_SP:Q_SP + 1]).then_inc(th_done, 1)
                act.wait_ge(th_done, c + 1)
                A(ra[:, :], ra[:, :], ACT.Exp, scale=par_rg[:, b, Q_NSP:Q_NSP + 1],
                  bias=par_rg[:, b, Q_NSP:Q_NSP + 1]).then_inc(a_done, 1)
                act.wait_ge(a_done, c + 1)
                A(rc[:, :], ra[:, :], ACT.Square).then_inc(a2_done, 1)

            def tile(c, b, fst):
                n = c * (3 * NS) + 6
                act.preload_act_table(ACT.Silu)
                gate_tanh(c + 1)
                act.wait_ge(w_loaded[1], c * 32 + 48)
                w_hi_part(0, 1)
                cv_setup(c + 1, 1 - b, not fst)
                rg_setup(c, b, fst, not fst)
                copy_v(c + 1, 1 - b)
                act.wait_ge(w_loaded[0], c * 48 + 64)
                w_hi_part(1, 0)
                rg_input(c, b, n + 6, fst)
                if not fst:
                    root(c - 1)
                act.wait_ge(w_loaded[0], c * 48 + 80)
                w_hi_part(2, 0)
                rg_high(c)
                silu_of_gc(c, n + 9, fst)
                act.wait_ge(w_loaded[0], c * 48 + 96)
                w_hi_part(0, 0)
                if not fst:
                    act.wait_ge(h_done, 2 * c)
                    act.wait_ge(b_done, c)
                gates_chunk(c, b, 0)
                act.wait_ge(proj, n + 15)
                if not fst:
                    act.wait_ge(yr_out, 16 * c)
                act.wait_ge(w_loaded[1], c * 32 + 64)
                w_hi_part(1, 1)
                gates_chunk(c, b, 1)
                gates_chunk(c, b, 2, (5, 6))
                A(y_rg[:, :].rearrange("p (j n) -> p j n", j=3), ps[:, 1:4, 0:OCH], ACT.Silu)\
                    .then_inc(gr_read, 1)
                decay(c, b, fst)

            gate_tanh(0)
            act.wait_ge(w_loaded[0], 48)
            w_hi_part(0, 0)
            act.wait_ge(pads, 3)
            act.wait_ge(der, DER_STEPS)
            cv_setup(0, 0, False)
            copy_v(0, 0)
            act.wait_ge(w_loaded[1], 32)
            w_hi_part(1, 1)
            tile(0, 0, True)
            with act.Fori(0, KT // 2 - 1) as i:
                tile(i * 2 + 1, 1, False)
                tile(i * 2 + 2, 0, False)

            c = KT - 1
            n = c * (3 * NS) + 6
            rg_setup(c, 1, False, True)
            rg_input(c, 1, n, False)
            root(c - 1)
            act.preload_act_table(ACT.Silu)
            silu_of_gc(c, n + 3, False)
            act.wait_ge(w_loaded[0], 16 * (3 * KT + 1))
            w_hi_part(0, 0)

            def last_silu(j):
                act.wait_ge(proj, n + 7 + j)
                act.wait_ge(yr_out, 16 * c)
                A(y_rg[:, j * OCH:(j + 1) * OCH], ps[:, LAST_GR_BANK[j], 0:OCH], ACT.Silu)\
                    .then_inc(gr_read, 1)

            for k in range(KT):
                act.wait_ge(centred, k + 1)
                if k == 5:
                    A(sq5[:, :], conv_out[:, k, :], ACT.Square).then_inc(squared, 1)
                    continue
                if k >= 4:
                    act.wait_ge(sq_used, SQ_SLOT[k] + 1)
                A(sqs[:, SQ_SLOT[k], :], conv_out[:, k, :], ACT.Square).then_inc(squared, 1)
            act.preload_act_table_set("natural_log_exp_and_others")
            act.wait_ge(sq_used, len(SQ_TILES))
            A(rstd_b[:, :].rearrange("p (j n) -> p j n", j=3), ps[:, 4:7, 0:C_CH], ACT.Ln,
              bias=eps_col[:, :]).then_inc(ln_rstd, 1)
            act.wait_ge(ln_rstd, 1)
            A(rstd_b[:, :], rstd_b[:, :], ACT.Exp, scale=-0.5).then_inc(ln_rstd, 1)
            act.preload_act_table(ACT.Silu)
            for step, k in (("silu", 0), ("silu", 1), ("hi", 0), ("silu", 2), ("hi", 1), ("silu", 3),
                            ("hi", 2), ("silu", 4), ("silu", 5), ("hi", 4), ("silu", 6), ("hi", 5),
                            ("silu", 7), ("hi", 7)):
                if step == "silu":
                    act.wait_ge(z_done, k + 1)
                    A(conv_out[:, k, :], conv_out[:, k, :], ACT.Silu, scale=par[:, k, P_LG:P_LG + 1],
                      bias=par[:, k, P_LB:P_LB + 1]).then_inc(ln_silu, 1)
                else:
                    act.wait_ge(ln_silu, k + 1)
                    act.wait_ge(proj, 3 * N_IN)
                    A(act_hi[:, k, 0:SEQ], conv_out[:, k, 0:SEQ], ACT.Copy).then_inc(v_hi, 1)
                    A(act_hi[:, k, SEQ:TO], conv_out[:, k, C_SAMPLE:C_LEN], ACT.Copy).then_inc(v_hi, 1)
            last_silu(0)
            last_silu(1)
            last_silu(2)
            act.wait_ge(w_loaded[1], 16 * (2 * KT + 1))
            w_hi_part(1, 1)
            act.wait_ge(h_done, 2 * c)
            act.wait_ge(b_done, c)
            gates_chunk(c, 1, 0, (1, 2))

            def pw_weights(p):
                for h in range(2):
                    act.wait_ge(pw, p * 2 + h + 1)
                    act.wait_ge(w_loaded[h], p * 16 + 16 * ((3 if h == 0 else 2) * KT + 2))
                    w_hi_part(h, h)
                    if isinstance(p, int):
                        gates_chunk(c, 1, 1 + h, (7, 3))
                if isinstance(p, int):
                    decay(c, 1, False)
                    root(c)

            pw_weights(0)
            with act.Fori(1, KT // 2 - 1) as p:
                pw_weights(p)
            act.wait_ge(pw, KT - 1)
            act.wait_ge(w_loaded[0], 16 * (3 * KT + 1 + KT // 2))
            w_hi_part(0, 0)
            act.wait_ge(yc, 1)
            A(y0_hi[:, :], conv_out[:, 0, 0:TO], ACT.Copy).then_inc(yh, 1)
            act.wait_ge(pw, KT)
            for k in range(1, KT):
                act.wait_ge(yc, k + 1)
                A(act_hi[:, k, 0:TO], conv_out[:, k, 0:TO], ACT.Copy).then_inc(yh, 1)
                if k == 3:
                    act.wait_ge(w_loaded[1], 16 * (2 * KT + 1 + KT // 2))
                    w_hi_part(1, 1)
            act.wait_ge(yh, 1)
            A(act_hi[:, 0, 0:TO], y0_hi[:, :].bitcast(F32), ACT.Copy).then_inc(y0_placed, 1)
            act.wait_ge(st_turned, 1)
            for i in range(2):
                A(state_rows[0:NOUT, i * 512:(i + 1) * 512], ps[0:NOUT, 3 + 4 * i, :], ACT.Copy)\
                    .then_inc(st_rows, 1)
            act.wait_ge(yr_in, 16)
            for k in range(KT):
                A(act_lo[:, k, 0:TO], yr[:, k, :], ACT.Copy).then_inc(yh, 1)

            n_loads = [3 * KT + 1 + KT // 2, 2 * KT + 1 + KT // 2]

            def o_chunk(e, j, fst):
                c0, n = YCH[j]
                act.wait_ge(oproj, e * 3 + j + 1)
                if not (fst and j < 2):
                    act.wait_ge(o_turned, e * 3 + (0, -1, 1)[j])
                take_wait()
                A(o_c[:, j % 2:j % 2 + 1, 0:n], ps[:, j:j + 1, 0:n], ACT.Copy,
                  scale=par[:, bass.ds(e, 1), P_PG:P_PG + 1].rearrange("p a n -> p (a n)"))\
                    .then_inc(o_copied, 1)
                if not (fst and j == 0):
                    act.wait_ge(o_ssq, e * 3 + j)
                A(ps[:, 3, 0:n], ps[:, j, 0:n], ACT.Square).then_inc(o_sq, 1)

            def o_tile(e, fst):
                act.wait_ge(half_done, e + 1)
                act.wait_ge(w_loaded[0], e * 16 + 16 * (n_loads[0] + 1))
                w_hi_part(0, 0)
                for j in range(3):
                    o_chunk(e, j, fst)
                    if j == 1 and not fst:
                        act.wait_ge(oproj, e * 3 + 3)
                        act.wait_ge(w_loaded[1], e * 16 + 16 * (n_loads[1] + 1))
                        w_hi_part(1, 1)
                if fst:
                    act.wait_ge(w_loaded[1], 16 * (n_loads[1] + 1))
                    w_hi_part(1, 1)

            o_tile(0, True)
            with act.Fori(1, KT - 1) as e:
                o_tile(e, False)
            e = KT - 1
            act.preload_act_table(ACT.Sqrt)

            def roots(j):
                act.wait_ge(ss_done, j + 1)
                for i, (c0, rows) in enumerate(out_tiles[j]):
                    n = 3 * j + i
                    A(rs_o[0:rows, 0, n:n + 1], ps[0:rows, 7, i:i + 1], ACT.Sqrt,
                      bias=eps_col[0:rows, :]).then_inc(ss_root, 1)

            def scaled(j):
                n, rows = 3 * j + 2, out_tiles[j][2][1]
                act.wait_ge(o_placed, 3 * e + j + 1)
                act.wait_ge(ss_rs, n + 1)
                A(o_tok[0:rows, n], o_tok[0:rows, n], ACT.Copy, scale=rs_o[0:rows, 1, n:n + 1])\
                    .then_inc(o_scaled, 1)

            o_chunk(e, 0, False)
            roots(0)
            o_chunk(e, 1, False)
            scaled(0)
            roots(1)
            o_chunk(e, 2, False)
            scaled(1)
            roots(2)
            scaled(2)

        @block.vector
        def _(dve):
            STT, TT, TS = dve.scalar_tensor_tensor, dve.tensor_tensor, dve.tensor_scalar

            def w_lo_part(slot, stage, hi_count):
                dve.wait_ge(w_his, hi_count)
                TT(WLO[slot], wstage[:, stage], WHI[slot], ALU.subtract).then_inc(late_los, 1)

            def x_norm_part(t):
                rows = x_rows[t]
                dve.wait_ge(x_rt, t + 1)
                dve.reciprocal(sums[0:rows, t:t + 1], sums[0:rows, t:t + 1]).then_inc(x_rs, 1)
                dve.wait_ge(x_rs, t + 1)
                if t == 0:
                    dve.wait_ge(g_loaded, 16)
                if t >= 2:
                    dve.wait_ge(x_turned, t - 1)
                STT(out=x_norm[0:rows, t % 2, :], in0=x_in[0:rows, t % 4, :], scalar=sums[0:rows, t:t + 1],
                    in1=g_bcast[0:rows, :], op0=ALU.mult, op1=ALU.mult).then_inc(x_normed, 1)

            def x_lo_part(t):
                rows = x_rows[t]
                b = X_BANK[t % 3]
                dve.wait_ge(x_hi, t + 1)
                src = ps[:, b:b + 2, :].rearrange("p b (k t) -> p (b k) t", t=P)[:, :, 0:rows]
                TT(act_lo[:, :, t * P:t * P + rows], src, act_hi[:, :, t * P:t * P + rows],
                   ALU.subtract).then_inc(x_lo, 1)

            for t in range(NX + 2):
                if t < NX:
                    x_norm_part(t)
                if t >= 2:
                    x_lo_part(t - 2)

            step = [0]

            def chain(ins):
                step[0] += 1
                ins.then_inc(der, 1)
                dve.wait_ge(der, step[0])

            dve.wait_ge(par_ready, 1)
            lam = par[:, :, P_LAM]
            neg, z, s, s2 = (small[:, i, :] for i in range(4))
            poly = prm[:, :]
            chain(TS(neg, lam, -1.0, None, ALU.mult))
            TT(z, lam, neg, ALU.max).then_inc(der, 1)
            step[0] += 1
            dve.wait_ge(der_exp, 1)
            chain(TS(s, z, 2.0, None, ALU.add))
            chain(dve.reciprocal(s2, s))
            chain(TT(s, s2, z, ALU.mult))
            chain(TT(s2, s, s, ALU.mult))
            chain(TS(poly, s2, 1.0 / 17.0, None, ALU.mult))
            for d in (15, 13, 11, 9, 7, 5, 3):
                chain(STT(out=poly, in0=poly, scalar=1.0 / d, in1=s2, op0=ALU.add, op1=ALU.mult))
            chain(STT(out=poly, in0=poly, scalar=1.0, in1=s, op0=ALU.add, op1=ALU.mult))
            chain(TS(neg, neg, 0.0, None, ALU.max))
            chain(TS(neg, neg, 0.5, None, ALU.mult))
            chain(TT(poly, poly, neg, ALU.add))
            chain(TS(par[:, :, Q_SP], poly, 8.0, None, ALU.mult))
            TS(par[:, :, Q_NSP], poly, -8.0, None, ALU.mult).then_inc(der, 1)
            TS(par[:, :, Q_CW:Q_CW + CW], par[:, :, P_CW:P_CW + CW], 0.5, None, ALU.mult).then_inc(der, 1)
            TS(par[:, :, Q_BA:Q_BA + 2], par[:, :, P_BA:P_BA + 2], 0.5, None, ALU.mult).then_inc(der, 1)
            step[0] += 3
            dve.wait_ge(der, step[0])
            assert step[0] == DER_STEPS

            def tap(d, b, k):
                src, w = cv_in[:, b, META + k:META + k + C_LEN], par_cv[:, b, Q_CW + k:Q_CW + k + 1]
                if k > 0:
                    dve.wait_ge(taps, d * CPAD + k)
                if k == 0:
                    TS(acc[:, :], src, w, par_cv[:, b, P_CB:P_CB + 1], ALU.mult, ALU.add).then_inc(taps, 1)
                elif k < CPAD:
                    STT(out=acc[:, :], in0=src, scalar=w, in1=acc[:, :], op0=ALU.mult,
                        op1=ALU.add).then_inc(taps, 1)
                else:
                    STT(out=conv_out[:, bass.ds(d, 1), :].rearrange("p a n -> p (a n)"), in0=src, scalar=w,
                        in1=acc[:, :], op0=ALU.mult, op1=ALU.add).then_inc(conv_done, 1)

            def some_taps(d, b, first, end):
                for k in range(first, end):
                    tap(d, b, k)

            def conv_start(d, b, fst):
                if not fst:
                    dve.wait_ge(conv_done, d)
                dve.wait_ge(par_cv_set, d + 1)
                dve.wait_ge(cv_state_set, d + 1)
                dve.wait_ge(glu_done, 2 * d + 2)
                some_taps(d, b, 0, 2)
                for o, i in ((O_CP, META + SEQ), (O_CS, V_IN - CPAD)):
                    TS(states[:, bass.ds(d, 1), o:o + CPAD], cv_in[:, b:b + 1, i:i + CPAD],
                       0.5, None, ALU.mult).then_inc(cv_saved, 1)
                tap(d, b, 2)

            def gate_low(c):
                for i in range(2):
                    r = slice(64 * i, 64 * i + 64)
                    dve.wait_ge(gwh, 2 * c + i + 1)
                    TT(gate_l[r, :, 64 * i:64 * i + 64],
                       gate_w[r, :, bass.ds(c, 1), :].rearrange("p m a j -> p m (a j)"),
                       gate_h[r, :, 64 * i:64 * i + 64], ALU.subtract).then_inc(gwl, 1)

            def rtap(c, b, k):
                if k == 1:
                    dve.wait_ge(rtap0, c + 1)
                else:
                    dve.wait_ge(rtaps, 3 * c + k - 1)
                STT(out=rg_x[:, :], in0=rg_in[:, k:k + R_LEN], scalar=par_rg[:, b, P_RW + k:P_RW + k + 1],
                    in1=rg_x[:, :], op0=ALU.mult, op1=ALU.add).then_inc(rtaps, 1)

            def b_part(c):
                dve.wait_ge(root_done, c + 1)
                TT(rc[:, :], rc[:, :], rd[:, :], ALU.mult).then_inc(b_done, 1)

            def scan(c, b):
                dve.wait_ge(b_done, c + 1)
                dve.tensor_tensor_scan(rb[:, 0:META + SEQ], ra[:, 0:META + SEQ], rc[:, 0:META + SEQ], 0.0,
                                       ALU.mult, ALU.add).then_inc(h_done, 1)
                dve.tensor_tensor_scan(rb[:, R_SAMPLE:R_SAMPLE + DEC], ra[:, R_SAMPLE:R_SAMPLE + DEC],
                                       rc[:, R_SAMPLE:R_SAMPLE + DEC], par_rg[:, b, P_H0:P_H0 + 1],
                                       ALU.mult, ALU.add).then_inc(h_done, 1)

            def save_h(c):
                dve.wait_ge(h_done, 2 * c + 2)
                for o, i in ((O_HP, META + SEQ - 1), (O_HS, R_SAMPLE + DEC - 1)):
                    dve.tensor_copy(states[:, bass.ds(c, 1), o:o + 1],
                                    rb[:, i:i + 1].rearrange("p (a n) -> p a n", a=1)).then_inc(h_saved, 1)

            def save_rg(c):
                dve.wait_ge(x_read, 3 * c + 3)
                for o, i in ((O_RP, META + SEQ), (O_RS, R_SAMPLE_IN + DEC - RPAD)):
                    dve.tensor_copy(states[:, bass.ds(c, 1), o:o + RPAD],
                                    rg_in[:, i:i + RPAD].rearrange("p (a n) -> p a n", a=1)).then_inc(rg_saved, 1)

            def ix_part(c):
                dve.wait_ge(gates_read, 6 * c + 6)
                STT(out=rd[:, :], in0=rd[:, :], scalar=1.0, in1=rg_x[:, :], op0=ALU.add,
                    op1=ALU.mult).then_inc(ix_done, 1)

            def q_part(c):
                dve.wait_ge(a2_done, c + 1)
                dve.wait_ge(ix_done, c + 1)
                STT(out=rc[:, :], in0=rc[:, :], scalar=1.0, in1=rb[:, :], op0=ALU.add,
                    op1=ALU.mult).then_inc(q_done, 1)

            def rg_conv(c, b):
                for k in range(1, RW):
                    rtap(c, b, k)
                gate_low(c)

            def tile(c, b, at):
                d, o = c + 1, 1 - b
                if at == 0:
                    rg_conv(c, b)
                    save_rg(c)
                    b_part(c - 1)
                    scan(c - 1, 1 - b)
                    save_h(c - 1)
                conv_start(d, o, False)
                for k in range(3, CW):
                    if k == at:
                        rg_conv(c, b)
                        save_rg(c)
                    if at and k == at + 1:
                        b_part(c - 1)
                    if at and k == at + 2:
                        scan(c - 1, 1 - b)
                    if at and k == at + 3:
                        save_h(c - 1)
                    if k == 26:
                        ix_part(c)
                    if k == 28:
                        q_part(c)
                    tap(d, o, k)

            conv_start(0, 0, True)
            some_taps(0, 0, 3, 23)
            rg_conv(0, 0)
            some_taps(0, 0, 23, CW)
            save_rg(0)
            tile(0, 0, None)
            tile(1, 1, 0)
            tile(2, 0, 3)
            with dve.Fori(1, KT // 2 - 1) as i:
                tile(i * 2 + 1, 1, 6)
                tile(i * 2 + 2, 0, 6)

            c = KT - 1
            dve.wait_ge(cv_saved, 2 * KT)
            dve.wait_ge(conv_done, KT)
            dve.wait_ge(csummed, KT - 2)
            TT(csum[:, :], csum[:, :], conv_out[:, c, :], ALU.add).then_inc(csummed, 1)
            rtap(c, 1, 1)
            rtap(c, 1, 2)
            dve.wait_ge(mean_done, 1)
            for k in range(KT):
                t = conv_out[:, k, :].rearrange("p (j n) -> p j n", j=3)
                TT(t, t, ps[:, 1:4, 0:C_CH], ALU.subtract).then_inc(centred, 1)
            dve.wait_ge(squared, 6)
            TT(sqs[:, SQ_SLOT[4], :], sqs[:, SQ_SLOT[4], :], sq5[:, :], ALU.add).then_inc(sq_paired, 1)
            dve.wait_ge(squared, 8)
            TT(sqs[:, SQ_SLOT[6], :], sqs[:, SQ_SLOT[6], :], sqs[:, SQ_SLOT[7], :], ALU.add).then_inc(sq_paired, 1)
            b_part(c - 1)
            rtap(c, 1, 3)
            scan(c - 1, 0)
            dve.wait_ge(rtaps, 3 * c + 3)
            dve.tensor_copy(rg_xh[:, :], rg_x[:, :]).then_inc(rgxh, 1)
            save_h(c - 1)
            gate_low(c)
            w_lo_part(0, 0, N_PW + 1)
            save_rg(c)
            dve.wait_ge(ln_rstd, 2)
            for step, k in (("z", 0), ("z", 1), ("z", 2), ("z", 3), ("lo", 0), ("z", 4), ("z", 5),
                            ("lo", 2), ("hi", 3), ("lo", 3), ("z", 6), ("z", 7), ("hi", 6), ("lo", 5),
                            ("lo", 7)):
                if step == "z":
                    TT(conv_out[:, k, :], conv_out[:, k, :], rstd_b[:, :], ALU.mult).then_inc(z_done, 1)
                elif step == "hi":
                    dve.wait_ge(ln_silu, k + 1)
                    dve.wait_ge(proj, 3 * N_IN)
                    dve.tensor_copy(act_hi[:, k, 0:SEQ], conv_out[:, k, 0:SEQ]).then_inc(v_hi_dve, 1)
                    dve.tensor_copy(act_hi[:, k, SEQ:TO], conv_out[:, k, C_SAMPLE:C_LEN]).then_inc(v_hi_dve, 1)
                else:
                    hi_done(dve, k)
                    TT(act_lo[:, k, 0:SEQ], conv_out[:, k, 0:SEQ], act_hi[:, k, 0:SEQ],
                       ALU.subtract).then_inc(v_lo[1], 1)
                    TT(act_lo[:, k, SEQ:TO], conv_out[:, k, C_SAMPLE:C_LEN], act_hi[:, k, SEQ:TO],
                       ALU.subtract).then_inc(v_lo[1], 1)
            w_lo_part(1, 1, N_PW + 2)

            def pw_out(p, last=False):
                for h in range(2):
                    k = p * 2 + h
                    if last and h == 1:
                        yc_low(0)
                    dve.wait_ge(pw, k + 1)
                    dve.wait_ge(silu_loaded[h], p * 16 + 16)
                    STT(out=conv_out[:, bass.ds(k, 1), 0:TO].rearrange("p a (j n) -> p (a j) n", j=3),
                        in0=ps[:, PW_BANK[h]:PW_BANK[h] + 3, 0:OCH],
                        scalar=par[:, bass.ds(k, 1), P_B2:P_B2 + 1].rearrange("p a n -> p (a n)"),
                        in1=silu_l[:, h].rearrange("p (j n) -> p j n", j=3), op0=ALU.add,
                        op1=ALU.mult).then_inc(yc, 1)
                    if last and h == 1:
                        for k in range(1, 4):
                            yc_low(k)
                    w_lo_part(h, h, p * 2 + N_PW + 3 + h)

            def yc_low(k):
                dve.wait_ge(yh, k + 1)
                TT(yc_lo[:, k, 0:TO], conv_out[:, k, 0:TO], y0_hi[:, :] if k == 0 else act_hi[:, k, 0:TO],
                   ALU.subtract).then_inc(yl, 1)

            pw_out(0)
            ix_part(c)
            q_part(c)
            b_part(c)
            scan(c, 1)
            save_h(c)
            with dve.Fori(1, KT // 2 - 1) as p:
                pw_out(p)
            pw_out(KT // 2 - 1, last=True)
            for k in range(4, KT):
                yc_low(k)
            for k in range(KT):
                dve.wait_ge(yh, KT + k + 1)
                TT(yr_lo[:, k, :], yr[:, k, :], act_lo[:, k, 0:TO], ALU.subtract).then_inc(yl, 1)

            def place(e, j):
                dve.wait_ge(o_turned, e * 3 + j + 1)
                n = len(out_tiles[j])
                if j == 2:
                    n -= 1
                    dve.tensor_copy(o_tok[0:DEC, 8:9, bass.ds(e * P, P)],
                                    ps[0:DEC, 6:7, n * P:(n + 1) * P])
                dve.tensor_copy(o_tok[:, 3 * j:3 * j + n, bass.ds(e * P, P)],
                                ps[:, 4 + j, 0:n * P].rearrange("p (a n) -> p a n", n=P)).then_inc(o_placed, 1)

            def add_squares(e, j, fst):
                c0, n = YCH[j]
                dve.wait_ge(o_sq, e * 3 + j + 1)
                if fst:
                    dve.tensor_copy(ssq[:, c0:c0 + n], ps[:, 3, 0:n]).then_inc(o_ssq, 1)
                else:
                    dve.wait_ge(o_ssq, e * 3 + j - 2)
                    TT(ssq[:, c0:c0 + n], ssq[:, c0:c0 + n], ps[:, 3, 0:n], ALU.add).then_inc(o_ssq, 1)

            w_lo_part(0, 0, N_OUT + 3)
            dve.wait_ge(st_out, 16 * 6)
            for j in range(3):
                add_squares(0, j, True)
            w_lo_part(1, 1, N_OUT + 4)
            for j in range(2):
                place(0, j)
            with dve.Fori(1, KT - 1) as e:
                place(e - 1, 2)
                w_lo_part(0, 0, e * 2 + N_OUT + 3)
                add_squares(e, 0, False)
                add_squares(e, 1, False)
                place(e, 0)
                w_lo_part(1, 1, e * 2 + N_OUT + 4)
                add_squares(e, 2, False)
                place(e, 1)
            e = KT - 1

            def rstd(j):
                for i, (c0, rows) in enumerate(out_tiles[j]):
                    n = 3 * j + i
                    dve.wait_ge(ss_root, n + 1)
                    dve.reciprocal(rs_o[0:rows, 1, n:n + 1], rs_o[0:rows, 0, n:n + 1]).then_inc(ss_rs, 1)

            def y_tile(n):
                dve.wait_ge(o_placed, 3 * e + n // 3 + 1)
                dve.wait_ge(xr_loaded[n // 3], 16 * 3)
                dve.wait_ge(ss_rs, n + 1)
                x = x_res0[:, n] if n < 2 else x_res2[:, n - 2]
                STT(out=o_tok[:, n], in0=o_tok[:, n], scalar=rs_o[:, 1, n:n + 1], in1=x,
                    op0=ALU.mult, op1=ALU.add).then_inc(y_ready[0], 1)

            place(e - 1, 2)
            add_squares(e, 0, False)
            place(e, 0)
            rstd(0)
            y_tile(0)
            add_squares(e, 1, False)
            place(e, 1)
            y_tile(1)
            rstd(1)
            y_tile(3)
            add_squares(e, 2, False)
            place(e, 2)
            y_tile(4)
            rstd(2)
            y_tile(6)
            y_tile(7)


_INS = ["x_prompt", "x_sample", "state_rg_h", "state_rg_conv", "state_cv_conv", "meta_tokens", "pre_norm_g",
        "w_in", "rg_conv_w", "rg_conv_b", "rg_wa", "rg_ba", "rg_wx", "rg_bx", "rg_lambda", "cv_conv_w",
        "cv_conv_b", "cv_ln_g", "cv_ln_b", "cv_w_pw2", "cv_b_pw2", "w_out", "post_norm_g"]
_OUTS = [(1, SEQ, D), (1, DEC, D), (1, 1, D), (1, 1, RPAD, D), (1, 1, CPAD, D),
         (1, 1, D), (1, 1, RPAD, D), (1, 1, CPAD, D)]


def kernel(**inputs):
    import concourse.bacc as bacc
    from concourse.bass_utils import run_bass_kernel_spmd

    nc = bacc.Bacc("TRN2", target_bir_lowering=False, num_devices=1)
    arrays, args = {}, []
    for name in _INS:
        a = np.ascontiguousarray(inputs[name])
        arrays[f"in_{name}"] = a
        args.append(nc.dram_tensor(f"in_{name}", a.shape, mybir.dt.from_np(a.dtype), kind="ExternalInput").ap())
    for i, shape in enumerate(_OUTS):
        args.append(nc.dram_tensor(f"out_{i}", shape, F32, kind="ExternalOutput").ap())
    build(nc, *args)
    r = run_bass_kernel_spmd(nc, [arrays], core_ids=[0])
    return tuple(r.results[0][f"out_{i}"] for i in range(len(_OUTS)))
```
